# Optimizing a Trainium2 kernel written in Bass

```python
import math
import jax
import jax.numpy as jnp
from jax import lax
import numpy as np

D_MODEL = 1024
BATCH = 1
SEQ = 512
DEPTH = 1
DEC_BATCH = 8
DEC_SEQ = 4
PAST_LEN = 2048
PAGE_SIZE = 128

ATT_HEADS = 8
ATT_KV_HEADS = 2
ATT_HEAD_DIM = 64
ATT_GROUP = ATT_HEADS // ATT_KV_HEADS
WINDOW = 128
ROPE_THETA = 10000.0
DN_HEADS = 4
DN_HEAD_DIM = 128
CONV_WIDTH = 4
DN_CHUNK = 64
MEM_LEN = 256
X_HEADS = 4
X_HEAD_DIM = D_MODEL // X_HEADS
N_KEYS = 128
N_EXPERTS = N_KEYS * N_KEYS
PEER_HEADS = 8
PEER_QDIM = 256
PEER_TOPK = 16
PEER_BLOCK = 128
LN_EPS = 1e-5
RMS_EPS = 1e-6
NEG_INF = -1e30
DEEPNORM_ALPHA = (2 * DEPTH) ** 0.25
DEEPNORM_BETA = (8 * DEPTH) ** -0.25

ATT_Q = ATT_HEADS * ATT_HEAD_DIM
ATT_KV = ATT_KV_HEADS * ATT_HEAD_DIM
DN_W = DN_HEADS * DN_HEAD_DIM
MIX_WIDTH = ATT_Q + DN_W
CONV_CH = 3 * DN_W
IN_SIZES = (ATT_Q, ATT_KV, ATT_KV, CONV_CH, DN_HEADS, DN_HEADS, DN_W)
IN_SPLITS = tuple(int(s) for s in np.cumsum(IN_SIZES)[:-1])

kernel_name = 'hymba_swa_gdn_peer_step'

def layer_norm(x, g, b):
    xf = x.astype(jnp.float32)
    mu = jnp.mean(xf, -1, keepdims=True)
    var = jnp.mean(jnp.square(xf - mu), -1, keepdims=True)
    y = (xf - mu) * lax.rsqrt(var + LN_EPS) * g.astype(jnp.float32) + b.astype(jnp.float32)
    return y.astype(x.dtype)

def rope(x, pos):
    half = x.shape[-1] // 2
    inv_freq = ROPE_THETA ** (-jnp.arange(half, dtype=jnp.float32) / half)
    ang = pos.astype(jnp.float32)[:, None] * inv_freq[None, :]
    cos = jnp.cos(ang)[None, :, None, :]
    sin = jnp.sin(ang)[None, :, None, :]
    xf = x.astype(jnp.float32)
    x1, x2 = xf[..., :half], xf[..., half:]
    return jnp.concatenate([x1 * cos - x2 * sin, x2 * cos + x1 * sin], -1).astype(x.dtype)

def sink_softmax(s, sink):
    m = jnp.maximum(jnp.max(s, -1, keepdims=True), sink)
    p = jnp.exp(s - m)
    return p / (jnp.sum(p, -1, keepdims=True) + jnp.exp(sink - m))

def swa_banded(q, k, v, sinks):
    B, L = q.shape[:2]
    nb = L // WINDOW
    qb = q.reshape(B, nb, WINDOW, ATT_KV_HEADS, ATT_GROUP, ATT_HEAD_DIM)

    def band(t):
        tb = t.reshape(B, nb, WINDOW, ATT_KV_HEADS, ATT_HEAD_DIM)
        prev = jnp.concatenate([jnp.zeros_like(tb[:, :1]), tb[:, :-1]], 1)
        return jnp.concatenate([prev, tb], 2)

    kb, vb = band(k), band(v)
    s = jnp.einsum('bnqhgd,bnkhd->bnhgqk', qb, kb, preferred_element_type=jnp.float32) * ATT_HEAD_DIM ** -0.5
    qi = jnp.arange(WINDOW)[:, None]
    kj = jnp.arange(2 * WINDOW)[None, :]
    blk = jnp.arange(nb)[:, None, None]
    valid = (kj >= qi) & (kj <= qi + WINDOW) & (blk * WINDOW + kj >= WINDOW)
    s = jnp.where(valid[None, :, None, None], s, NEG_INF)
    p = sink_softmax(s, sinks.astype(jnp.float32).reshape(ATT_KV_HEADS, ATT_GROUP, 1, 1))
    o = jnp.einsum('bnhgqk,bnkhd->bnqhgd', p.astype(vb.dtype), vb)
    return o.reshape(B, L, ATT_Q)

def swa_cached(q, k, v, past_k, past_v, sinks):
    B, L = q.shape[:2]
    P = past_k.shape[1]
    kk = jnp.concatenate([past_k.astype(k.dtype), k], 1)
    vv = jnp.concatenate([past_v.astype(v.dtype), v], 1)
    qpos = jnp.arange(L)[:, None]
    kpos = jnp.arange(P + L)[None, :] - P
    valid = (kpos <= qpos) & (kpos >= qpos - WINDOW)
    qg = q.reshape(B, L, ATT_KV_HEADS, ATT_GROUP, ATT_HEAD_DIM)
    s = jnp.einsum('blhgd,bkhd->bhglk', qg, kk, preferred_element_type=jnp.float32) * ATT_HEAD_DIM ** -0.5
    s = jnp.where(valid, s, NEG_INF)
    p = sink_softmax(s, sinks.astype(jnp.float32).reshape(ATT_KV_HEADS, ATT_GROUP, 1, 1))
    o = jnp.einsum('bhglk,bkhd->blhgd', p.astype(vv.dtype), vv)
    return o.reshape(B, L, ATT_Q), kk[:, -P:], vv[:, -P:]

def causal_conv(xc, buf, w_conv):
    L = xc.shape[1]
    xp = jnp.concatenate([buf.astype(xc.dtype), xc], 1)
    y = xp[:, 0:L] * w_conv[0]
    for j in range(1, CONV_WIDTH):
        y = y + xp[:, j:j + L] * w_conv[j]
    return jax.nn.silu(y), xp[:, -(CONV_WIDTH - 1):]

def l2norm(t):
    return t * lax.rsqrt(jnp.sum(jnp.square(t), -1, keepdims=True) + RMS_EPS)

def gated_delta_chunked(q, k, v, g, beta, S0, C):
    B, L, H, _ = q.shape
    dv = v.shape[-1]
    N = L // C

    def blk(t):
        return jnp.moveaxis(t.reshape((B, N, C, H) + t.shape[3:]), 3, 2)

    q, k, v, g, beta = blk(q), blk(k), blk(v), blk(g), blk(beta)
    gc = jnp.cumsum(g, -1)
    tri_incl = jnp.tril(jnp.ones((C, C), dtype=bool))
    tri_strict = jnp.tril(jnp.ones((C, C), dtype=bool), -1)
    decay = jnp.exp(jnp.where(tri_incl, gc[..., :, None] - gc[..., None, :], -jnp.inf))
    k_beta = k * beta[..., None]
    A = jnp.where(tri_strict, jnp.einsum('bnhid,bnhjd->bnhij', k_beta, k) * decay, 0.0)
    rhs = jnp.concatenate([v * beta[..., None], k_beta * jnp.exp(gc)[..., None]], -1)
    sol = lax.linalg.triangular_solve(jnp.eye(C, dtype=jnp.float32) + A, rhs, left_side=True, lower=True)
    u, w = sol[..., :dv], sol[..., dv:]
    qk = jnp.einsum('bnhid,bnhjd->bnhij', q, k) * decay

    def step(S, xs):
        q_i, k_i, u_i, w_i, gc_i, qk_i = xs
        v_new = u_i - jnp.einsum('bhck,bhkv->bhcv', w_i, S)
        o = (jnp.einsum('bhck,bhkv->bhcv', q_i * jnp.exp(gc_i)[..., None], S)
             + jnp.einsum('bhij,bhjv->bhiv', qk_i, v_new))
        g_last = gc_i[..., -1]
        S = (S * jnp.exp(g_last)[..., None, None]
             + jnp.einsum('bhck,bhcv->bhkv', k_i * jnp.exp(g_last[..., None] - gc_i)[..., None], v_new))
        return S, o

    xs = tuple(jnp.moveaxis(t, 1, 0) for t in (q, k, u, w, gc, qk))
    S, o = lax.scan(step, S0, xs)
    o = jnp.swapaxes(jnp.moveaxis(o, 0, 1), 2, 3).reshape(B, L, H, dv)
    return o, S

def memory_kv(mem, w_ck, w_cv):
    B, M, _ = mem.shape
    mk = (mem @ w_ck).reshape(B, M, X_HEADS, X_HEAD_DIM)
    mv = (mem @ w_cv).reshape(B, M, X_HEADS, X_HEAD_DIM)
    return mk, mv

def cross_attention(x, mem_k, mem_v, w_cq, w_co):
    B, L, _ = x.shape
    q = (x @ w_cq).reshape(B, L, X_HEADS, X_HEAD_DIM)
    s = jnp.einsum('blhd,bmhd->bhlm', q, mem_k.astype(q.dtype), preferred_element_type=jnp.float32) * X_HEAD_DIM ** -0.5
    p = jax.nn.softmax(s, -1)
    o = jnp.einsum('bhlm,bmhd->blhd', p.astype(x.dtype), mem_v.astype(x.dtype))
    return o.reshape(B, L, D_MODEL) @ w_co

def peer(x, w_pq, keys1, keys2, expert_u, expert_v):
    T = x.shape[0]
    n_blk = -(-T // PEER_BLOCK)
    xb = jnp.pad(x, ((0, n_blk * PEER_BLOCK - T), (0, 0))).reshape(n_blk, PEER_BLOCK, D_MODEL)
    half = PEER_QDIM // 2

    def block(xt):
        q = jnp.einsum('td,dhq->thq', xt, w_pq, preferred_element_type=jnp.float32)
        s1 = jnp.einsum('thc,kc->thk', q[..., :half], keys1.astype(jnp.float32))
        s2 = jnp.einsum('thc,kc->thk', q[..., half:], keys2.astype(jnp.float32))
        v1, i1 = lax.top_k(s1, PEER_TOPK)
        v2, i2 = lax.top_k(s2, PEER_TOPK)
        cand = (v1[..., :, None] + v2[..., None, :]).reshape(PEER_BLOCK, PEER_HEADS, PEER_TOPK * PEER_TOPK)
        sc, ci = lax.top_k(cand, PEER_TOPK)
        eid = (jnp.take_along_axis(i1, ci // PEER_TOPK, -1) * N_KEYS
               + jnp.take_along_axis(i2, ci % PEER_TOPK, -1))
        gate = jax.nn.softmax(sc, -1)
        hid = jax.nn.gelu(jnp.einsum('td,thkd->thk', xt, expert_u[eid], preferred_element_type=jnp.float32))
        return jnp.einsum('thk,thkd->td', (gate * hid).astype(xt.dtype), expert_v[eid])

    return lax.map(block, xb).reshape(n_blk * PEER_BLOCK, D_MODEL)[:T]

def decoder_layer(x, pos0, swa_past_k, swa_past_v, dn_s0, conv_buf, mem_k, mem_v,
                  w_in, w_conv, dn_a_log, dn_dt_bias, dn_norm_g, attn_sinks, w_o, ln1_g, ln1_b,
                  w_cq, w_co, ln2_g, ln2_b, w_pq, peer_keys1, peer_keys2, peer_u, peer_v, ln3_g, ln3_b):
    B, L, _ = x.shape
    f32 = jnp.float32
    pos = pos0 + jnp.arange(L, dtype=jnp.int32)
    h = x @ w_in
    aq, ak, av, dqkv, db, da, dz = jnp.split(h, IN_SPLITS, axis=-1)
    aq = rope(aq.reshape(B, L, ATT_HEADS, ATT_HEAD_DIM), pos)
    ak = rope(ak.reshape(B, L, ATT_KV_HEADS, ATT_HEAD_DIM), pos)
    av = av.reshape(B, L, ATT_KV_HEADS, ATT_HEAD_DIM)
    if swa_past_k is None:
        a_out = swa_banded(aq, ak, av, attn_sinks)
        new_k, new_v = ak[:, -WINDOW:], av[:, -WINDOW:]
    else:
        a_out, new_k, new_v = swa_cached(aq, ak, av, swa_past_k, swa_past_v, attn_sinks)
    c_out, new_conv = causal_conv(dqkv, conv_buf, w_conv)
    dq, dk, dv = jnp.split(c_out.astype(f32).reshape(B, L, 3 * DN_HEADS, DN_HEAD_DIM), 3, axis=2)
    dq = l2norm(dq) * DN_HEAD_DIM ** -0.5
    dk = l2norm(dk)
    beta = jax.nn.sigmoid(db.astype(f32))
    g = -jnp.exp(dn_a_log.astype(f32)) * jax.nn.softplus(da.astype(f32) + dn_dt_bias.astype(f32))
    chunk = DN_CHUNK if L % DN_CHUNK == 0 else L
    o, S = gated_delta_chunked(dq, dk, dv, g, beta, dn_s0.astype(f32), chunk)
    o = o * lax.rsqrt(jnp.mean(jnp.square(o), -1, keepdims=True) + RMS_EPS) * dn_norm_g.astype(f32)
    o = o * jax.nn.silu(dz.astype(f32).reshape(B, L, DN_HEADS, DN_HEAD_DIM))
    mix = jnp.concatenate([a_out, o.reshape(B, L, DN_W).astype(x.dtype)], -1) @ w_o
    x1 = layer_norm(DEEPNORM_ALPHA * x + mix, ln1_g, ln1_b)
    x2 = layer_norm(DEEPNORM_ALPHA * x1 + cross_attention(x1, mem_k, mem_v, w_cq, w_co), ln2_g, ln2_b)
    ffn = peer(x2.reshape(B * L, D_MODEL), w_pq, peer_keys1, peer_keys2, peer_u, peer_v).reshape(B, L, D_MODEL)
    x3 = layer_norm(DEEPNORM_ALPHA * x2 + ffn, ln3_g, ln3_b)
    return x3, new_k, new_v, S.astype(x.dtype), new_conv.astype(x.dtype)

def setup_inputs(seed: int = 0) -> dict:
    key = jax.random.key(seed)
    keys = iter(jax.random.split(key, 48))
    f32 = jnp.float32

    def normal(shape, scale):
        return jax.random.normal(next(keys), shape, f32) * scale

    s_in = D_MODEL ** -0.5
    beta = DEEPNORM_BETA
    x_prompt = normal((BATCH, SEQ, D_MODEL), 1.0)
    x_sample = normal((DEC_BATCH, DEC_SEQ, D_MODEL), 1.0)
    cache_swa_k = normal((DEPTH, DEC_BATCH, WINDOW, ATT_KV_HEADS, ATT_HEAD_DIM), 1.0)
    cache_swa_v = normal((DEPTH, DEC_BATCH, WINDOW, ATT_KV_HEADS, ATT_HEAD_DIM), beta)
    state_dn = normal((DEPTH, DEC_BATCH, DN_HEADS, DN_HEAD_DIM, DN_HEAD_DIM), 0.1)
    state_dn_conv = normal((DEPTH, DEC_BATCH, CONV_WIDTH - 1, CONV_CH), 1.0)
    cache_mem_k = normal((DEPTH, DEC_BATCH, MEM_LEN, X_HEADS, X_HEAD_DIM), 1.0)
    cache_mem_v = normal((DEPTH, DEC_BATCH, MEM_LEN, X_HEADS, X_HEAD_DIM), beta)
    mem_prompt = normal((BATCH, MEM_LEN, D_MODEL), 1.0)
    w_in = jnp.concatenate([
        normal((DEPTH, D_MODEL, ATT_Q), s_in),
        normal((DEPTH, D_MODEL, ATT_KV), s_in),
        normal((DEPTH, D_MODEL, ATT_KV), s_in * beta),
        normal((DEPTH, D_MODEL, 2 * DN_W), s_in),
        normal((DEPTH, D_MODEL, DN_W), s_in * beta),
        normal((DEPTH, D_MODEL, 2 * DN_HEADS), s_in),
        normal((DEPTH, D_MODEL, DN_W), s_in)], axis=-1)
    w_conv = normal((DEPTH, CONV_WIDTH, CONV_CH), CONV_WIDTH ** -0.5)
    dn_a_log = jnp.log(jax.random.uniform(next(keys), (DEPTH, DN_HEADS), f32, 1.0, 16.0))
    dt = jnp.exp(jax.random.uniform(next(keys), (DEPTH, DN_HEADS), f32, math.log(1e-3), math.log(1e-1)))
    dn_dt_bias = dt + jnp.log(-jnp.expm1(-dt))
    dn_norm_g = 1.0 + normal((DEPTH, DN_HEAD_DIM), 0.05)
    attn_sinks = normal((DEPTH, ATT_HEADS), 0.5)
    w_o = normal((DEPTH, MIX_WIDTH, D_MODEL), MIX_WIDTH ** -0.5 * beta)
    ln1_g = 1.0 + normal((DEPTH, D_MODEL), 0.05)
    ln1_b = normal((DEPTH, D_MODEL), 0.02)
    w_cq = normal((DEPTH, D_MODEL, D_MODEL), s_in)
    w_ck = normal((DEPTH, D_MODEL, D_MODEL), s_in)
    w_cv = normal((DEPTH, D_MODEL, D_MODEL), s_in * beta)
    w_co = normal((DEPTH, D_MODEL, D_MODEL), s_in * beta)
    ln2_g = 1.0 + normal((DEPTH, D_MODEL), 0.05)
    ln2_b = normal((DEPTH, D_MODEL), 0.02)
    w_pq = normal((DEPTH, D_MODEL, PEER_HEADS, PEER_QDIM), s_in)
    peer_keys1 = normal((DEPTH, N_KEYS, PEER_QDIM // 2), (PEER_QDIM // 2) ** -0.5)
    peer_keys2 = normal((DEPTH, N_KEYS, PEER_QDIM // 2), (PEER_QDIM // 2) ** -0.5)
    peer_u = normal((DEPTH, N_EXPERTS, D_MODEL), s_in)
    peer_v = normal((DEPTH, N_EXPERTS, D_MODEL), beta)
    ln3_g = 1.0 + normal((DEPTH, D_MODEL), 0.05)
    ln3_b = normal((DEPTH, D_MODEL), 0.02)
    return {
        'x_prompt': x_prompt, 'x_sample': x_sample,
        'cache_swa_k': cache_swa_k, 'cache_swa_v': cache_swa_v,
        'state_dn': state_dn, 'state_dn_conv': state_dn_conv,
        'cache_mem_k': cache_mem_k, 'cache_mem_v': cache_mem_v,
        'mem_prompt': mem_prompt,
        'w_in': w_in, 'w_conv': w_conv, 'dn_a_log': dn_a_log, 'dn_dt_bias': dn_dt_bias,
        'dn_norm_g': dn_norm_g, 'attn_sinks': attn_sinks, 'w_o': w_o, 'ln1_g': ln1_g, 'ln1_b': ln1_b,
        'w_cq': w_cq, 'w_ck': w_ck, 'w_cv': w_cv, 'w_co': w_co, 'ln2_g': ln2_g, 'ln2_b': ln2_b,
        'w_pq': w_pq, 'peer_keys1': peer_keys1, 'peer_keys2': peer_keys2,
        'peer_u': peer_u, 'peer_v': peer_v, 'ln3_g': ln3_g, 'ln3_b': ln3_b,
    }

def reference(x_prompt, x_sample, cache_swa_k, cache_swa_v, state_dn, state_dn_conv, cache_mem_k, cache_mem_v,
              mem_prompt, w_in, w_conv, dn_a_log, dn_dt_bias, dn_norm_g, attn_sinks, w_o, ln1_g, ln1_b,
              w_cq, w_ck, w_cv, w_co, ln2_g, ln2_b, w_pq, peer_keys1, peer_keys2, peer_u, peer_v, ln3_g, ln3_b):
    B = x_prompt.shape[0]
    zero_state = jnp.zeros((B, DN_HEADS, DN_HEAD_DIM, DN_HEAD_DIM), jnp.float32)
    zero_conv = jnp.zeros((B, CONV_WIDTH - 1, CONV_CH), x_prompt.dtype)
    y_prompt, y_sample = x_prompt, x_sample
    p_k, p_v, p_s, p_c, p_mk, p_mv = [], [], [], [], [], []
    s_k, s_v, s_s, s_c = [], [], [], []
    for l in range(DEPTH):
        lw = (w_in[l], w_conv[l], dn_a_log[l], dn_dt_bias[l], dn_norm_g[l], attn_sinks[l], w_o[l],
              ln1_g[l], ln1_b[l], w_cq[l], w_co[l], ln2_g[l], ln2_b[l], w_pq[l], peer_keys1[l],
              peer_keys2[l], peer_u[l], peer_v[l], ln3_g[l], ln3_b[l])
        mk, mv = memory_kv(mem_prompt, w_ck[l], w_cv[l])
        y_prompt, pk, pv, ps, pc = decoder_layer(y_prompt, 0, None, None, zero_state, zero_conv, mk, mv, *lw)
        y_sample, sk, sv, ss, sc = decoder_layer(y_sample, PAST_LEN, cache_swa_k[l], cache_swa_v[l], state_dn[l],
                                                 state_dn_conv[l], cache_mem_k[l], cache_mem_v[l], *lw)
        p_k.append(pk); p_v.append(pv); p_s.append(ps); p_c.append(pc); p_mk.append(mk); p_mv.append(mv)
        s_k.append(sk); s_v.append(sv); s_s.append(ss); s_c.append(sc)
    swa_k_prompt, swa_v_prompt = jnp.stack(p_k), jnp.stack(p_v)
    dn_state_prompt, dn_conv_prompt = jnp.stack(p_s), jnp.stack(p_c)
    mem_k_prompt, mem_v_prompt = jnp.stack(p_mk), jnp.stack(p_mv)
    swa_k_sample, swa_v_sample = jnp.stack(s_k), jnp.stack(s_v)
    dn_state_sample, dn_conv_sample = jnp.stack(s_s), jnp.stack(s_c)
    return (y_prompt, y_sample, swa_k_prompt, swa_v_prompt, dn_state_prompt, dn_conv_prompt,
            mem_k_prompt, mem_v_prompt, swa_k_sample, swa_v_sample, dn_state_sample, dn_conv_sample)


_drawn_inputs = setup_inputs


def setup_inputs(seed=0):
    import zlib

    import numpy as np

    out = dict(_drawn_inputs(seed))
    spreads = {}
    factors = {'attn_sinks': 8.0, 'ln3_b': 2.69}
    for name, (base, spread) in spreads.items():
        noise = np.random.default_rng([zlib.crc32(name.encode()), seed]).standard_normal(out[name].shape)
        drawn = base * np.exp(spread * noise) if base else spread * noise
        out[name] = jnp.asarray(drawn.astype(out[name].dtype))
    for name, factor in factors.items():
        out[name] = (out[name] * factor).astype(out[name].dtype)
    return out
```

```python
from contextlib import ExitStack

import concourse.bass as bass
from concourse import mybir

F32 = mybir.dt.float32
U32 = mybir.dt.uint32
ALU = mybir.AluOpType
ACT = mybir.ActivationFunctionType
AX = mybir.AxisListType.X

P = 128
D = 1024
KD = D // P
SEQ = 512
NB, NL = 8, 4
SAMP = NB * NL
TOK = SEQ + SAMP
HALF = TOK // 2
NT = 5
ROWS = [P, P, P, P, SAMP]
ALPHA = 2.0 ** 0.25
HD = 64
DNH, DK = 4, 128
MEM = 256
XH = 4
NK = 128
PH, TOPK = 8, 16
LN_EPS, RMS_EPS = 1e-5, 1e-6
NEG = -1e30

C_Q, C_K, C_V, C_CONV, C_B, C_Z = 0, 512, 640, 768, 2304, 2312
CONV = 1536
CCH = CONV // P
PADW = 3 + SEQ + NB * 7

LEVELS = 7
_at = 0


def _cols(n):
    global _at
    _at += n
    return _at - n


K_ID = _cols(P)
K_SWA = _cols(2 * P)
K_SMP = _cols(P + SAMP)
K_UT = _cols(P)
K_ONE = _cols(P)
K_UTS = _cols(SAMP)
K_ONES = _cols(SAMP)
K_LEV = _cols(LEVELS * P)
K_BM = _cols(NB * SAMP)
K_BR = _cols(NB)
K_IOTA = _cols(NK)
K_COS = _cols(NT * 32)
K_SIN = _cols(NT * 32)
K_N = _at

ARENA = 53000
A_CST = 0
A_X = A_CST + K_N
A_XT = A_X + NT * D
A_FREE = A_XT + KD * TOK


def constants():
    import numpy as np
    c = np.zeros((P, K_N), np.float32)
    p, f = np.arange(P)[:, None], np.arange(P)[None, :]
    c[:, K_ID:K_ID + P] = p == f
    c[:, K_SWA:K_SWA + P] = np.where(f >= p, 0.0, NEG)
    c[:, K_SWA + P:K_SWA + 2 * P] = np.where(f <= p, 0.0, NEG)
    b, l = (np.arange(P) % SAMP) // NL, np.arange(P) % NL
    t = np.arange(SAMP)
    c[:, K_SMP:K_SMP + P] = np.where(f >= l[:, None], 0.0, NEG)
    c[:, K_SMP + P:K_SMP + P + SAMP] = np.where(
        (t[None] // NL == b[:, None]) & (t[None] % NL <= l[:, None]), 0.0, NEG)
    c[:, K_UT:K_UT + P] = p <= f
    c[:, K_ONE:K_ONE + P] = 1.0
    same = t[:, None] // NL == t[None] // NL
    c[:SAMP, K_UTS:K_UTS + SAMP] = same & (t[:, None] <= t[None])
    c[:SAMP, K_ONES:K_ONES + SAMP] = same
    for v in range(LEVELS):
        s = 1 << v
        c[:, K_LEV + v * P:K_LEV + (v + 1) * P] = (f // (2 * s) == p // (2 * s)) & (f % (2 * s) >= s) & (p % (2 * s) < s)
    c[:, K_BM:K_BM + NB * SAMP] = (t[None] // NL == np.arange(NB)[:, None]).reshape(1, -1)
    c[:SAMP, K_BR:K_BR + NB] = t[:, None] // NL == np.arange(NB)[None]
    c[:, K_IOTA:K_IOTA + NK] = f
    inv = (np.float32(10000.0) ** (-np.arange(32, dtype=np.float32) / np.float32(32))).astype(np.float32)
    for n in range(NT):
        pos = (np.arange(P) + n * P if n < 4 else 2048 + np.arange(P) % NL).astype(np.float32)
        ang = (pos[:, None] * inv[None]).astype(np.float32)
        c[:, K_COS + 32 * n:K_COS + 32 * n + 32] = np.cos(ang)
        c[:, K_SIN + 32 * n:K_SIN + 32 * n + 32] = np.sin(ang)
    return c


class Program:

    def __init__(self, nc, dram):
        self.nc, self.dram = nc, dram


class Steps:

    def __init__(self, sem):
        self.sem, self.n = sem, 0

    def on(self, eng):
        self.eng = eng
        return self

    def __call__(self, ins):
        self.n += 1
        ins.then_inc(self.sem, 1)
        self.eng.wait_ge(self.sem, self.n)


def words(c, at, *shape, rows=P):
    n = 1
    for s in shape:
        n *= s
    v = c.arena[0:rows, at:at + n]
    if len(shape) == 1:
        return v
    names = "abcd"[:len(shape)]
    return v.rearrange(f"p ({' '.join(names)}) -> p {' '.join(names)}", **dict(zip(names, shape)))


def cst(c, at, n, rows=P):
    return c.arena[0:rows, A_CST + at:A_CST + at + n]


def over(ap, axis, shape):
    return ap.unsqueeze(axis).broadcast_to(shape)


def bank(c, i, n=512, rows=P):
    return c.ps[0:rows, 512 * i:512 * i + n]


def tile_cols(n):
    return slice(P * n, P * n + ROWS[n])


A_HA = A_FREE
A_HD = A_HA + NT * 768
A_SIL = A_HD + NT * 520
A_NEWC = A_SIL + CCH * TOK
A_CS = A_NEWC + CCH * 27
A_CW = A_CS + CONV
A_RING = A_CW + CCH * 28
A_HC = A_RING + 4 * KD * 520
assert A_HC + CCH * PADW <= ARENA

PIECES = [(C_CONV, 512), (C_CONV + 512, 512), (C_CONV + 1024, 512), (C_B, 520), (C_Q, 512), (C_K, 256)]


def projection_plan():
    plan = [("x", None, n, h) for n in range(NT) for h in range(2)] + [("state", None)]
    for p in range(3):
        plan += [("conv", p, 4 * p + j, h) for j in range(4) for h in range(2)]
    plan += [("token", 3, n, 0, 8, "b") for n in range(NT)]
    plan += [("token", 3, n, 8, 512, "z") for n in range(NT)]
    plan += [("token", 4, n, 0, 512, "q") for n in range(NT)]
    plan += [("token", 5, n, 0, 256, "kv") for n in range(NT)]
    return plan


def phase_project(c):
    nc, d = c.nc, c.dram
    xa = words(c, A_X, NT, D)
    xt = words(c, A_XT, KD, TOK)
    ha = words(c, A_HA, NT, 768)
    hd = words(c, A_HD, NT, 520)
    sil = words(c, A_SIL, CCH, TOK)
    newc = words(c, A_NEWC, CCH, 27)
    cs = words(c, A_CS, CONV, rows=28)
    cw = words(c, A_CW, CCH, 28)
    ring = words(c, A_RING, 4, KD, 520)
    hc = words(c, A_HC, CCH, PADW)
    hcs = hc[:, :, 3 + SEQ:].rearrange("p c (b j) -> p c b j", j=7)
    ident = cst(c, K_ID, P)
    plan = projection_plan()
    first, last = {}, {}
    for g, item in enumerate(plan):
        first.setdefault(item[1], g)
        last[item[1]] = g
    conv_group = {item[2]: g for g, item in enumerate(plan) if item[0] == "conv" and item[3] == 1}
    state_group = next(g for g, item in enumerate(plan) if item[0] == "state")

    consts_in, x_in, state_in = c.sem("consts_in"), [c.sem(f"x_in{n}") for n in range(NT)], c.sem("conv_state_in")
    piece_in = [c.sem(f"w_in_piece{s}") for s in range(4)]
    group_done, evacuated = c.sem("proj_group_done"), c.sem("proj_evacuated")
    pads, conv_done, sil_done = c.sem("conv_pads_set"), c.sem("conv_chunk_done"), c.sem("conv_silu_done")

    with nc.Block(no_gpsimd_drain=True) as block:
        @block.sync
        def _(sp):
            sp.dma_start(cst(c, 0, K_N), d.consts).then_inc(consts_in, 16)
            for n in range(NT):
                src = d.x_prompt[0, P * n:P * n + P] if n < 4 else d.x_sample.rearrange("b l d -> (b l) d")
                sp.dma_start(xa[0:ROWS[n], n], src).then_inc(x_in[n], 16)
            sp.dma_start(cs[0:24], d.state_dn_conv[0].rearrange("b j c -> (b j) c")).then_inc(state_in, 16)
            sp.dma_start(cs[24:28], d.w_conv[0]).then_inc(state_in, 16)
            for p, (c0, w) in enumerate(PIECES):
                if p >= 4:
                    sp.wait_ge(group_done, last[p - 4] + 1)
                src = d.w_in[0].rearrange("(k p) c -> p k c", p=P)[:, :, c0:c0 + w]
                sp.dma_start(ring[:, p % 4, :, 0:w], src).then_inc(piece_in[p % 4], 16)

        @block.tensor
        def _(pe):
            pe.wait_ge(consts_in, 16)
            for g, item in enumerate(plan):
                if g >= 8:
                    pe.wait_ge(evacuated, g - 7)
                kind, p = item[0], item[1]
                if p is not None and first[p] == g:
                    pe.wait_ge(piece_in[p % 4], 16 * (p // 4 + 1))
                if p == 0 and first[p] == g:
                    pe.wait_ge(evacuated, 2 * NT)
                if kind == "x":
                    n, h = item[2:]
                    r = ROWS[n]
                    if h == 0:
                        pe.wait_ge(x_in[n], 16)
                    for j in range(4):
                        k = 4 * h + j
                        ins = pe.transpose(bank(c, g % 8)[:, r * j:r * j + r], xa[0:r, n, P * k:P * k + P], ident[0:r, 0:r])
                elif kind == "state":
                    pe.wait_ge(state_in, 32)
                    for j in range(CCH):
                        ins = pe.transpose(bank(c, g % 8)[:, 28 * j:28 * j + 28], cs[:, P * j:P * j + P], ident[0:28, 0:28])
                elif kind == "conv":
                    ch, h = item[2:]
                    j = ch % 4
                    for k in range(KD):
                        ins = pe.matmul(bank(c, g % 8, HALF), ring[:, p % 4, k, P * j:P * j + P],
                                        xt[:, k, HALF * h:HALF * h + HALF], start=(k == 0), stop=(k == KD - 1))
                else:
                    n, c0, w = item[2:5]
                    for k in range(KD):
                        ins = pe.matmul(bank(c, g % 8, w, ROWS[n]), xt[:, k, tile_cols(n)], ring[:, p % 4, k, c0:c0 + w],
                                        start=(k == 0), stop=(k == KD - 1))
                ins.then_inc(group_done, 1)

        @block.scalar
        def _(act):
            def silu(ch):
                act.wait_ge(conv_done, ch + 1)
                act.activation(sil[:, ch], sil[:, ch], ACT.Silu).then_inc(sil_done, 1)

            for g, item in enumerate(plan):
                act.wait_ge(group_done, g + 1)
                kind = item[0]
                src = bank(c, g % 8)
                if kind == "x":
                    n, h = item[2:]
                    r = ROWS[n]
                    ins = act.copy(xt[:, 4 * h:4 * h + 4, tile_cols(n)], src[:, 0:4 * r].rearrange("p (k t) -> p k t", k=4))
                elif kind == "state":
                    ins = act.copy(cw[:], src[:, 0:CCH * 28].rearrange("p (c j) -> p c j", j=28))
                elif kind == "conv":
                    ch, h = item[2:]
                    if h == 0:
                        ins = act.copy(hc[:, ch, 3:3 + HALF], src[:, 0:HALF])
                    else:
                        act.copy(hc[:, ch, 3 + HALF:3 + SEQ], src[:, 0:SEQ - HALF])
                        ins = act.copy(hcs[:, ch, :, 3:7], src[:, SEQ - HALF:HALF].rearrange("p (b l) -> p b l", l=NL))
                else:
                    n, c0, w, what = item[2:]
                    dst = {"b": hd[:, n, 0:8], "z": hd[:, n, 8:520], "q": ha[:, n, 0:512], "kv": ha[:, n, 512:768]}[what]
                    if what in "bz" and n == 4:
                        act.wait_ge(pads, 1)
                    ins = act.copy(dst[0:ROWS[n]], src[0:ROWS[n], 0:w])
                ins.then_inc(evacuated, 1)
                if kind == "conv" and item[3] == 1 and item[2] >= 1:
                    silu(item[2] - 1)
            silu(CCH - 1)

        @block.vector
        def _(v):
            step = c.dve_step.on(v)
            v.memset(hc[:, :, 0:3], 0.0)
            v.memset(hd[:, 4, :], 0.0).then_inc(pads, 1)
            v.wait_ge(evacuated, state_group + 1)
            v.wait_ge(pads, 1)
            for j in range(CCH):
                ins = v.tensor_copy(hcs[:, j, :, 0:3], cw[:, j, 0:24].rearrange("p (b j) -> p b j", j=3))
            step(ins)
            for ch in range(CCH):
                v.wait_ge(evacuated, conv_group[ch] + 1)
                yp = sil[:, ch, 0:SEQ]
                ys = sil[:, ch, SEQ:TOK].rearrange("p (b l) -> p b l", l=NL)
                for j in range(4):
                    w = cw[:, ch, 24 + j:25 + j]
                    if j == 0:
                        v.tensor_scalar(yp, hc[:, ch, 0:SEQ], w, None, ALU.mult)
                        ins = v.tensor_scalar(ys, hcs[:, ch, :, 0:NL], w, None, ALU.mult)
                    else:
                        v.scalar_tensor_tensor(yp, hc[:, ch, j:j + SEQ], w, yp, ALU.mult, ALU.add)
                        ins = v.scalar_tensor_tensor(ys, hcs[:, ch, :, j:j + NL], w, ys, ALU.mult, ALU.add)
                    if j < 3:
                        step(ins)
                ins.then_inc(conv_done, 1)
                v.tensor_copy(newc[:, ch, 0:3], hc[:, ch, SEQ:SEQ + 3])
                ins = v.tensor_copy(newc[:, ch, 3:27].rearrange("p (b j) -> p b j", j=3), hcs[:, ch, :, 4:7])
            step(ins)


A_CT = A_SIL + CCH * TOK + CCH * 27
A_MIX = A_CT + NT * CONV
A_SWA = A_MIX + NT * D
A_QR = A_SWA
A_QT = A_QR + NT * 640
A_SM = A_QT + 5 * TOK
A_PT = A_SM + 2 * 1024
A_KC = A_PT + 1024
A_VC = A_KC + NB * P
A_KCT = A_VC + NB * P
A_QM = A_KCT + NB * P
A_NCO = A_QM + NB * P
A_RT = A_SM
A_SW1 = A_NCO + CONV
assert A_SW1 + 300 <= ARENA


def phase_window(c):
    nc, d = c.nc, c.dram
    ha = words(c, A_HA, NT, 768)
    sil = words(c, A_SIL, CCH, TOK)
    newc = words(c, A_NEWC, CCH, 27)
    ct = words(c, A_CT, NT, CONV)
    mix = words(c, A_MIX, NT, D)
    mixt = words(c, A_XT, KD, TOK)
    qr = words(c, A_QR, NT, 640)
    qt = words(c, A_QT, 5, TOK)
    sm = words(c, A_SM, 2, 4, 2 * P)
    pt = words(c, A_PT, 8, P)
    kc, vc, kct, qm = (words(c, a, NB, P) for a in (A_KC, A_VC, A_KCT, A_QM))
    nco = words(c, A_NCO, CONV, rows=27)
    rt = words(c, A_RT, 4, 10, 32)
    sink = words(c, A_SW1, 8)
    sink_rows = words(c, A_SW1 + 8, 2)
    mx, nmx, dsk, ssum, den = (words(c, A_SW1 + 16 + 16 * i, 4, 4) for i in range(5))
    qs = words(c, A_SW1 + 96, 4 * SAMP)
    ident = cst(c, K_ID, P)

    sink_in, cache_in = c.sem("sinks_in"), c.sem("window_cache_in")
    turned, turned_out = c.sem("turned"), c.sem("turned_out")
    rotated = c.sem("tile_rotated")
    newc_out = c.sem("new_conv_rows_ready")
    scored, masked, expd, ptd, pt_out, av_done, av_out = (
        c.sem(x) for x in ("scores_done", "scores_masked", "exp_done", "probs_turned", "probs_turned_out", "window_av_done",
                           "window_av_out"))
    masked_s = c.sem("sample_scores_masked")
    stored = c.sem("window_stored")
    units = [(n, kv) for n in range(4) for kv in range(2)]

    turns = [("new", q) for q in range(3)] + [("conv", n, q) for n in range(NT) for q in range(3)]
    turns += [(w, n) for n in range(NT) for w in ("q", "k")] + [("cache", h) for h in range(2)]
    turn_no = {t: i for i, t in enumerate(turns)}

    with nc.Block(no_gpsimd_drain=True) as block:
        @block.sync
        def _(sp):
            sp.dma_start(sink, d.attn_sinks[0].partition_broadcast(P)).then_inc(sink_in, 16)
            for j in range(4):
                sp.dma_start(sink_rows[SAMP * j:SAMP * j + SAMP], d.attn_sinks[0, j:8:4].partition_broadcast(SAMP),
                             allow_slow_non_contiguous=True).then_inc(sink_in, 16)
            sp.dma_start(kc[:], d.cache_swa_k[0].rearrange("b w h d -> w b (h d)")).then_inc(cache_in, 16)
            sp.dma_start(vc[:], d.cache_swa_v[0].rearrange("b w h d -> w b (h d)")).then_inc(cache_in, 16)
            sp.wait_ge(turned_out, 3)
            sp.dma_start(d.dn_conv_prompt[0, 0], nco[0:3]).then_inc(stored, 16)
            sp.dma_start(d.dn_conv_sample[0].rearrange("b j c -> (b j) c"), nco[3:27]).then_inc(stored, 16)
            sp.wait_ge(rotated, NT)
            flat = "b w h d -> b w (h d)"
            sp.dma_start(d.swa_k_prompt[0, 0].rearrange("w h d -> w (h d)"), qr[:, 3, 512:640]).then_inc(stored, 16)
            sp.dma_start(d.swa_v_prompt[0, 0].rearrange("w h d -> w (h d)"), ha[:, 3, 640:768]).then_inc(stored, 16)
            for b in range(NB):
                sp.dma_start(d.swa_k_sample[0].rearrange(flat)[b, P - NL:P], qr[NL * b:NL * b + NL, 4, 512:640]).then_inc(stored, 16)
                sp.dma_start(d.swa_v_sample[0].rearrange(flat)[b, P - NL:P], ha[NL * b:NL * b + NL, 4, 640:768]).then_inc(stored, 16)
            sp.wait_ge(cache_in, 32)
            sp.dma_start(d.swa_k_sample[0, :, 0:P - NL].rearrange("b w h d -> w b (h d)"), kc[NL:P]).then_inc(stored, 16)
            sp.dma_start(d.swa_v_sample[0, :, 0:P - NL].rearrange("b w h d -> w b (h d)"), vc[NL:P]).then_inc(stored, 16)
            sp.wait_ge(stored, 16 * (4 + 2 * NB + 2))

        @block.tensor
        def _(pe):
            for i, t in enumerate(turns):
                if i >= 4:
                    pe.wait_ge(turned_out, i - 3)
                o = bank(c, i % 4)
                if t[0] == "new":
                    for j in range(4):
                        ins = pe.transpose(o[0:27, P * j:P * j + P], newc[:, 4 * t[1] + j], ident)
                elif t[0] == "conv":
                    _, n, q = t
                    for j in range(4):
                        ins = pe.transpose(o[0:ROWS[n], P * j:P * j + P], sil[:, 4 * q + j, tile_cols(n)], ident)
                elif t[0] in "qk":
                    n, r = t[1], ROWS[t[1]]
                    pe.wait_ge(rotated, n + 1)
                    for j in range(4 if t[0] == "q" else 1):
                        c0 = P * j + (512 if t[0] == "k" else 0)
                        ins = pe.transpose(o[:, r * j:r * j + r], qr[0:r, n, c0:c0 + P], ident[0:r, 0:r])
                else:
                    pe.wait_ge(cache_in, 32)
                    for j in range(4):
                        ins = pe.transpose(o[:, P * j:P * j + P], kc[:, 4 * t[1] + j], ident)
                ins.then_inc(turned, 1)

            def scores(u):
                n, kv = units[u]
                if u >= 2:
                    pe.wait_ge(masked, u - 1)
                hp = slice(HD * kv, HD * kv + HD)
                for j in range(4):
                    lo = 0 if n else P
                    o = bank(c, 2 * (u % 2) + j // 2)[:, 256 * (j % 2) + lo:256 * (j % 2) + 256]
                    keys = qt[hp, 4, P * n - P + lo:P * n + P]
                    ins = pe.matmul(o, qt[hp, j, tile_cols(n)], keys, start=True, stop=True)
                ins.then_inc(scored, 1)

            def values(u):
                n, kv = units[u]
                pe.wait_ge(expd, u + 1)
                if u >= 1:
                    pe.wait_ge(pt_out, u)
                halves = (0, 1) if n else (1,)
                for h in halves:
                    for j in range(4):
                        ins = pe.transpose(bank(c, 4 + h)[:, P * j:P * j + P], sm[:, u % 2, j, P * h:P * h + P], ident)
                ins.then_inc(ptd, 1)
                pe.wait_ge(pt_out, u + 1)
                if u >= 2:
                    pe.wait_ge(av_out, u - 1)
                for j in range(4):
                    for h in halves:
                        v = ha[:, n - 1 + h, 640 + HD * kv:704 + HD * kv]
                        ins = pe.matmul(bank(c, 6 + u % 2)[:, HD * j:HD * j + HD], pt[:, 4 * h + j], v,
                                        start=(h == halves[0]), stop=(h == 1))
                ins.then_inc(av_done, 1)

            pe.wait_ge(turned_out, len(turns))
            for u in range(len(units) + 1):
                if u < len(units):
                    scores(u)
                if u:
                    values(u - 1)

            nu = len(units)
            pe.wait_ge(masked, nu + 1)
            for kv in range(2):
                hp = slice(HD * kv, HD * kv + HD)
                o = bank(c, kv)
                for b in range(NB):
                    pe.matmul(o[:, 0:P], qm[hp, b], kct[hp, b], start=(b == 0), stop=(b == NB - 1))
                ins = pe.matmul(o[:, P:P + SAMP], qs[hp], qt[hp, 4, SEQ:TOK], start=True, stop=True)
                ins.then_inc(scored, 1)
            pe.wait_ge(pt_out, nu)
            pe.wait_ge(av_out, nu)
            for kv in range(2):
                pe.wait_ge(masked, nu + 2 + kv)
                pe.transpose(bank(c, 4 + kv)[:, 0:P], sm[:, kv, 0, 0:P], ident)
                pe.transpose(bank(c, 4 + kv)[0:SAMP, P:2 * P], sm[:, kv, 0, P:P + SAMP], ident).then_inc(ptd, 1)
            for kv in range(2):
                pe.wait_ge(pt_out, nu + 1 + kv)
                pk = pt[:, 2 * kv].rearrange("p (j q b l) -> p q b j l", q=2, b=NB, l=NL)
                pn = pt[0:SAMP, 2 * kv + 1].rearrange("p (j q t) -> p q j t", q=2, t=SAMP)
                for q in range(2):
                    o = bank(c, 6 + kv)[HD * q:HD * q + HD, 0:2 * SAMP].rearrange("p (j b l) -> p b j l", b=NB, l=NL)
                    pe.matmul(bank(c, 6 + kv)[HD * q:HD * q + HD, 0:2 * SAMP], ha[0:SAMP, 4, 640 + HD * kv:704 + HD * kv],
                              pn[:, q], start=True, stop=False)
                    for b in range(NB):
                        ins = pe.matmul(o[:, b], vc[:, b, HD * kv:HD * kv + HD], pk[:, q, b], start=False, stop=(b == NB - 1))
                ins.then_inc(av_done, 1)

        @block.scalar
        def _(act):
            for i, t in enumerate(turns):
                act.wait_ge(turned, i + 1)
                o = bank(c, i % 4)
                if t[0] == "new":
                    ins = act.copy(nco[:, 512 * t[1]:512 * t[1] + 512], o[0:27])
                elif t[0] == "conv":
                    r = ROWS[t[1]]
                    ins = act.copy(ct[0:r, t[1], 512 * t[2]:512 * t[2] + 512], o[0:r])
                elif t[0] == "q":
                    r = ROWS[t[1]]
                    ins = act.copy(qt[:, 0:4, tile_cols(t[1])], o[:, 0:4 * r].rearrange("p (j t) -> p j t", j=4))
                elif t[0] == "k":
                    ins = act.copy(qt[:, 4, tile_cols(t[1])], o[:, 0:ROWS[t[1]]])
                else:
                    ins = act.copy(kct[:, 4 * t[1]:4 * t[1] + 4], o.rearrange("p (b w) -> p b w", b=4))
                ins.then_inc(turned_out, 1)
            for u, (n, kv) in enumerate(units):
                act.wait_ge(masked, u + 1)
                lo = 0 if n else P
                act.activation(dsk[:, u % 4], dsk[:, u % 4], ACT.Exp)
                for j in range(4):
                    ins = act.activation(sm[:, u % 2, j, lo:], sm[:, u % 2, j, lo:], ACT.Exp, bias=nmx[:, u % 4, j:j + 1],
                                         accum_out=ssum[:, u % 4, j:j + 1])
                ins.then_inc(expd, 1)
                act.wait_ge(ptd, u + 1)
                for h in ((0, 1) if n else (1,)):
                    ins = act.copy(pt[:, 4 * h:4 * h + 4], bank(c, 4 + h).rearrange("p (j q) -> p j q", j=4))
                ins.then_inc(pt_out, 1)
            nu = len(units)
            for kv in range(2):
                act.wait_ge(masked_s, kv + 1)
                act.activation(dsk[:, kv, 0:1], dsk[:, kv, 0:1], ACT.Exp)
                act.activation(sm[:, kv, 0, 0:P + SAMP], sm[:, kv, 0, 0:P + SAMP], ACT.Exp, bias=nmx[:, kv, 0:1],
                               accum_out=ssum[:, kv, 0:1]).then_inc(expd, 1)
            for kv in range(2):
                act.wait_ge(ptd, nu + 1 + kv)
                act.copy(pt[:, 2 * kv], bank(c, 4 + kv)[:, 0:P])
                act.copy(pt[0:SAMP, 2 * kv + 1], bank(c, 4 + kv)[0:SAMP, P:2 * P]).then_inc(pt_out, 1)
            for kv in range(2):
                act.wait_ge(av_done, nu + 1 + kv)
                act.copy(mixt[:, 2 * kv:2 * kv + 2, SEQ:TOK],
                         bank(c, 6 + kv)[:, 0:2 * SAMP].rearrange("p (j t) -> p j t", j=2)).then_inc(av_out, 1)
            act.wait_ge(av_out, nu + 2)

        @block.vector
        def _(v):
            step = c.dve_step.on(v)
            for n in range(NT):
                r = ROWS[n]
                h = ha[0:r, n, 0:640].rearrange("p (h s d) -> p s h d", s=2, d=32)
                cos = over(cst(c, K_COS + 32 * n, 32, r), 1, [r, 10, 32])
                sin = over(cst(c, K_SIN + 32 * n, 32, r), 1, [r, 10, 32])
                a, b_, e, f = (rt[0:r, i] for i in range(4))
                v.tensor_tensor(a, h[:, 0], cos, ALU.mult)
                v.tensor_tensor(b_, h[:, 1], sin, ALU.mult)
                v.tensor_tensor(e, h[:, 1], cos, ALU.mult)
                step(v.tensor_tensor(f, h[:, 0], sin, ALU.mult))
                q = qr[0:r, n, 0:512].rearrange("p (j g s d) -> p s g j d", g=2, s=2, d=32)
                k = qr[0:r, n, 512:640].rearrange("p (g s d) -> p s g d", s=2, d=32)
                for s, (x, y, op) in enumerate(((a, b_, ALU.subtract), (e, f, ALU.add))):
                    for g in range(2):
                        v.tensor_tensor(q[:, s, g], x[:, 4 * g:4 * g + 4], y[:, 4 * g:4 * g + 4], op)
                    ins = v.tensor_tensor(k[:, s], x[:, 8:10], y[:, 8:10], op)
                ins.then_inc(rotated, 1)
                v.wait_ge(rotated, n + 1)
            v.wait_ge(sink_in, 80)

            def mask(u):
                n, kv = units[u]
                lo = 0 if n else P
                v.wait_ge(scored, u + 1)
                if u >= 2:
                    v.wait_ge(ptd, u - 1)
                for i in range(2):
                    s = bank(c, 2 * (u % 2) + i).rearrange("p (j w) -> p j w", j=2)[:, :, lo:]
                    m = over(cst(c, K_SWA + lo, 2 * P - lo), 1, [P, 2, 2 * P - lo])
                    ins = v.scalar_tensor_tensor(sm[:, u % 2, 2 * i:2 * i + 2, lo:], s, HD ** -0.5, m, ALU.mult, ALU.add)
                step(ins)
                step(v.tensor_reduce(mx[:, u % 4], sm[:, u % 2, :, lo:], AX, ALU.max))
                sk = sink[:, 4 * kv:4 * kv + 4]
                step(v.tensor_tensor(mx[:, u % 4], mx[:, u % 4], sk, ALU.max))
                v.tensor_scalar(nmx[:, u % 4], mx[:, u % 4], -1.0, None, ALU.mult)
                v.tensor_tensor(dsk[:, u % 4], sk, mx[:, u % 4], ALU.subtract).then_inc(masked, 1)

            def divide(u):
                n, kv = units[u]
                v.wait_ge(expd, u + 1)
                step(v.tensor_tensor(den[:, u % 4], ssum[:, u % 4], dsk[:, u % 4], ALU.add))
                step(v.reciprocal(den[:, u % 4], den[:, u % 4]))
                v.wait_ge(av_done, u + 1)
                o = bank(c, 6 + u % 2)[:, 0:4 * HD].rearrange("p (j d) -> p j d", j=4)
                v.tensor_tensor(mix[:, n, 256 * kv:256 * kv + 256].rearrange("p (j d) -> p j d", j=4), o,
                                over(den[:, u % 4], 2, [P, 4, HD]), ALU.mult).then_inc(av_out, 1)

            nu = len(units)
            v.wait_ge(turned_out, len(turns))
            for u in range(nu + 1):
                if u < nu:
                    mask(u)
                if u:
                    divide(u - 1)
            v.tensor_copy(qs.rearrange("p (j t) -> p j t", j=4), qt[:, 0:4, SEQ:TOK])
            v.tensor_tensor(qm[:].rearrange("p b (j t) -> p b j t", j=4), over(qt[:, 0:4, SEQ:TOK], 1, [P, NB, 4, SAMP]),
                            over(cst(c, K_BM, NB * SAMP).rearrange("p (b t) -> p b t", b=NB), 2, [P, NB, 4, SAMP]),
                            ALU.mult).then_inc(masked, 1)
            for kv in range(2):
                v.wait_ge(scored, nu + 1 + kv)
                v.wait_ge(ptd, nu)
                step(v.scalar_tensor_tensor(sm[:, kv, 0, 0:P + SAMP], bank(c, kv, P + SAMP), HD ** -0.5,
                                            cst(c, K_SMP, P + SAMP), ALU.mult, ALU.add))
                step(v.tensor_reduce(mx[:, kv, 0:1], sm[:, kv, 0, 0:P + SAMP], AX, ALU.max))
                step(v.tensor_tensor(mx[:, kv, 0:1], mx[:, kv, 0:1], sink_rows[:, kv:kv + 1], ALU.max))
                v.tensor_scalar(nmx[:, kv, 0:1], mx[:, kv, 0:1], -1.0, None, ALU.mult)
                v.tensor_tensor(dsk[:, kv, 0:1], sink_rows[:, kv:kv + 1], mx[:, kv, 0:1], ALU.subtract).then_inc(masked_s, 1)
            for kv in range(2):
                v.wait_ge(expd, nu + 1 + kv)
                step(v.tensor_tensor(den[:, kv, 0:1], ssum[:, kv, 0:1], dsk[:, kv, 0:1], ALU.add))
                step(v.reciprocal(den[:, kv, 0:1], den[:, kv, 0:1]))
                v.tensor_scalar(sm[:, kv, 0, 0:P + SAMP], sm[:, kv, 0, 0:P + SAMP], den[:, kv, 0:1], None,
                                ALU.mult).then_inc(masked, 1)


UW = 4 * 4 * P + 4 * SAMP
A_QT2 = A_HA
A_S = A_QT2 + 2 * 3 * 512
A_NG = A_S + 512
A_S0 = A_SIL
A_AM = A_S0 + NB * 512
A_VN = A_AM + 1024
A_GB = A_VN + 512
A_QE = A_GB + 512
assert A_QE + 512 <= A_CT
A_T = A_MIX + NT * D
A_TT, A_AT, A_M1, A_QET, A_QK = (A_T + UW * i for i in range(1, 6))
A_X1 = A_T + 6 * UW
A_WM = A_X1 + 1024
A_SM3 = A_WM + 2 * NB * SAMP
assert A_SM3 + 372 <= ARENA


def phase_delta(c):
    nc, d = c.nc, c.dram
    ct, mix, hd = words(c, A_CT, NT, CONV), words(c, A_MIX, NT, D), words(c, A_HD, NT, 520)
    qkt = words(c, A_QT2, 2, 3, 512)
    s_p, s_s = words(c, A_S, DNH, DK), words(c, A_S0, NB, DNH, DK)
    ng = words(c, A_NG, DK)
    am, vn, gb, qe = words(c, A_AM, 2, 512), words(c, A_VN, DNH, DK), words(c, A_GB, DNH, P), words(c, A_QE, 512)
    x1 = words(c, A_X1, 1024)
    wm = words(c, A_WM, 2, NB, SAMP)
    at = [A_SM3]

    def small(*shape):
        n = 1
        for s in shape:
            n *= s
        at[0] += n
        assert at[0] <= ARENA
        return words(c, at[0] - n, *shape)

    ss, beta, g, tz = small(NT, 8), small(NT, 4), small(NT, 4), small(NT, 4)
    gc, eg = small(NT, 8), small(NT, 8)
    egl, egs = small(4, 4), small(4, NB)
    alog, dtb, ms = small(4), small(4), small(NT, 4)

    def unit(base, n, rows=P):
        r = ROWS[n]
        return c.arena[0:rows, base + 512 * n:base + 512 * n + 4 * r].rearrange("p (h t) -> p h t", h=4)

    def mask(k_prompt, k_sample, n):
        return cst(c, k_prompt, P) if n < 4 else cst(c, k_sample, SAMP, SAMP)

    ident = cst(c, K_ID, P)
    s = c.sem
    params_in, states_in = s("delta_params_in"), s("delta_states_in")
    z_done, small_act = s("delta_z_silu"), s("delta_small_by_act")
    squares, betas = s("delta_squares_summed"), s("delta_small_by_dve")
    spread, cums, gc_out, dd_set, exps, dd_exp = (s("delta_" + x) for x in ("decay_spread", "cumulated", "cumulated_out",
                                                                         "differences_set", "row_exps", "decay_exps"))
    prepared, turned3, turned3_act, turned3_dve, kk, at_set = (s("delta_" + x) for x in (
        "rows_prepared", "rows_turned", "turned_out_act", "turned_out_dve", "products", "a_set"))
    am_set, m1, m1_out, pp, t_new = (s("inverse_" + x) for x in ("a_masked", "m1", "m1_out", "products", "updated"))
    uw, u_out, w_out = s("delta_uw"), s("delta_u_out"), s("delta_w_out")
    ws, vnew, od, o_out, sd, s_new = (s("scan_" + x) for x in ("ws", "new_values", "outputs", "outputs_out", "state_delta",
                                                               "state_new"))
    wm_set, km_set = s("sample_w_masked"), s("sample_k_masked")
    root, sroot = s("delta_mean_squares"), s("delta_roots")
    s_zero = s("state_cleared")
    stored = s("delta_stored")
    items = [(lev, n) for lev in range(LEVELS) for n in range(NT) if n < 4 or lev < 2]
    item_no = {x: i for i, x in enumerate(items)}

    with nc.Block(no_gpsimd_drain=True) as block:
        @block.sync
        def _(sp):
            sp.dma_start(alog, d.dn_a_log[0].partition_broadcast(P)).then_inc(params_in, 16)
            sp.dma_start(dtb, d.dn_dt_bias[0].partition_broadcast(P)).then_inc(params_in, 16)
            sp.dma_start(ng, d.dn_norm_g[0].partition_broadcast(P)).then_inc(params_in, 16)
            sp.dma_start(s_s[:].rearrange("p b h v -> p (b h) v"), d.state_dn[0].rearrange("b h k v -> k (b h) v")).then_inc(states_in, 16)
            sp.wait_ge(s_new, 4)
            sp.dma_start(d.dn_state_prompt[0, 0].rearrange("h k v -> k h v"), s_p).then_inc(stored, 16)
            sp.wait_ge(s_new, 8)
            sp.dma_start(d.dn_state_sample[0].rearrange("b h k v -> k (b h) v"), s_s[:].rearrange("p b h v -> p (b h) v")).then_inc(stored, 16)
            sp.wait_ge(stored, 32)

        @block.tensor
        def _(pe):
            for n in range(NT):
                r = ROWS[n]
                ut, one = mask(K_UT, K_UTS, n), mask(K_ONE, K_ONES, n)
                pe.wait_ge(spread, n + 1)
                if n:
                    pe.wait_ge(gc_out, n)
                    pe.wait_ge(dd_set, n)
                pe.matmul(bank(c, 0, 4, r), ut, g[0:r, n], start=True, stop=True)
                pe.matmul(bank(c, 0, 8, r)[:, 4:8], one, g[0:r, n], start=True, stop=True)
                for h in range(DNH):
                    ins = pe.matmul(bank(c, 1)[:, r * h:r * h + r], gb[0:r, h], ut, start=True, stop=True)
                ins.then_inc(cums, 1)
                pe.wait_ge(prepared, n + 1)
                if n:
                    pe.wait_ge(turned3_act, n)
                    pe.wait_ge(turned3_dve, n)
                kb = x1[:, 0:512]
                for i, src in enumerate((ct[:, n, 0:512], ct[:, n, 512:1024], kb, qe)):
                    for h in range(DNH):
                        ins = pe.transpose(bank(c, 2 + i)[:, r * h:r * h + r], src[0:r, P * h:P * h + P], ident[0:r, 0:r])
                ins.then_inc(turned3, 1)
                pe.wait_ge(turned3_act, n + 1)
                pe.wait_ge(turned3_dve, n + 1)
                if n:
                    pe.wait_ge(at_set, n)
                q3 = [qkt[:, n % 2, i, 0:4 * r].rearrange("p (h t) -> p h t", h=4) for i in range(3)]
                for h in range(DNH):
                    pe.matmul(bank(c, 6, 512, r)[:, r * h:r * h + r], q3[1][:, h], q3[2][:, h], start=True, stop=True)
                for h in range(DNH):
                    ins = pe.matmul(bank(c, 7, 512, r)[:, r * h:r * h + r], q3[1][:, h], q3[0][:, h], start=True, stop=True)
                ins.then_inc(kk, 1)

            def first(i):
                lev, n = items[i]
                r = ROWS[n]
                pe.wait_ge(am_set, i + 1)
                if lev:
                    pe.wait_ge(t_new, item_no[lev - 1, n] + 1)
                if i >= 2:
                    pe.wait_ge(m1_out, i - 1)
                a = am[0:r, i % 2, 0:4 * r].rearrange("p (h t) -> p h t", h=4)
                for h in range(DNH):
                    ins = pe.matmul(bank(c, i % 2, 512, r)[:, r * h:r * h + r], a[:, h], unit(A_T, n, r)[:, h], start=True, stop=True)
                ins.then_inc(m1, 1)

            def second(i):
                lev, n = items[i]
                r = ROWS[n]
                pe.wait_ge(m1_out, i + 1)
                if i >= 2:
                    pe.wait_ge(t_new, i - 1)
                t, tt, x = unit(A_T, n, r), unit(A_TT, n, r), unit(A_M1, n, r)
                for h in range(DNH):
                    pe.matmul(bank(c, 2 + i % 2, 512, r)[:, r * h:r * h + r], tt[:, h], x[:, h], start=True, stop=True)
                for h in range(DNH):
                    ins = pe.matmul(bank(c, 4 + i % 2, 512, r)[:, r * h:r * h + r], x[:, h], tt[:, h], start=True, stop=True)
                ins.then_inc(pp, 1)

            pe.wait_ge(at_set, NT)
            for i in range(len(items) + 1):
                if i < len(items):
                    first(i)
                if i:
                    second(i - 1)

            pe.wait_ge(t_new, len(items))
            for n in range(NT):
                r = ROWS[n]
                if n >= 2:
                    pe.wait_ge(u_out, n - 1)
                    pe.wait_ge(w_out, n - 1)
                tt = unit(A_TT, n, r)
                for h in range(DNH):
                    pe.matmul(bank(c, n % 2, 512, r)[:, P * h:P * h + P], tt[:, h], ct[0:r, n, 1024 + P * h:1152 + P * h], start=True, stop=True)
                for h in range(DNH):
                    ins = pe.matmul(bank(c, 2 + n % 2)[:, r * h:r * h + r], ct[0:r, n, P * h:P * h + P], tt[:, h], start=True, stop=True)
                ins.then_inc(uw, 1)

            pe.wait_ge(u_out, NT)
            pe.wait_ge(w_out, NT)
            for n in range(4):
                if n:
                    pe.wait_ge(s_new, n)
                else:
                    pe.wait_ge(s_zero, 1)
                for h in range(DNH):
                    ins = pe.matmul(bank(c, 4)[:, P * h:P * h + P], unit(A_M1, n)[:, h], s_p[:, h], start=True, stop=True)
                ins.then_inc(ws, 1)
                pe.wait_ge(vnew, n + 1)
                for h in range(DNH):
                    ins = pe.matmul(bank(c, 5)[:, P * h:P * h + P], ct[:, n, 512 + P * h:640 + P * h], vn[:, h], start=True, stop=True)
                ins.then_inc(sd, 1)
                if n >= 2:
                    pe.wait_ge(o_out, n - 1)
                for h in range(DNH):
                    pe.matmul(bank(c, 6 + n % 2)[:, P * h:P * h + P], unit(A_QET, n)[:, h], s_p[:, h], start=True, stop=False)
                    ins = pe.matmul(bank(c, 6 + n % 2)[:, P * h:P * h + P], unit(A_QK, n)[:, h], vn[:, h], start=False, stop=True)
                ins.then_inc(od, 1)
            pe.wait_ge(states_in, 16)
            pe.wait_ge(o_out, 4)
            pe.wait_ge(s_new, 4)
            for h in range(DNH):
                pe.wait_ge(wm_set, h + 1)
                for b in range(NB):
                    ins = pe.matmul(bank(c, 4, 512, SAMP)[:, P * h:P * h + P], wm[:, 0, b], s_s[:, b, h], start=(b == 0), stop=(b == NB - 1))
                ins.then_inc(ws, 1)
                pe.wait_ge(vnew, 5 + h)
                for b in range(NB):
                    pe.matmul(bank(c, 6, 512, SAMP)[:, P * h:P * h + P], wm[:, 1, b], s_s[:, b, h], start=(b == 0), stop=False)
                pe.matmul(bank(c, 6, 512, SAMP)[:, P * h:P * h + P], unit(A_QK, 4, SAMP)[:, h], vn[0:SAMP, h], start=False, stop=True).then_inc(od, 1)
                pe.wait_ge(km_set, h + 1)
                km = x1[0:SAMP].rearrange("p (b k) -> p b k", b=NB)
                for b in range(NB):
                    ins = pe.matmul(bank(c, 2 + b // 4)[:, P * (b % 4):P * (b % 4) + P], km[:, b], vn[0:SAMP, h], start=True, stop=True)
                ins.then_inc(sd, 1)

        @block.scalar
        def _(act):
            step = c.act_step.on(act)
            for n in range(NT):
                ins = act.activation(hd[0:ROWS[n], n, 8:520], hd[0:ROWS[n], n, 8:520], ACT.Silu)
            ins.then_inc(z_done, 1)
            act.wait_ge(params_in, 48)
            act.activation(beta[:], hd[:, :, 0:4], ACT.Exp, scale=-1.0).then_inc(small_act, 1)
            act.activation(alog, alog, ACT.Exp).then_inc(small_act, 1)
            act.wait_ge(betas, 1)
            act.activation(g[:], g[:], ACT.Exp, scale=-1.0).then_inc(small_act, 1)
            act.wait_ge(betas, 2)
            act.activation(g[:], g[:], ACT.Ln).then_inc(small_act, 1)
            act.wait_ge(squares, 1)
            act.activation(ss[:], ss[:], ACT.Sqrt).then_inc(small_act, 1)
            for n in range(NT):
                r = ROWS[n]
                act.wait_ge(gc_out, n + 1)
                act.activation(eg[0:r, n], eg[0:r, n], ACT.Exp)
                total = egl[:, n] if n < 4 else egs[:]
                act.activation(total, total, ACT.Exp).then_inc(exps, 1)
                act.wait_ge(dd_set, n + 1)
                dd = x1[0:r, 512:512 + 4 * r]
                act.activation(dd, dd, ACT.Exp).then_inc(dd_exp, 1)
                act.wait_ge(turned3, n + 1)
                act.copy(qkt[:, n % 2, 1, 0:4 * r], bank(c, 3, 4 * r))
                act.copy(qkt[:, n % 2, 2, 0:4 * r], bank(c, 4, 4 * r)).then_inc(turned3_act, 1)
            for i, (lev, n) in enumerate(items):
                r = ROWS[n]
                act.wait_ge(m1, i + 1)
                act.copy(unit(A_M1, n, r), bank(c, i % 2, 4 * r, r).rearrange("p (h t) -> p h t", h=4)).then_inc(m1_out, 1)
            for n in range(NT):
                r = ROWS[n]
                act.wait_ge(uw, n + 1)
                act.copy(unit(A_M1, n), bank(c, 2 + n % 2, 4 * r).rearrange("p (h t) -> p h t", h=4)).then_inc(w_out, 1)
            for n in range(4):
                act.wait_ge(od, n + 1)
                act.copy(mix[:, n, 512:1024], bank(c, 6 + n % 2)).then_inc(o_out, 1)
            act.wait_ge(od, 8)
            act.copy(mix[0:SAMP, 4, 512:1024], bank(c, 6, 512, SAMP)).then_inc(o_out, 1)
            act.wait_ge(root, 1)
            act.activation(ms[:], ms[:], ACT.Sqrt).then_inc(sroot, 1)

        @block.vector
        def _(v):
            step = c.dve_step.on(v)
            step(v.memset(ss[:], 0.0))
            for n in range(NT):
                r = ROWS[n]
                step(v.tensor_tensor(x1[0:r], ct[0:r, n, 0:1024], ct[0:r, n, 0:1024], ALU.mult))
                step(v.tensor_reduce(ss[0:r, n], x1[0:r].rearrange("p (h k) -> p h k", h=8), AX, ALU.add))
            v.tensor_scalar(ss[:], ss[:], RMS_EPS, None, ALU.add).then_inc(squares, 1)
            v.wait_ge(params_in, 48)
            step(v.tensor_tensor(tz[:], hd[:, :, 4:8], over(dtb, 1, [P, NT, 4]), ALU.add))
            v.scalar_tensor_tensor(g[:], tz[:], -1.0, tz[:], ALU.mult, ALU.max).then_inc(betas, 1)
            v.wait_ge(small_act, 2)
            step(v.tensor_scalar(beta[:], beta[:], 1.0, None, ALU.add))
            step(v.reciprocal(beta[:], beta[:]))
            v.wait_ge(small_act, 3)
            v.tensor_scalar(g[:], g[:], 1.0, None, ALU.add).then_inc(betas, 1)
            v.wait_ge(small_act, 4)
            step(v.scalar_tensor_tensor(g[:], tz[:], 0.0, g[:], ALU.max, ALU.add))
            step(v.scalar_tensor_tensor(g[:], g[:], -1.0, over(alog, 1, [P, NT, 4]), ALU.mult, ALU.mult))
            v.wait_ge(small_act, 5)
            step(v.reciprocal(ss[:], ss[:]))
            step(v.tensor_scalar(ss[:, :, 0:4], ss[:, :, 0:4], DK ** -0.5, None, ALU.mult))

            def rows(n, a, k, scale, out, heads=4):
                r = ROWS[n]
                src = ct[0:r, n, a:a + P * heads].rearrange("p (h k) -> p h k", h=heads)
                return v.tensor_tensor(out[0:r].rearrange("p (h k) -> p h k", h=heads), src, over(scale[0:r, n, k:k + heads], 2, [r, heads, P]), ALU.mult)

            for n in range(NT):
                r = ROWS[n]
                v.tensor_copy(gb[0:r], over(g[0:r, n], 2, [r, 4, P])).then_inc(spread, 1)
                step(rows(n, 0, 0, ss, ct[:, n, 0:1024], 8))
                v.wait_ge(cums, n + 1)
                v.tensor_copy(gc[0:r, n], bank(c, 0, 8, r))
                if n < 4:
                    ins = v.tensor_copy(egl[:, n], bank(c, 1).rearrange("p (h t) -> p h t", h=4)[:, :, P - 1])
                else:
                    ins = v.tensor_copy(egs[:], bank(c, 1, 4 * SAMP).rearrange("p (h b l) -> p h b l", h=4, l=NL)[:, :, :, NL - 1])
                step(ins)
                v.tensor_copy(eg[0:r, n, 0:4], gc[0:r, n, 0:4])
                v.tensor_tensor(eg[0:r, n, 4:8], gc[0:r, n, 4:8], gc[0:r, n, 0:4], ALU.subtract).then_inc(gc_out, 1)
                if n:
                    v.wait_ge(at_set, n)
                dd = x1[0:r, 512:512 + 4 * r].rearrange("p (h t) -> p h t", h=4)
                for h in range(DNH):
                    ins = v.tensor_scalar(dd[:, h], bank(c, 1, 4 * r, r)[:, r * h:r * h + r], gc[0:r, n, h:h + 1], 0.0, ALU.subtract, ALU.min)
                ins.then_inc(dd_set, 1)
                if n:
                    v.wait_ge(turned3, n)
                v.wait_ge(exps, n + 1)
                rows(n, 512, 0, beta, x1[:, 0:512])
                rows(n, 0, 0, eg, qe)
                rows(n, 1024, 0, beta, ct[:, n, 1024:1536]).then_inc(prepared, 1)
                v.wait_ge(dd_exp, n + 1)
                step(v.tensor_tensor(dd, dd, over(mask(K_UT, K_UTS, n), 1, [r, 4, r]), ALU.mult))
                v.wait_ge(turned3, n + 1)
                v.tensor_copy(qkt[:, n % 2, 0, 0:4 * r], bank(c, 2, 4 * r))
                v.tensor_copy(unit(A_QET, n), bank(c, 5, 4 * r).rearrange("p (h t) -> p h t", h=4)).then_inc(turned3_dve, 1)
                kb = x1[0:r, 0:512].rearrange("p (h k) -> p h k", h=4)
                v.tensor_tensor(ct[0:r, n, 0:512].rearrange("p (h k) -> p h k", h=4), kb, over(eg[0:r, n, 0:4], 2, [r, 4, P]), ALU.mult)
                rows(n, 512, 4, eg, ct[:, n, 512:1024])
                for a in (A_T, A_TT):
                    v.tensor_copy(unit(a, n, r), over(ident[0:r, 0:r], 1, [r, 4, r]))
                v.wait_ge(kk, n + 1)
                v.tensor_tensor(unit(A_AT, n, r), bank(c, 6, 4 * r, r).rearrange("p (h t) -> p h t", h=4), dd, ALU.mult)
                v.tensor_tensor(unit(A_QK, n, r), bank(c, 7, 4 * r, r).rearrange("p (h t) -> p h t", h=4), dd, ALU.mult).then_inc(at_set, 1)

            v.wait_ge(at_set, NT)

            def mask_a(i):
                lev, n = items[i]
                r = ROWS[n]
                if i >= 2:
                    v.wait_ge(m1, i - 1)
                v.tensor_tensor(am[0:r, i % 2, 0:4 * r].rearrange("p (h t) -> p h t", h=4), unit(A_AT, n, r),
                                over(cst(c, K_LEV + lev * P, r, r), 1, [r, 4, r]), ALU.mult).then_inc(am_set, 1)

            def update(i):
                n = items[i][1]
                r = ROWS[n]
                v.wait_ge(pp, i + 1)
                for a, b_ in ((A_T, 2), (A_TT, 4)):
                    ins = v.tensor_tensor(unit(a, n, r), unit(a, n, r), bank(c, b_ + i % 2, 4 * r, r).rearrange("p (h t) -> p h t", h=4), ALU.subtract)
                ins.then_inc(t_new, 1)

            mask_a(0)
            for i in range(len(items)):
                if i + 1 < len(items):
                    mask_a(i + 1)
                update(i)
            v.memset(s_p[:], 0.0).then_inc(s_zero, 1)
            for n in range(NT):
                r = ROWS[n]
                v.wait_ge(uw, n + 1)
                v.tensor_copy(ct[0:r, n, 1024:1536], bank(c, n % 2, 512, r)).then_inc(u_out, 1)
            v.wait_ge(u_out, NT)
            for n in range(4):
                v.wait_ge(ws, n + 1)
                if n:
                    v.wait_ge(od, n)
                v.tensor_tensor(vn[:].rearrange("p h k -> p (h k)"), ct[:, n, 1024:1536], bank(c, 4), ALU.subtract).then_inc(vnew, 1)
                v.wait_ge(od, n + 1)
                v.wait_ge(exps, NT)
                for h in range(DNH):
                    ins = v.scalar_tensor_tensor(s_p[:, h], s_p[:, h], egl[:, n, h:h + 1], bank(c, 5)[:, P * h:P * h + P], ALU.mult, ALU.add)
                ins.then_inc(s_new, 1)
            v.wait_ge(states_in, 16)
            v.wait_ge(w_out, NT)
            bm = cst(c, K_BM, NB * SAMP).rearrange("p (b t) -> p b t", b=NB)
            for h in range(DNH):
                if h:
                    v.wait_ge(od, 4 + h)
                v.tensor_tensor(wm[:, 0], over(unit(A_M1, 4)[:, h], 1, [P, NB, SAMP]), bm, ALU.mult)
                v.tensor_tensor(wm[:, 1], over(unit(A_QET, 4)[:, h], 1, [P, NB, SAMP]), bm, ALU.mult).then_inc(wm_set, 1)
                if h:
                    v.wait_ge(sd, 4 + h)
                v.tensor_tensor(x1[0:SAMP].rearrange("p (b k) -> p b k", b=NB), over(ct[0:SAMP, 4, 512 + P * h:640 + P * h], 1, [SAMP, NB, DK]),
                                over(cst(c, K_BR, NB, SAMP), 2, [SAMP, NB, DK]), ALU.mult).then_inc(km_set, 1)
                v.wait_ge(ws, 5 + h)
                v.tensor_tensor(vn[0:SAMP, h], ct[0:SAMP, 4, 1024 + P * h:1152 + P * h], bank(c, 4, 512, SAMP)[:, P * h:P * h + P], ALU.subtract).then_inc(vnew, 1)
                v.wait_ge(od, 5 + h)
                step(v.tensor_tensor(s_s[:, :, h], s_s[:, :, h], over(egs[:, h], 2, [P, NB, DK]), ALU.mult))
                v.wait_ge(sd, 5 + h)
                for i in range(2):
                    ins = v.tensor_tensor(s_s[:, 4 * i:4 * i + 4, h], s_s[:, 4 * i:4 * i + 4, h], bank(c, 2 + i).rearrange("p (b k) -> p b k", b=4), ALU.add)
                ins.then_inc(s_new, 1)
            v.wait_ge(o_out, 5)
            step(v.memset(ms[:], 1.0))
            for n in range(NT):
                r = ROWS[n]
                if n == 0:
                    v.wait_ge(sd, 8)
                step(v.tensor_tensor(x1[0:r, 0:512], mix[0:r, n, 512:1024], mix[0:r, n, 512:1024], ALU.mult))
                step(v.tensor_reduce(ms[0:r, n], x1[0:r, 0:512].rearrange("p (h k) -> p h k", h=4), AX, ALU.add))
            v.tensor_scalar(ms[:], ms[:], 1.0 / DK, RMS_EPS, ALU.mult, ALU.add).then_inc(root, 1)
            v.wait_ge(sroot, 1)
            step(v.reciprocal(ms[:], ms[:]))
            v.wait_ge(z_done, 1)
            for n in range(NT):
                r = ROWS[n]
                o = mix[0:r, n, 512:1024].rearrange("p (h k) -> p h k", h=4)
                step(v.tensor_tensor(o, o, over(ms[0:r, n], 2, [r, 4, P]), ALU.mult))
                step(v.tensor_tensor(o, o, over(ng[0:r], 1, [r, 4, P]), ALU.mult))
                step(v.tensor_tensor(o, o, hd[0:r, n, 8:520].rearrange("p (h k) -> p h k", h=4), ALU.mult))


class LayerNorm:
    def __init__(self, c, name, gain_bias, at):
        self.c, self.xa, self.gb = c, words(c, A_X, NT, D), gain_bias
        self.stats, self.mean_var = words(c, at, NT, 12), words(c, at + NT * 12, NT, 2)
        self.gb_in, self.var_set, self.std_set, self.normed = (c.sem(name + x) for x in ("_gain_in", "_var_set", "_std_set", "_tile_done"))

    SIZE = NT * 14

    def load(self, sp, g, b):
        sp.dma_start(self.gb[:, 0:D], g[0].partition_broadcast(P)).then_inc(self.gb_in, 16)
        sp.dma_start(self.gb[:, D:2 * D], b[0].partition_broadcast(P)).then_inc(self.gb_in, 16)

    def statistics(self, v, step, n):
        r = ROWS[n]
        st, mv = self.stats[0:r, n].rearrange("p (h s) -> p h s", h=2), self.mean_var[0:r, n]
        for h in range(2):
            ins = v.bn_stats(st[:, h], self.xa[0:r, n, 512 * h:512 * h + 512])
        step(ins)
        step(v.bn_aggr(mv, self.stats[0:r, n]))
        v.tensor_scalar(mv[:, 1:2], mv[:, 1:2], LN_EPS, None, ALU.add).then_inc(self.var_set, 1)

    def root(self, act, n):
        r = ROWS[n]
        act.wait_ge(self.var_set, n + 1)
        mv = self.mean_var[0:r, n]
        act.activation(mv[:, 1:2], mv[:, 1:2], ACT.Sqrt).then_inc(self.std_set, 1)

    def finish(self, v, step, n):
        r = ROWS[n]
        x, mv = self.xa[0:r, n], self.mean_var[0:r, n]
        v.wait_ge(self.std_set, n + 1)
        step(v.reciprocal(mv[:, 1:2], mv[:, 1:2]))
        step(v.tensor_scalar(x, x, mv[:, 0:1], mv[:, 1:2], ALU.subtract, ALU.mult))
        if n == 0:
            v.wait_ge(self.gb_in, 32)
        step(v.tensor_tensor(x, x, self.gb[0:r, 0:D], ALU.mult))
        v.tensor_tensor(x, x, self.gb[0:r, D:2 * D], ALU.add).then_inc(self.normed, 1)


def turn_x(pe, c, n, h, o):
    xa, ident, r = words(c, A_X, NT, D), cst(c, K_ID, P), ROWS[n]
    for j in range(4):
        k = 4 * h + j
        ins = pe.transpose(bank(c, o)[:, r * j:r * j + r], xa[0:r, n, P * k:P * k + P], ident[0:r, 0:r])
    return ins


def keep_turned_x(act, c, n, h, o):
    r = ROWS[n]
    return act.copy(words(c, A_XT, KD, TOK)[:, 4 * h:4 * h + 4, tile_cols(n)], bank(c, o, 4 * r).rearrange("p (k t) -> p k t", k=4))


L_G = A_FREE
R0 = L_G + 2 * D
R1, R2 = R0 + KD * D, R0 + 2 * KD * D
L_MEMT = R0 + 3 * KD * D
L_MEM = L_MEMT + KD * MEM
L_MKT = L_MEM + 2 * D
L_MV = L_MKT + KD * MEM
L_Q = L_MV + 2 * D
L_S = L_Q + KD * TOK
assert L_S + 1800 <= ARENA and R2 + KD * D > A_MIX


def mix_plan():
    plan = [("mix", n, h, "act") for n in range(NT) for h in range(2) if n < 4 or h]
    plan += [("mem", m, h, "act") for m in range(2) for h in range(2)]
    plan += [("out", n, h, "dve") for n in range(NT) for h in range(2)]
    plan += [("mk", m, h, "act") for m in range(2) for h in range(2)]
    plan += [("mkt", m, h, "act") for m in range(2) for h in range(2)]
    plan += [("mv", m, h, "act") for m in range(2) for h in range(2)]
    return plan + [("x1", n, h, "act") for n in range(NT) for h in range(2)]


def emptied(plan, g, engine):
    return sum(1 for item in plan[:g + 1] if item[-1] == engine)


def phase_mix(c):
    nc, d = c.nc, c.dram
    xa, xt, mix = words(c, A_X, NT, D), words(c, A_XT, KD, TOK), words(c, A_MIX, NT, D)
    w_o, w_ck, w_cv = (words(c, a, KD, D) for a in (R0, R1, R2))
    memt, mem = words(c, L_MEMT, KD, MEM), words(c, L_MEM, 2, D)
    mkt, mv, mk = words(c, L_MKT, KD, MEM), words(c, L_MV, 2, D), words(c, L_Q, 2, D)
    ident = cst(c, K_ID, P)
    plan = mix_plan()
    last = {item[0]: g for g, item in enumerate(plan)}
    ln = LayerNorm(c, "ln1", words(c, L_G, 2 * D), L_S)
    mem_in, wo_in, wck_in, wcv_in = (c.sem(x) for x in ("mem_in", "w_o_in", "w_ck_in", "w_cv_in"))
    done, by_act, by_dve = c.sem("mix_group_done"), c.sem("mix_emptied_act"), c.sem("mix_emptied_dve")
    stored = c.sem("mem_kv_stored")
    c.wcq_in, c.wco_in = c.shared_sem("w_cq_in"), c.shared_sem("w_co_in")
    rows = "(k p) c -> p k c"

    with nc.Block(no_gpsimd_drain=True) as block:
        @block.sync
        def _(sp):
            sp.dma_start(mem, d.mem_prompt[0].rearrange("(m p) c -> p m c", p=P)).then_inc(mem_in, 16)
            sp.dma_start(w_o, d.w_o[0].rearrange(rows, p=P)).then_inc(wo_in, 16)
            ln.load(sp, d.ln1_g, d.ln1_b)
            sp.dma_start(w_ck, d.w_ck[0].rearrange(rows, p=P)).then_inc(wck_in, 16)
            sp.wait_ge(by_act, emptied(plan, last["mix"], "act"))
            sp.dma_start(w_cv, d.w_cv[0].rearrange(rows, p=P)).then_inc(wcv_in, 16)
            sp.wait_ge(done, last["mk"] + 1)
            sp.dma_start(w_ck, d.w_cq[0].rearrange(rows, p=P)).then_inc(c.wcq_in, 16)
            sp.wait_ge(done, last["mv"] + 1)
            sp.dma_start(w_cv, d.w_co[0].rearrange(rows, p=P)).then_inc(c.wco_in, 16)
            sp.wait_ge(by_act, emptied(plan, last["mv"], "act"))
            sp.dma_start(d.mem_k_prompt[0, 0].rearrange("(m p) h c -> p m (h c)", p=P), mk).then_inc(stored, 16)
            sp.dma_start(d.mem_v_prompt[0, 0].rearrange("(m p) h c -> p m (h c)", p=P), mv).then_inc(stored, 16)
            sp.wait_ge(stored, 32)

        @block.tensor
        def _(pe):
            for g, (kind, n, h, _) in enumerate(plan):
                if g >= 8:
                    who = plan[g - 8][-1]
                    pe.wait_ge(by_act if who == "act" else by_dve, emptied(plan, g - 8, who))
                o = bank(c, g % 8)
                if kind == "mix":
                    r = ROWS[n]
                    for j in range(4):
                        k = 4 * h + j
                        ins = pe.transpose(o[:, r * j:r * j + r], mix[0:r, n, P * k:P * k + P], ident[0:r, 0:r])
                elif kind == "mem":
                    pe.wait_ge(mem_in, 16)
                    for j in range(4):
                        k = 4 * h + j
                        ins = pe.transpose(o[:, P * j:P * j + P], mem[:, n, P * k:P * k + P], ident)
                elif kind == "out":
                    if (n, h) == (0, 0):
                        pe.wait_ge(wo_in, 16)
                        pe.wait_ge(by_act, emptied(plan, last["mix"], "act"))
                    for k in range(KD):
                        ins = pe.matmul(o[0:ROWS[n]], xt[:, k, tile_cols(n)], w_o[:, k, 512 * h:512 * h + 512], start=(k == 0), stop=(k == KD - 1))
                elif kind in ("mk", "mv"):
                    if (n, h) == (0, 0):
                        pe.wait_ge(wck_in if kind == "mk" else wcv_in, 16)
                        pe.wait_ge(by_act, emptied(plan, last["mem"], "act"))
                    w = w_ck if kind == "mk" else w_cv
                    for k in range(KD):
                        ins = pe.matmul(o, memt[:, k, P * n:P * n + P], w[:, k, 512 * h:512 * h + 512], start=(k == 0), stop=(k == KD - 1))
                elif kind == "mkt":
                    pe.wait_ge(by_act, emptied(plan, last["mk"], "act"))
                    for j in range(4):
                        k = 4 * h + j
                        ins = pe.transpose(o[:, P * j:P * j + P], mk[:, n, P * k:P * k + P], ident)
                else:
                    if h == 0:
                        pe.wait_ge(ln.normed, n + 1)
                    ins = turn_x(pe, c, n, h, g % 8)
                ins.then_inc(done, 1)

        @block.scalar
        def _(act):
            for g, (kind, n, h, who) in enumerate(plan):
                if who != "act":
                    if h:
                        ln.root(act, n)
                    continue
                act.wait_ge(done, g + 1)
                src = bank(c, g % 8)
                if kind == "mix":
                    r = ROWS[n]
                    cols = tile_cols(n)
                    ins = act.copy(xt[:, 4 * h:4 * h + 4, cols], src[:, 0:4 * r].rearrange("p (k t) -> p k t", k=4))
                elif kind in ("mem", "mkt"):
                    dst = memt if kind == "mem" else mkt
                    ins = act.copy(dst[:, 4 * h:4 * h + 4, P * n:P * n + P], src.rearrange("p (k t) -> p k t", k=4))
                elif kind in ("mk", "mv"):
                    ins = act.copy((mk if kind == "mk" else mv)[:, n, 512 * h:512 * h + 512], src)
                else:
                    ins = keep_turned_x(act, c, n, h, g % 8)
                ins.then_inc(by_act, 1)

        @block.vector
        def _(v):
            step = c.dve_step.on(v)
            for n in range(NT + 1):
                if n < NT:
                    r = ROWS[n]
                    for h in range(2):
                        g = plan.index(("out", n, h, "dve"))
                        v.wait_ge(done, g + 1)
                        x = xa[0:r, n, 512 * h:512 * h + 512]
                        ins = v.scalar_tensor_tensor(x, x, ALPHA, bank(c, g % 8, 512, r), ALU.mult, ALU.add)
                        ins.then_inc(by_dve, 1)
                    v.wait_ge(by_dve, 2 * n + 2)
                    ln.statistics(v, step, n)
                if n:
                    ln.finish(v, step, n - 1)


X_PT = R0
X_P = X_PT + XH * 2 * TOK
X_K, X_V = R1, R1 + 2 * 2 * D
X_KT = L_MEMT
X_QM = L_G
assert X_P + 2 * D <= R1 and X_KT + 2 * KD * MEM <= L_MKT


def phase_cross(c):
    nc, d = c.nc, c.dram
    xa, xt, ot = words(c, A_X, NT, D), words(c, A_XT, KD, TOK), words(c, A_XT, KD, TOK)
    w_cq, w_co = words(c, R1, KD, D), words(c, R2, KD, D)
    mkt, mv, q = words(c, L_MKT, KD, MEM), words(c, L_MV, 2, D), words(c, L_Q, KD, TOK)
    pt, pr = words(c, X_PT, XH, 2, TOK), words(c, X_P, 2, XH, MEM)
    ks, vs, kt = words(c, X_K, 2, 2 * D), words(c, X_V, 2, 2 * D), words(c, X_KT, 2, KD * MEM)
    qm = words(c, X_QM, NB, KD, SAMP)
    ident = cst(c, K_ID, P)
    mx, sums = words(c, L_S + LayerNorm.SIZE, NT, 4), words(c, L_S + LayerNorm.SIZE + 20, NT, 4)
    ln = LayerNorm(c, "ln2", words(c, L_G, 2 * D), L_S)
    scale = (D // XH) ** -0.5
    s = c.sem
    q_done, q_out, qm_set = s("cross_q_done"), s("cross_q_out"), s("cross_q_masked")
    scored, max_set, expd, prob_set, ptd, pt_out = (s("cross_" + x) for x in ("scored", "max_set", "exp_done", "probs_set",
                                                                             "probs_turned", "probs_turned_out"))
    av, av_out = s("cross_av_done"), s("cross_av_out")
    k_in, v_in = [s(f"mem_k_in{i}") for i in range(2)], [s(f"mem_v_in{i}") for i in range(2)]
    k_turned, k_out_act, k_out_dve, k_used, v_used = (s("mem_k_" + x) for x in ("turned", "out_act", "out_dve", "scored", "v_used"))
    od, resid, x2d, x2_out = s("cross_out_done"), s("cross_residual_set"), s("x2_turned"), s("x2_turned_out")

    with nc.Block(no_gpsimd_drain=True) as block:
        @block.sync
        def _(sp):
            sp.wait_ge(q_done, 16)
            for b in range(NB):
                if b >= 2:
                    sp.wait_ge(k_used, b - 1)
                sp.dma_start(ks[:, b % 2].rearrange("p (m c) -> p m c", m=2), d.cache_mem_k[0, b].rearrange("(m p) h c -> p m (h c)", p=P)).then_inc(k_in[b % 2], 16)
                if b < 2:
                    sp.dma_start(vs[:, b].rearrange("p (m c) -> p m c", m=2), d.cache_mem_v[0, b].rearrange("(m p) h c -> p m (h c)", p=P)).then_inc(v_in[b], 16)
            sp.wait_ge(k_used, NB)
            ln.load(sp, d.ln2_g, d.ln2_b)
            for b in range(2, NB):
                sp.wait_ge(v_used, b - 1)
                sp.dma_start(vs[:, b % 2].rearrange("p (m c) -> p m c", m=2), d.cache_mem_v[0, b].rearrange("(m p) h c -> p m (h c)", p=P)).then_inc(v_in[b % 2], 16)

        @block.tensor
        def _(pe):
            pe.wait_ge(c.wcq_in, 16)
            for g in range(16):
                ch, h = g // 2, g % 2
                if g >= 8:
                    pe.wait_ge(q_out, g - 7)
                for k in range(KD):
                    ins = pe.matmul(bank(c, g % 8, HALF), w_cq[:, k, P * ch:P * ch + P], xt[:, k, HALF * h:HALF * h + HALF], start=(k == 0), stop=(k == KD - 1))
                ins.then_inc(q_done, 1)
            pe.wait_ge(q_out, 16)

            def scores(n):
                if n >= 2:
                    pe.wait_ge(expd, n - 1)
                for h in range(XH):
                    for e in range(2):
                        ins = pe.matmul(bank(c, 2 * (n % 2) + h // 2)[:, MEM * (h % 2):MEM * (h % 2) + MEM], q[:, 2 * h + e, tile_cols(n)],
                                        mkt[:, 2 * h + e], start=(e == 0), stop=(e == 1))
                ins.then_inc(scored, 1)

            def turn_probs(n):
                r = ROWS[n]
                pe.wait_ge(prob_set, n + 1)
                if n:
                    pe.wait_ge(pt_out, n)
                for m in range(2):
                    for h in range(XH):
                        ins = pe.transpose(bank(c, 4 + m)[:, r * h:r * h + r], pr[0:r, n % 2, h, P * m:P * m + P], ident[0:r, 0:r])
                ins.then_inc(ptd, 1)

            for n in range(5):
                if n < 4:
                    scores(n)
                if n:
                    turn_probs(n - 1)
            pe.wait_ge(pt_out, 4)
            for g in range(KD):
                if g >= 2:
                    pe.wait_ge(av_out, g - 1)
                for m in range(2):
                    ins = pe.matmul(bank(c, 6 + g % 2), mv[:, m, P * g:P * g + P], pt[:, g // 2, m, 0:SEQ], start=(m == 0), stop=(m == 1))
                ins.then_inc(av, 1)
            pe.wait_ge(expd, 4)
            pe.wait_ge(av_out, KD)
            pe.wait_ge(qm_set, 1)
            for b in range(NB):
                pe.wait_ge(k_in[b % 2], 16 * (b // 2 + 1))
                if b:
                    pe.wait_ge(k_out_act, b)
                    pe.wait_ge(k_out_dve, b)
                for m in range(2):
                    for ch in range(KD):
                        ins = pe.transpose(bank(c, 2 * m + ch // 4)[:, P * (ch % 4):P * (ch % 4) + P], ks[:, b % 2, D * m + P * ch:D * m + P * ch + P], ident)
                ins.then_inc(k_turned, 1)
                pe.wait_ge(k_out_act, b + 1)
                pe.wait_ge(k_out_dve, b + 1)
                for h in range(XH):
                    for e in range(2):
                        ch = 2 * h + e
                        ins = pe.matmul(bank(c, 6 + h // 2, 512, SAMP)[:, MEM * (h % 2):MEM * (h % 2) + MEM], qm[:, b, ch], kt[:, b % 2, MEM * ch:MEM * ch + MEM],
                                        start=(b == 0 and e == 0 and h % 2 == 0), stop=(b == NB - 1 and e == 1), skip_group_check=True)
                ins.then_inc(k_used, 1)
            turn_probs(4)
            pe.wait_ge(pt_out, 5)
            for b in range(NB):
                pe.wait_ge(v_in[b % 2], 16 * (b // 2 + 1))
                for ch in range(KD):
                    for m in range(2):
                        o = bank(c, 0)[:, SAMP * ch + NL * b:SAMP * ch + NL * b + NL]
                        ins = pe.matmul(o, vs[:, b % 2, D * m + P * ch:D * m + P * ch + P], pt[:, ch // 2, m, SEQ + NL * b:SEQ + NL * b + NL],
                                        start=(b == 0 and ch == 0 and m == 0), stop=(b == NB - 1 and ch == KD - 1 and m == 1), skip_group_check=True)
                ins.then_inc(v_used, 1)
            pe.wait_ge(av_out, KD + 1)
            pe.wait_ge(c.wco_in, 16)

            def project(n):
                if n >= 2:
                    pe.wait_ge(resid, 2 * (n - 1))
                for h in range(2):
                    for k in range(KD):
                        ins = pe.matmul(bank(c, 4 + 2 * (n % 2) + h, 512, ROWS[n]), ot[:, k, tile_cols(n)], w_co[:, k, 512 * h:512 * h + 512], start=(k == 0), stop=(k == KD - 1))
                    ins.then_inc(od, 1)

            def turn(n):
                pe.wait_ge(ln.normed, n + 1)
                for h in range(2):
                    if n >= 2:
                        pe.wait_ge(x2_out, 2 * n + h - 3)
                    turn_x(pe, c, n, h, (2 * n + h) % 4).then_inc(x2d, 1)

            for n in range(NT):
                project(n)
            for n in range(NT):
                turn(n)

        @block.scalar
        def _(act):
            for g in range(16):
                act.wait_ge(q_done, g + 1)
                act.copy(q[:, g // 2, HALF * (g % 2):HALF * (g % 2) + HALF], bank(c, g % 8, HALF)).then_inc(q_out, 1)

            def exps(n, b0):
                r = ROWS[n]
                act.wait_ge(max_set, n + 1)
                if n >= 2:
                    act.wait_ge(ptd, n - 1)
                for h in range(XH):
                    ins = act.activation(pr[0:r, n % 2, h], bank(c, b0 + h // 2, 512, r)[:, MEM * (h % 2):MEM * (h % 2) + MEM], ACT.Exp,
                                         bias=mx[0:r, n, h:h + 1], scale=scale, accum_out=sums[0:r, n, h:h + 1])
                ins.then_inc(expd, 1)

            def keep_probs(n):
                r = ROWS[n]
                act.wait_ge(ptd, n + 1)
                for m in range(2):
                    ins = act.copy(pt[:, :, m, tile_cols(n)], bank(c, 4 + m, 4 * r).rearrange("p (h t) -> p h t", h=XH))
                ins.then_inc(pt_out, 1)

            for n in range(5):
                if n < 4:
                    exps(n, 2 * (n % 2))
                if n:
                    keep_probs(n - 1)
            for g in range(KD):
                act.wait_ge(av, g + 1)
                act.copy(ot[:, g, 0:SEQ], bank(c, 6 + g % 2)).then_inc(av_out, 1)
            for b in range(NB):
                act.wait_ge(k_turned, b + 1)
                if b >= 2:
                    act.wait_ge(k_used, b - 1)
                dst = kt[:, b % 2].rearrange("p (c m t) -> p c m t", c=KD, m=2)
                for e in range(2):
                    ins = act.copy(dst[:, 4 * e:4 * e + 4, 0], bank(c, e).rearrange("p (c t) -> p c t", c=4))
                ins.then_inc(k_out_act, 1)
            exps(4, 6)
            keep_probs(4)
            act.wait_ge(v_used, NB)
            act.copy(ot[:, :, SEQ:TOK], bank(c, 0, KD * SAMP).rearrange("p (c t) -> p c t", c=KD)).then_inc(av_out, 1)
            for n in range(NT):
                ln.root(act, n)
            for n in range(NT):
                for h in range(2):
                    act.wait_ge(x2d, 2 * n + h + 1)
                    keep_turned_x(act, c, n, h, (2 * n + h) % 4).then_inc(x2_out, 1)

        @block.vector
        def _(v):
            step = c.dve_step.on(v)

            def maxima(n, b0):
                r = ROWS[n]
                if n < 4:
                    v.wait_ge(scored, n + 1)
                for i in range(2):
                    ins = v.tensor_reduce(mx[0:r, n, 2 * i:2 * i + 2], bank(c, b0 + i, 512, r).rearrange("p (h m) -> p h m", h=2), AX, ALU.max)
                step(ins)
                v.tensor_scalar(mx[0:r, n], mx[0:r, n], -scale, None, ALU.mult).then_inc(max_set, 1)

            def divide(n):
                r = ROWS[n]
                v.wait_ge(expd, n + 1)
                step(v.reciprocal(sums[0:r, n], sums[0:r, n]))
                x = pr[0:r, n % 2]
                v.tensor_tensor(x, x, over(sums[0:r, n], 2, [r, XH, MEM]), ALU.mult).then_inc(prob_set, 1)

            v.wait_ge(q_out, 16)
            bm = cst(c, K_BM, NB * SAMP).rearrange("p (b t) -> p b t", b=NB)
            v.tensor_tensor(qm[:], over(q[:, :, SEQ:TOK], 1, [P, NB, KD, SAMP]), over(bm, 2, [P, NB, KD, SAMP]), ALU.mult).then_inc(qm_set, 1)
            for n in range(5):
                if n < 4:
                    maxima(n, 2 * (n % 2))
                if n:
                    divide(n - 1)
            for b in range(NB):
                v.wait_ge(k_turned, b + 1)
                if b >= 2:
                    v.wait_ge(k_used, b - 1)
                dst = kt[:, b % 2].rearrange("p (c m t) -> p c m t", c=KD, m=2)
                for e in range(2):
                    ins = v.tensor_copy(dst[:, 4 * e:4 * e + 4, 1], bank(c, 2 + e).rearrange("p (c t) -> p c t", c=4))
                ins.then_inc(k_out_dve, 1)
            v.wait_ge(k_used, NB)
            maxima(4, 6)
            divide(4)
            for n in range(NT + 1):
                if n < NT:
                    r = ROWS[n]
                    for h in range(2):
                        v.wait_ge(od, 2 * n + h + 1)
                        x = xa[0:r, n, 512 * h:512 * h + 512]
                        v.scalar_tensor_tensor(x, x, ALPHA, bank(c, 4 + 2 * (n % 2) + h, 512, r), ALU.mult, ALU.add).then_inc(resid, 1)
                    v.wait_ge(resid, 2 * n + 2)
                    ln.statistics(v, step, n)
                if n:
                    ln.finish(v, step, n - 1)


F_W = A_FREE
F_Q = F_W + PH * KD * 2 * NK
F_KEY = F_Q + 2 * PH * TOK
F_S = F_KEY + 4 * NK
F_V = F_S + 2 * 16 * NK
F_C = F_V + 3 * 256
F_E = F_C + PH * 256
F_B = F_E + PH * 256
F_T = F_B + 11 * 128
assert F_T + 3 * TOK <= ARENA
LOWEST = -3e38


def phase_retrieve(c):
    nc, d = c.nc, c.dram
    xt = words(c, A_XT, KD, TOK)
    w, q = words(c, F_W, PH, KD, 2 * NK), words(c, F_Q, 2 * PH, TOK)
    key, keyt = words(c, F_KEY, 2, NK), words(c, F_KEY + 2 * NK, 2, NK)
    sc = words(c, F_S, 2, 16, NK)
    best, where, wheref = words(c, F_V, 16, 16), words(c, F_V + 256, 256).bitcast(U32), words(c, F_V + 512, 16, 16)
    where = where.rearrange("p (g k) -> p g k", g=16)
    cand, hot = words(c, F_C, PH, 256), words(c, F_E, PH, 256)
    row = [words(c, F_B + 128 * i, 128) for i in range(11)]
    top, pair, hi, lo = row[0], row[1].bitcast(U32), row[2].bitcast(U32), row[3].bitcast(U32)
    hif, lof = row[4], row[5]
    kept = words(c, F_B + 6 * 128, 3, 128)
    diff, tot = row[9], row[10]
    kt = words(c, F_T, 3, TOK)
    ident, iota = cst(c, K_ID, P), cst(c, K_IOTA, NK)
    s = c.sem
    w_in, key_in = [s(f"w_pq_in{h}") for h in range(PH)], s("peer_keys_in")
    keys_turned, keys_out = s("keys_turned"), s("keys_turned_out")
    q_done, q_out, scored, score_out = s("peer_q_done"), s("peer_q_out"), s("peer_scored"), s("peer_scores_out")
    picked, diff_set, exp_set, kept_set, turned, turned_out = (s("peer_" + x) for x in (
        "keys_picked", "gate_logits_set", "gate_exps", "pairs_kept", "pairs_turned", "pairs_turned_out"))

    with nc.Block(no_gpsimd_drain=True) as block:
        @block.sync
        def _(sp):
            sp.dma_start(key[:, 0], d.peer_keys1[0]).then_inc(key_in, 16)
            sp.dma_start(key[:, 1], d.peer_keys2[0]).then_inc(key_in, 16)
            for h in range(PH):
                sp.dma_start(w[:, h], d.w_pq[0, :, h].rearrange("(k p) c -> p k c", p=P)).then_inc(w_in[h], 16)

        @block.tensor
        def _(pe):
            pe.wait_ge(key_in, 32)
            for i in range(2):
                ins = pe.transpose(bank(c, 7)[:, NK * i:NK * i + NK], key[:, i], ident)
            ins.then_inc(keys_turned, 1)
            for g in range(4 * PH):
                ch, h = g // 2, g % 2
                if g % 4 == 0:
                    pe.wait_ge(w_in[g // 4], 16)
                if g >= 4:
                    pe.wait_ge(q_out, g - 3)
                for k in range(KD):
                    ins = pe.matmul(bank(c, g % 4, HALF), w[:, ch // 2, k, NK * (ch % 2):NK * (ch % 2) + NK], xt[:, k, HALF * h:HALF * h + HALF],
                                    start=(k == 0), stop=(k == KD - 1))
                ins.then_inc(q_done, 1)
            pe.wait_ge(q_out, 4 * PH)
            pe.wait_ge(keys_out, 1)

            def score(n):
                r = ROWS[n]
                for i in range(4):
                    if n:
                        pe.wait_ge(score_out, 4 * n - 3 + i)
                    for j in range(4):
                        ins = pe.matmul(bank(c, i, 512, r)[:, NK * j:NK * j + NK], q[:, 4 * i + j, tile_cols(n)], keyt[:, j % 2], start=True, stop=True)
                    ins.then_inc(scored, 1)

            score(0)
            for n in range(NT):
                r = ROWS[n]
                if n + 1 < NT:
                    score(n + 1)
                pe.wait_ge(kept_set, n + 1)
                if n:
                    pe.wait_ge(turned_out, n)
                for i in range(3):
                    ins = pe.transpose(bank(c, 6)[:, r * i:r * i + r], kept[0:r, i], ident[0:r, 0:r])
                ins.then_inc(turned, 1)

        @block.scalar
        def _(act):
            act.wait_ge(keys_turned, 1)
            act.copy(keyt[:], bank(c, 7, 2 * NK).rearrange("p (i k) -> p i k", i=2)).then_inc(keys_out, 1)
            for g in range(4 * PH):
                act.wait_ge(q_done, g + 1)
                act.copy(q[:, g // 2, HALF * (g % 2):HALF * (g % 2) + HALF], bank(c, g % 4, HALF)).then_inc(q_out, 1)

            def keep_scores(n):
                for i in range(4):
                    act.wait_ge(scored, 4 * n + i + 1)
                    if n >= 2 and i == 0:
                        act.wait_ge(picked, n - 1)
                    act.copy(sc[0:ROWS[n], n % 2, 4 * i:4 * i + 4], bank(c, i, 512, ROWS[n]).rearrange("p (g k) -> p g k", g=4)).then_inc(score_out, 1)

            keep_scores(0)
            for n in range(NT):
                r = ROWS[n]
                if n + 1 < NT:
                    keep_scores(n + 1)
                act.wait_ge(diff_set, n + 1)
                act.activation(diff[0:r], diff[0:r], ACT.Exp).then_inc(exp_set, 1)
                act.wait_ge(turned, n + 1)
                act.copy(kt[:, :, tile_cols(n)], bank(c, 6, 3 * r).rearrange("p (i t) -> p i t", i=3)).then_inc(turned_out, 1)

        @block.vector
        def _(v):
            step = c.dve_step.on(v)

            def best16(values, vals, idx, groups):
                for half in range(2):
                    k = slice(8 * half, 8 * half + 8)
                    for g in range(groups):
                        ins = v.max(vals(g)[:, k], values(g))
                    step(ins)
                    for g in range(groups):
                        ins = v.max_index(idx(g)[:, k], vals(g)[:, k], values(g))
                    if half == 0:
                        step(ins)
                        for g in range(groups):
                            ins = v.match_replace(values(g), vals(g)[:, k], values(g), LOWEST)
                    step(ins)

            for n in range(NT):
                r = ROWS[n]
                v.wait_ge(score_out, 4 * n + 4)
                best16(lambda g: sc[0:r, n % 2, g], lambda g: best[0:r, g], lambda g: where[0:r, g], 16)
                v.tensor_copy(wheref[0:r], where[0:r]).then_inc(picked, 1)
                b2 = best[0:r].rearrange("p (h s) k -> p s h k", s=2)
                c3 = cand[0:r].rearrange("p h (i j) -> p h i j", i=16)
                step(v.tensor_tensor(c3, over(b2[:, 0], 3, [r, PH, 16, 16]), over(b2[:, 1], 2, [r, PH, 16, 16]), ALU.add))
                t3, p3 = (x[0:r].rearrange("p (h k) -> p h k", h=PH) for x in (top, pair))
                best16(lambda g: cand[0:r, g], lambda g: t3[:, g], lambda g: p3[:, g], PH)
                v.tensor_scalar(hi[0:r], pair[0:r], 4, None, ALU.logical_shift_right)
                v.tensor_scalar(lo[0:r], pair[0:r], 15, None, ALU.bitwise_and)
                d3, s8 = diff[0:r].rearrange("p (h k) -> p h k", h=PH), tot[0:r, 0:PH]
                if n:
                    v.wait_ge(kept_set, n)
                v.tensor_tensor(d3, t3, over(t3[:, :, 0], 2, [r, PH, 16]), ALU.subtract).then_inc(diff_set, 1)
                v.wait_ge(diff_set, n + 1)
                v.tensor_copy(hif[0:r], hi[0:r])
                step(v.tensor_copy(lof[0:r], lo[0:r]))
                if n:
                    v.wait_ge(turned, n)
                for i, x in enumerate((hif, lof)):
                    h3 = hot[0:r].rearrange("p h (k j) -> p (h k) j", j=16)
                    h4 = hot[0:r].rearrange("p h (k j) -> p h k j", j=16)
                    keys = wheref[0:r].rearrange("p (h s) k -> p s h k", s=2)[:, i]
                    step(v.tensor_tensor(h3, over(x[0:r], 2, [r, 128, 16]), over(iota[0:r, 0:16], 1, [r, 128, 16]), ALU.is_equal))
                    step(v.tensor_tensor(h4, h4, over(keys, 2, [r, PH, 16, 16]), ALU.mult))
                    step(v.tensor_reduce(kept[0:r, i], h3, AX, ALU.add))
                v.wait_ge(exp_set, n + 1)
                step(v.tensor_reduce(s8, d3, AX, ALU.add))
                step(v.reciprocal(s8, s8))
                v.tensor_tensor(kept[0:r, 2].rearrange("p (h k) -> p h k", h=PH), d3, over(s8, 2, [r, PH, 16]), ALU.mult).then_inc(kept_set, 1)


TG = 32
NTG = TOK // TG
F_HOT = A_FREE
F_GST = F_HOT + 4 * 2 * 4 * P
assert F_GST + 2 * NK * TG <= F_Q


def after(eng, sem, n):
    if not isinstance(n, int) or n > 0:
        eng.wait_ge(sem, n)


def peeled(eng, first, last, body):
    for i in range(first):
        body(i, i % 2)
    with eng.Fori(first, last - 1, 2) as i:
        body(i, first % 2)
        body(i + 1, (first + 1) % 2)


def phase_gates(c):
    nc, d = c.nc, c.dram
    kt = words(c, F_T, 3, TOK)
    hot = words(c, F_HOT, 4, 2, 4 * P)
    gst = words(c, F_GST, 2, NK, TG)
    iota = cst(c, K_IOTA, NK)
    s = c.sem
    hot_set, made, kept, stored = s("one_hots_set"), s("gates_made"), s("gates_kept"), [s(f"gates_stored{i}") for i in range(2)]
    c.gates_dram = nc.dram_tensor("gates", (P, NTG, NK, TG), F32)[:, :, :, :]
    QG = TG // 4

    with nc.Block(no_gpsimd_drain=True) as block:
        @block.vector
        def _(v):
            def body(tg, slot):
                for j in range(QG):
                    g = tg * QG + j
                    after(v, made, g - 3)
                    for t in range(4):
                        col = tg * TG + (4 * j + t)
                        v.tensor_scalar(hot[:, j % 4, 1, P * t:P * t + P], iota, kt[:, 1, bass.ds(col, 1)], None, ALU.is_equal)
                        ins = v.tensor_scalar(hot[:, j % 4, 0, P * t:P * t + P], iota, kt[:, 0, bass.ds(col, 1)], kt[:, 2, bass.ds(col, 1)],
                                              ALU.is_equal, ALU.mult)
                    ins.then_inc(hot_set, 1)
            peeled(v, 1, NTG, body)

        @block.tensor
        def _(pe):
            def body(tg, slot):
                for j in range(QG):
                    g = tg * QG + j
                    pe.wait_ge(hot_set, g + 1)
                    after(pe, kept, g - 7)
                    for t in range(4):
                        ins = pe.matmul(bank(c, j)[:, P * t:P * t + P], hot[:, j % 4, 1, P * t:P * t + P], hot[:, j % 4, 0, P * t:P * t + P], start=True, stop=True)
                    ins.then_inc(made, 1)
            peeled(pe, 1, NTG, body)

        @block.scalar
        def _(act):
            def body(tg, slot):
                after(act, stored[slot], (tg // 2) * 16 if isinstance(tg, int) else (tg - slot) * 8)
                for j in range(QG):
                    act.wait_ge(made, tg * QG + j + 1)
                    act.copy(gst[:, slot, :, 4 * j:4 * j + 4].rearrange("p k t -> p t k"), bank(c, j).rearrange("p (t k) -> p t k", t=4)).then_inc(kept, 1)
            peeled(act, 1, NTG, body)

        @block.sync
        def _(sp):
            def body(tg, slot):
                sp.wait_ge(kept, tg * QG + QG)
                sp.dma_start(c.gates_dram[:, bass.ds(tg, 1)].rearrange("p g k t -> p (g k) t"), gst[:, slot]).then_inc(stored[slot], 16)
            peeled(sp, 1, NTG, body)
            sp.wait_ge(stored[0], 16 * ((NTG + 1) // 2))
            sp.wait_ge(stored[1], 16 * (NTG // 2))


GB = 4
NG = NK // GB
E_ACC = A_FREE
E_U = E_ACC + KD * TOK
E_V = E_U + 2 * GB * D
E_G = E_V + 2 * GB * D
E_UT = E_G + 2 * GB * TOK
E_H = E_UT + 2 * D
E_W = E_H + 2 * TOK
assert E_W + 2 * GB * TOK <= ARENA


def phase_experts(c):
    nc, d = c.nc, c.dram
    xt, acc = words(c, A_XT, KD, TOK), words(c, E_ACC, KD, TOK)
    u, vv = words(c, E_U, 2, GB, D), words(c, E_V, 2, GB, D)
    gt, ut = words(c, E_G, 2, NTG, GB, TG), words(c, E_UT, 2, KD, P)
    hid, gated = words(c, E_H, 2, TOK), words(c, E_W, 2, GB, TOK)
    ident = cst(c, K_ID, P)
    s = c.sem
    u_in, v_in, g_in = ([s(f"{x}_in{i}") for i in range(2)] for x in ("expert_u", "expert_v", "expert_gates"))
    turned, ut_act, ut_dve, hid_done, gelu_done, gated_set, out_done, added, cleared = (s("expert_" + x) for x in (
        "u_turned", "u_kept_act", "u_kept_dve", "hidden_done", "gelu_done", "gated", "out_done", "added", "cleared"))
    u_rows = d.peer_u[0].rearrange("(b a) d -> a b d", a=P)
    v_rows = d.peer_v[0].rearrange("(b a) d -> a b d", a=P)
    OPS = 2 * KD
    PER = OPS // GB

    def loads(n, slot):
        return 16 * (n // 2 + 1) if isinstance(n, int) else (n - slot) * 8 + 16

    with nc.Block(no_gpsimd_drain=True) as block:
        @block.sync
        def _(sp):
            def body(g, slot):
                after(sp, turned, (g - 1) * (2 * GB))
                sp.dma_start(u[:, slot], u_rows[:, bass.ds(g * GB, GB)]).then_inc(u_in[slot], 16)
                after(sp, gated_set, (g - 1) * GB)
                sp.dma_start(gt[:, slot].rearrange("p g b t -> p g (b t)"),
                             c.gates_dram[:, :, bass.ds(g * GB, GB)].rearrange("p g b t -> p g (b t)")).then_inc(g_in[slot], 16)
                after(sp, out_done, (g - 1) * OPS)
                sp.dma_start(vv[:, slot], v_rows[:, bass.ds(g * GB, GB)]).then_inc(v_in[slot], 16)
            peeled(sp, 2, NG, body)

        @block.tensor
        def _(pe):
            def outputs(g, slot, part):
                if part == 0:
                    pe.wait_ge(v_in[slot], loads(g, slot))
                    pe.wait_ge(gated_set, g * GB + GB)
                for i in range(PER * part, PER * part + PER):
                    ch, h = i // 2, i % 2
                    after(pe, added, g * OPS + (i - 3))
                    for b in range(GB):
                        ins = pe.matmul(bank(c, 4 + i % 4, HALF), vv[:, slot, b, P * ch:P * ch + P], gated[:, slot, b, HALF * h:HALF * h + HALF],
                                        start=(b == 0), stop=(b == GB - 1))
                    ins.then_inc(out_done, 1)

            def body(g, slot):
                pe.wait_ge(u_in[slot], loads(g, slot))
                for b in range(GB):
                    n = g * GB + b
                    for h in range(2):
                        after(pe, (ut_act, ut_dve)[h], n)
                        for j in range(4):
                            k = 4 * h + j
                            ins = pe.transpose(bank(c, h)[:, P * j:P * j + P], u[:, slot, b, P * k:P * k + P], ident)
                        ins.then_inc(turned, 1)
                    if not isinstance(g, int) or g > 0:
                        outputs(g - 1, 1 - slot, b)
                    pe.wait_ge(ut_act, n + 1)
                    pe.wait_ge(ut_dve, n + 1)
                    for h in range(2):
                        after(pe, gelu_done, 2 * n - 1 + h)
                        for k in range(KD):
                            ins = pe.matmul(bank(c, 2 + h, HALF), ut[:, b % 2, k], xt[:, k, HALF * h:HALF * h + HALF], start=(k == 0), stop=(k == KD - 1))
                        ins.then_inc(hid_done, 1)
            peeled(pe, 2, NG, body)
            for part in range(GB):
                outputs(NG - 1, (NG - 1) % 2, part)

        @block.scalar
        def _(act):
            def body(g, slot):
                for b in range(GB):
                    n = g * GB + b
                    act.wait_ge(turned, 2 * n + 1)
                    after(act, hid_done, 2 * n - 2)
                    act.copy(ut[:, b % 2, 0:4], bank(c, 0).rearrange("p (k a) -> p k a", k=4)).then_inc(ut_act, 1)
                    after(act, gated_set, n - 1)
                    for h in range(2):
                        act.wait_ge(hid_done, 2 * n + 1 + h)
                        act.activation(hid[:, b % 2, HALF * h:HALF * h + HALF], bank(c, 2 + h, HALF), ACT.Gelu_apprx_tanh).then_inc(gelu_done, 1)
            peeled(act, 2, NG, body)

        @block.vector
        def _(v):
            def add(g, part):
                for i in range(PER * part, PER * part + PER):
                    ch, h = i // 2, i % 2
                    v.wait_ge(out_done, g * OPS + (i + 1))
                    after(v, added, g * OPS + (i - 15))
                    a = acc[:, ch, HALF * h:HALF * h + HALF]
                    v.tensor_tensor(a, a, bank(c, 4 + i % 4, HALF), ALU.add).then_inc(added, 1)

            def body(g, slot):
                for b in range(GB):
                    n = g * GB + b
                    v.wait_ge(turned, 2 * n + 2)
                    after(v, hid_done, 2 * n - 2)
                    v.tensor_copy(ut[:, b % 2, 4:8], bank(c, 1).rearrange("p (k a) -> p k a", k=4)).then_inc(ut_dve, 1)
                    if not isinstance(g, int) or g > 0:
                        add(g - 1, b)
                    if b == 0:
                        v.wait_ge(g_in[slot], loads(g, slot))
                        after(v, out_done, (g - 1) * OPS)
                    v.wait_ge(gelu_done, 2 * n + 2)
                    v.tensor_tensor(gated[:, slot, b].rearrange("p (g t) -> p g t", t=TG), hid[:, b % 2].rearrange("p (g t) -> p g t", t=TG),
                                    gt[:, slot, :, b], ALU.mult).then_inc(gated_set, 1)
            v.memset(acc[:], 0.0).then_inc(cleared, 1)
            v.wait_ge(cleared, 1)
            peeled(v, 2, NG, body)
            for part in range(GB):
                add(NG - 1, part)


def phase_finish(c):
    nc, d = c.nc, c.dram
    xa, acc, ident = words(c, A_X, NT, D), words(c, E_ACC, KD, TOK), cst(c, K_ID, P)
    ln = LayerNorm(c, "ln3", words(c, E_U, 2 * D), E_V)
    turned, resid, stored = c.sem("ffn_turned"), c.sem("ffn_residual_set"), c.sem("y_stored")

    with nc.Block(no_gpsimd_drain=True) as block:
        @block.sync
        def _(sp):
            ln.load(sp, d.ln3_g, d.ln3_b)
            for n in range(NT):
                sp.wait_ge(ln.normed, n + 1)
                dst = d.y_prompt[0, P * n:P * n + P] if n < 4 else d.y_sample.rearrange("b l d -> (b l) d")
                sp.dma_start(dst, xa[0:ROWS[n], n]).then_inc(stored, 16)
            sp.wait_ge(stored, 16 * NT)

        @block.tensor
        def _(pe):
            for n in range(NT):
                r = ROWS[n]
                for h in range(2):
                    g = 2 * n + h
                    if g >= 8:
                        pe.wait_ge(resid, g - 7)
                    for j in range(4):
                        ins = pe.transpose(bank(c, g % 8, 512, r)[:, P * j:P * j + P], acc[:, 4 * h + j, tile_cols(n)], ident)
                    ins.then_inc(turned, 1)

        @block.scalar
        def _(act):
            for n in range(NT):
                ln.root(act, n)

        @block.vector
        def _(v):
            step = c.dve_step.on(v)
            for n in range(NT + 1):
                if n < NT:
                    r = ROWS[n]
                    for h in range(2):
                        g = 2 * n + h
                        v.wait_ge(turned, g + 1)
                        x = xa[0:r, n, 512 * h:512 * h + 512]
                        v.scalar_tensor_tensor(x, x, ALPHA, bank(c, g % 8, 512, r), ALU.mult, ALU.add).then_inc(resid, 1)
                    v.wait_ge(resid, 2 * n + 2)
                    ln.statistics(v, step, n)
                if n:
                    ln.finish(v, step, n - 1)

PHASES = [phase_project, phase_window, phase_delta, phase_mix, phase_cross, phase_retrieve, phase_gates,
          phase_experts, phase_finish]


_INS = ["x_prompt", "x_sample", "cache_swa_k", "cache_swa_v", "state_dn", "state_dn_conv", "cache_mem_k", "cache_mem_v",
        "mem_prompt", "w_in", "w_conv", "dn_a_log", "dn_dt_bias", "dn_norm_g", "attn_sinks", "w_o", "ln1_g", "ln1_b",
        "w_cq", "w_ck", "w_cv", "w_co", "ln2_g", "ln2_b", "w_pq", "peer_keys1", "peer_keys2", "peer_u", "peer_v",
        "ln3_g", "ln3_b"]
_OUTS = [("y_prompt", (1, SEQ, D)), ("y_sample", (NB, NL, D)), ("swa_k_prompt", (1, 1, P, 2, HD)),
         ("swa_v_prompt", (1, 1, P, 2, HD)), ("dn_state_prompt", (1, 1, DNH, DK, DK)), ("dn_conv_prompt", (1, 1, 3, CONV)),
         ("mem_k_prompt", (1, 1, MEM, XH, D // XH)), ("mem_v_prompt", (1, 1, MEM, XH, D // XH)),
         ("swa_k_sample", (1, NB, P, 2, HD)), ("swa_v_sample", (1, NB, P, 2, HD)),
         ("dn_state_sample", (1, NB, DNH, DK, DK)), ("dn_conv_sample", (1, NB, 3, CONV))]


def hymba_step(nc, dram, phases=None, debug=None):
    with ExitStack() as ctx:
        c = Program(nc, dram)
        c.shared_sem = lambda name: ctx.enter_context(nc.semaphore(name))
        c.arena = ctx.enter_context(nc.sbuf_tensor("arena", [P, ARENA], F32))
        c.ps = ctx.enter_context(nc.psum_tensor("ps", [P, 8 * 512], F32))
        c.dve_step = Steps(c.shared_sem("dve_step"))
        c.act_step = Steps(c.shared_sem("act_step"))
        for phase in phases or PHASES:
            own = []
            c.sem = lambda name: own.append(nc.alloc_semaphore(name)) or own[-1]
            phase(c)
            nc.clear_and_free_semaphores(own)
            nc.all_engine_barrier()
        if debug:
            debug(c)


def kernel(**inputs):
    from collections import namedtuple
    import numpy as np
    import concourse.bacc as bacc
    from concourse.bass_utils import run_bass_kernel_spmd

    nc = bacc.Bacc("TRN2", target_bir_lowering=False, num_devices=1)
    arrays = {"consts": constants()}
    for name in _INS:
        arrays[name] = np.ascontiguousarray(inputs[name])
    aps = {}
    for name, a in arrays.items():
        aps[name] = nc.dram_tensor(name, a.shape, mybir.dt.from_np(a.dtype), kind="ExternalInput").ap()
    for name, shape in _OUTS:
        aps[name] = nc.dram_tensor(name, shape, F32, kind="ExternalOutput").ap()
    hymba_step(nc, namedtuple("Dram", aps)(*aps.values()))
    r = run_bass_kernel_spmd(nc, [arrays], core_ids=[0])
    return tuple(r.results[0][name] for name, _ in _OUTS)
```

```python
from contextlib import ExitStack

import concourse.bass as bass
from concourse import mybir

F32 = mybir.dt.float32
F32R = mybir.dt.float32r
U32 = mybir.dt.uint32
ALU = mybir.AluOpType
ACT = mybir.ActivationFunctionType
AX = mybir.AxisListType.X

P = 128
D = 1024
KD = D // P
SEQ = 512
NB, NL = 8, 4
SAMP = NB * NL
TOK = SEQ + SAMP
HALF = TOK // 2
NT = 5
ROWS = [P, P, P, P, SAMP]
ALPHA = 2.0 ** 0.25
HD = 64
DNH, DK = 4, 128
MEM = 256
XH = 4
NK = 128
PH, TOPK = 8, 16
LN_EPS, RMS_EPS = 1e-5, 1e-6
NEG = -1e30

C_Q, C_K, C_V, C_CONV, C_B, C_Z = 0, 512, 640, 768, 2304, 2312
CONV = 1536
CCH = CONV // P
PADW = 3 + SEQ + NB * 7

LEVELS = 7
_at = 0


def _cols(n):
    global _at
    _at += n
    return _at - n


K_ID = _cols(P)
K_SWA = _cols(2 * P)
K_SMP = _cols(P + SAMP)
K_UT = _cols(P)
K_ONE = _cols(P)
K_UTS = _cols(SAMP)
K_ONES = _cols(SAMP)
K_LEV = _cols(LEVELS * P)
K_BM = _cols(NB * SAMP)
K_BR = _cols(NB)
K_IOTA = _cols(NK)
K_COS = _cols(NT * 32)
K_SIN = _cols(NT * 32)
K_HEAD = _cols(P)
K_N = _at

ARENA = 53136
A_CST = 0
A_X = A_CST + K_N
A_XT = A_X + NT * D
A_FREE = A_XT + KD * TOK


def constants():
    import numpy as np
    c = np.zeros((P, K_N), np.float32)
    p, f = np.arange(P)[:, None], np.arange(P)[None, :]
    c[:, K_ID:K_ID + P] = p == f
    c[:, K_SWA:K_SWA + P] = np.where(f >= p, 0.0, NEG)
    c[:, K_SWA + P:K_SWA + 2 * P] = np.where(f <= p, 0.0, NEG)
    b, l = (np.arange(P) % SAMP) // NL, np.arange(P) % NL
    t = np.arange(SAMP)
    c[:, K_SMP:K_SMP + P] = np.where(f >= l[:, None], 0.0, NEG)
    c[:, K_SMP + P:K_SMP + P + SAMP] = np.where(
        (t[None] // NL == b[:, None]) & (t[None] % NL <= l[:, None]), 0.0, NEG)
    c[:, K_UT:K_UT + P] = p <= f
    c[:, K_ONE:K_ONE + P] = 1.0
    same = t[:, None] // NL == t[None] // NL
    c[:SAMP, K_UTS:K_UTS + SAMP] = same & (t[:, None] <= t[None])
    c[:SAMP, K_ONES:K_ONES + SAMP] = same
    for v in range(LEVELS):
        s = 1 << v
        c[:, K_LEV + v * P:K_LEV + (v + 1) * P] = (f // (2 * s) == p // (2 * s)) & (f % (2 * s) >= s) & (p % (2 * s) < s)
    c[:, K_BM:K_BM + NB * SAMP] = (t[None] // NL == np.arange(NB)[:, None]).reshape(1, -1)
    c[:SAMP, K_BR:K_BR + NB] = t[:, None] // NL == np.arange(NB)[None]
    c[:, K_IOTA:K_IOTA + NK] = f
    c[:, K_HEAD:K_HEAD + P] = p // TOPK == f // TOPK
    inv = (np.float32(10000.0) ** (-np.arange(32, dtype=np.float32) / np.float32(32))).astype(np.float32)
    for n in range(NT):
        pos = (np.arange(P) + n * P if n < 4 else 2048 + np.arange(P) % NL).astype(np.float32)
        ang = (pos[:, None] * inv[None]).astype(np.float32)
        c[:, K_COS + 32 * n:K_COS + 32 * n + 32] = np.cos(ang)
        c[:, K_SIN + 32 * n:K_SIN + 32 * n + 32] = np.sin(ang)
    return c


class Program:

    def __init__(self, nc, dram):
        self.nc, self.dram = nc, dram


class Steps:

    def __init__(self, sem):
        self.sem, self.n = sem, 0

    def on(self, eng):
        self.eng = eng
        return self

    def __call__(self, ins):
        self.n += 1
        ins.then_inc(self.sem, 1)
        self.eng.wait_ge(self.sem, self.n)


def words(c, at, *shape, rows=P):
    n = 1
    for s in shape:
        n *= s
    start = max(x for x in c.tensors if x <= at)
    v = c.tensors[start][0:rows, at - start:at - start + n]
    return shaped(v, *shape)


def shaped(v, *shape):
    if len(shape) == 1:
        return v
    names = "abcd"[:len(shape)]
    return v.rearrange(f"p ({' '.join(names)}) -> p {' '.join(names)}", **dict(zip(names, shape)))


def cst(c, at, n, rows=P):
    return c.tensors[0][0:rows, A_CST + at:A_CST + at + n]


def over(ap, axis, shape):
    return ap.unsqueeze(axis).broadcast_to(shape)


def bank(c, i, n=512, rows=P):
    return c.ps[0:rows, 512 * i:512 * i + n]


def tile_cols(n):
    return slice(P * n, P * n + ROWS[n])


A_HA = A_FREE
A_HD = A_HA + NT * 768
A_SIL = A_HD + NT * 520
A_NEWC = A_SIL + CCH * TOK
A_CS = A_NEWC + CCH * 27
A_CW = A_CS + CONV
A_RING = A_CW + CCH * 28
A_HC = A_RING + 4 * KD * 520
assert A_HC + CCH * PADW <= ARENA

PIECES = [(C_CONV, 512), (C_CONV + 512, 512), (C_CONV + 1024, 512), (C_B, 520), (C_Q, 512), (C_K, 256)]


def projection_plan():
    plan = [("x", None, n, h) for n in range(NT) for h in range(2)] + [("state", None)]
    for p in range(3):
        plan += [("conv", p, 4 * p + j, h) for j in range(4) for h in range(2)]
    plan += [("token", 3, n, 0, 8, "b") for n in range(NT)]
    plan += [("token", 3, n, 8, 512, "z") for n in range(NT)]
    plan += [("token", 4, n, 0, 512, "q") for n in range(NT)]
    plan += [("token", 5, n, 0, 256, "kv") for n in range(NT)]
    return plan


def phase_project(c):
    nc, d = c.nc, c.dram
    xa = words(c, A_X, NT, D)
    xt = words(c, A_XT, KD, TOK)
    ha = words(c, A_HA, NT, 768)
    hd = words(c, A_HD, NT, 520)
    sil = words(c, A_SIL, CCH, TOK)
    newc = words(c, A_NEWC, CCH, 27)
    cs = words(c, A_CS, CONV, rows=28)
    cw = words(c, A_CW, CCH, 28)
    ring = words(c, A_RING, 4, KD, 520)
    hc = words(c, A_HC, CCH, PADW)
    hcs = hc[:, :, 3 + SEQ:].rearrange("p c (b j) -> p c b j", j=7)
    ident = cst(c, K_ID, P)
    plan = projection_plan()
    first, last = {}, {}
    for g, item in enumerate(plan):
        first.setdefault(item[1], g)
        last[item[1]] = g
    conv_group = {item[2]: g for g, item in enumerate(plan) if item[0] == "conv" and item[3] == 1}
    state_group = next(g for g, item in enumerate(plan) if item[0] == "state")

    consts_in, x_in, state_in = c.sem("consts_in"), [c.sem(f"x_in{n}") for n in range(NT)], c.sem("conv_state_in")
    piece_in = [c.sem(f"w_in_piece{s}") for s in range(4)]
    group_done, evacuated = c.sem("proj_group_done"), c.sem("proj_evacuated")
    pads, conv_done, sil_done = c.sem("conv_pads_set"), c.sem("conv_chunk_done"), c.sem("conv_silu_done")

    with nc.Block(no_gpsimd_drain=True) as block:
        @block.sync
        def _(sp):
            sp.dma_start(cst(c, 0, K_N), d.consts).then_inc(consts_in, 16)
            for n in range(NT):
                src = d.x_prompt[0, P * n:P * n + P] if n < 4 else d.x_sample.rearrange("b l d -> (b l) d")
                sp.dma_start(xa[0:ROWS[n], n], src).then_inc(x_in[n], 16)
            sp.dma_start(cs[0:24], d.state_dn_conv[0].rearrange("b j c -> (b j) c")).then_inc(state_in, 16)
            sp.dma_start(cs[24:28], d.w_conv[0]).then_inc(state_in, 16)
            for p, (c0, w) in enumerate(PIECES):
                if p >= 4:
                    sp.wait_ge(group_done, last[p - 4] + 1)
                src = d.w_in[0].rearrange("(k p) c -> p k c", p=P)[:, :, c0:c0 + w]
                sp.dma_start(ring[:, p % 4, :, 0:w], src).then_inc(piece_in[p % 4], 16)

        @block.tensor
        def _(pe):
            pe.wait_ge(consts_in, 16)
            for g, item in enumerate(plan):
                if g >= 8:
                    pe.wait_ge(evacuated, g - 7)
                kind, p = item[0], item[1]
                if p is not None and first[p] == g:
                    pe.wait_ge(piece_in[p % 4], 16 * (p // 4 + 1))
                if p == 0 and first[p] == g:
                    pe.wait_ge(evacuated, 2 * NT)
                if kind == "x":
                    n, h = item[2:]
                    r = ROWS[n]
                    if h == 0:
                        pe.wait_ge(x_in[n], 16)
                    for j in range(4):
                        k = 4 * h + j
                        ins = pe.transpose(bank(c, g % 8)[:, r * j:r * j + r], xa[0:r, n, P * k:P * k + P], ident[0:r, 0:r])
                elif kind == "state":
                    pe.wait_ge(state_in, 32)
                    for j in range(CCH):
                        ins = pe.transpose(bank(c, g % 8)[:, 28 * j:28 * j + 28], cs[:, P * j:P * j + P], ident[0:28, 0:28])
                elif kind == "conv":
                    ch, h = item[2:]
                    j = ch % 4
                    for k in range(KD):
                        ins = pe.matmul(bank(c, g % 8, HALF), ring[:, p % 4, k, P * j:P * j + P],
                                        xt[:, k, HALF * h:HALF * h + HALF], start=(k == 0), stop=(k == KD - 1))
                else:
                    n, c0, w = item[2:5]
                    for k in range(KD):
                        ins = pe.matmul(bank(c, g % 8, w, ROWS[n]), xt[:, k, tile_cols(n)], ring[:, p % 4, k, c0:c0 + w],
                                        start=(k == 0), stop=(k == KD - 1))
                ins.then_inc(group_done, 1)

        @block.scalar
        def _(act):
            def silu(ch):
                act.wait_ge(conv_done, ch + 1)
                act.activation(sil[:, ch], sil[:, ch], ACT.Silu).then_inc(sil_done, 1)

            for g, item in enumerate(plan):
                act.wait_ge(group_done, g + 1)
                kind = item[0]
                src = bank(c, g % 8)
                if kind == "x":
                    n, h = item[2:]
                    r = ROWS[n]
                    ins = act.copy(xt[:, 4 * h:4 * h + 4, tile_cols(n)], src[:, 0:4 * r].rearrange("p (k t) -> p k t", k=4))
                elif kind == "state":
                    ins = act.copy(cw[:], src[:, 0:CCH * 28].rearrange("p (c j) -> p c j", j=28))
                elif kind == "conv":
                    ch, h = item[2:]
                    if h == 0:
                        ins = act.copy(hc[:, ch, 3:3 + HALF], src[:, 0:HALF])
                    else:
                        act.copy(hc[:, ch, 3 + HALF:3 + SEQ], src[:, 0:SEQ - HALF])
                        ins = act.copy(hcs[:, ch, :, 3:7], src[:, SEQ - HALF:HALF].rearrange("p (b l) -> p b l", l=NL))
                else:
                    n, c0, w, what = item[2:]
                    dst = {"b": hd[:, n, 0:8], "z": hd[:, n, 8:520], "q": ha[:, n, 0:512], "kv": ha[:, n, 512:768]}[what]
                    if what in "bz" and n == 4:
                        act.wait_ge(pads, 1)
                    ins = act.copy(dst[0:ROWS[n]], src[0:ROWS[n], 0:w])
                ins.then_inc(evacuated, 1)
                if kind == "conv" and item[3] == 1 and item[2] >= 1:
                    silu(item[2] - 1)
            silu(CCH - 1)

        @block.vector
        def _(v):
            step = c.dve_step.on(v)
            v.memset(hc[:, :, 0:3], 0.0)
            v.memset(hd[:, 4, :], 0.0).then_inc(pads, 1)
            v.wait_ge(evacuated, state_group + 1)
            v.wait_ge(pads, 1)
            for j in range(CCH):
                ins = v.tensor_copy(hcs[:, j, :, 0:3], cw[:, j, 0:24].rearrange("p (b j) -> p b j", j=3))
            step(ins)
            for ch in range(CCH):
                v.wait_ge(evacuated, conv_group[ch] + 1)
                yp = sil[:, ch, 0:SEQ]
                ys = sil[:, ch, SEQ:TOK].rearrange("p (b l) -> p b l", l=NL)
                for j in range(4):
                    w = cw[:, ch, 24 + j:25 + j]
                    if j == 0:
                        v.tensor_scalar(yp, hc[:, ch, 0:SEQ], w, None, ALU.mult)
                        ins = v.tensor_scalar(ys, hcs[:, ch, :, 0:NL], w, None, ALU.mult)
                    else:
                        v.scalar_tensor_tensor(yp, hc[:, ch, j:j + SEQ], w, yp, ALU.mult, ALU.add)
                        ins = v.scalar_tensor_tensor(ys, hcs[:, ch, :, j:j + NL], w, ys, ALU.mult, ALU.add)
                    if j < 3:
                        step(ins)
                ins.then_inc(conv_done, 1)
                v.tensor_copy(newc[:, ch, 0:3], hc[:, ch, SEQ:SEQ + 3])
                ins = v.tensor_copy(newc[:, ch, 3:27].rearrange("p (b j) -> p b j", j=3), hcs[:, ch, :, 4:7])
            step(ins)


A_CT = A_SIL + CCH * TOK + CCH * 27
A_MIX = A_CT + NT * CONV
A_SWA = A_MIX + NT * D
A_QR = A_SWA
A_QT = A_QR + NT * 640
A_SM = A_QT + 5 * TOK
A_PT = A_SM + 2 * 1024
A_KC = A_PT + 1024
A_VC = A_KC + NB * P
A_KCT = A_VC + NB * P
A_QM = A_KCT + NB * P
A_NCO = A_QM + NB * P
A_RT = A_SM
A_SW1 = A_NCO + CONV
assert A_SW1 + 300 <= ARENA


def phase_window(c):
    nc, d = c.nc, c.dram
    ha = words(c, A_HA, NT, 768)
    sil = words(c, A_SIL, CCH, TOK)
    newc = words(c, A_NEWC, CCH, 27)
    ct = words(c, A_CT, NT, CONV)
    mix = words(c, A_MIX, NT, D)
    mixt = words(c, A_XT, KD, TOK)
    qr = words(c, A_QR, NT, 640)
    qt = words(c, A_QT, 5, TOK)
    sm = words(c, A_SM, 2, 4, 2 * P)
    pt = words(c, A_PT, 8, P)
    kc, vc, kct, qm = (words(c, a, NB, P) for a in (A_KC, A_VC, A_KCT, A_QM))
    nco = words(c, A_NCO, CONV, rows=27)
    rt = words(c, A_RT, 4, 10, 32)
    sink = words(c, A_SW1, 8)
    sink_rows = words(c, A_SW1 + 8, 2)
    mx, nmx, dsk, ssum, den = (words(c, A_SW1 + 16 + 16 * i, 4, 4) for i in range(5))
    qs = words(c, A_SW1 + 96, 4 * SAMP)
    ident = cst(c, K_ID, P)

    sink_in, cache_in = c.sem("sinks_in"), c.sem("window_cache_in")
    turned, turned_out = c.sem("turned"), c.sem("turned_out")
    rotated = c.sem("tile_rotated")
    newc_out = c.sem("new_conv_rows_ready")
    scored, masked, expd, ptd, pt_out, av_done, av_out = (
        c.sem(x) for x in ("scores_done", "scores_masked", "exp_done", "probs_turned", "probs_turned_out", "window_av_done",
                           "window_av_out"))
    masked_s = c.sem("sample_scores_masked")
    stored = c.sem("window_stored")
    units = [(n, kv) for n in range(4) for kv in range(2)]

    turns = [("new", q) for q in range(3)] + [("conv", n, q) for n in range(NT) for q in range(3)]
    turns += [(w, n) for n in range(NT) for w in ("q", "k")] + [("cache", h) for h in range(2)]
    turn_no = {t: i for i, t in enumerate(turns)}

    with nc.Block(no_gpsimd_drain=True) as block:
        @block.sync
        def _(sp):
            sp.dma_start(sink, d.attn_sinks[0].partition_broadcast(P)).then_inc(sink_in, 16)
            for j in range(4):
                sp.dma_start(sink_rows[SAMP * j:SAMP * j + SAMP], d.attn_sinks[0, j:8:4].partition_broadcast(SAMP),
                             allow_slow_non_contiguous=True).then_inc(sink_in, 16)
            sp.dma_start(kc[:], d.cache_swa_k[0].rearrange("b w h d -> w b (h d)")).then_inc(cache_in, 16)
            sp.dma_start(vc[:], d.cache_swa_v[0].rearrange("b w h d -> w b (h d)")).then_inc(cache_in, 16)
            sp.wait_ge(turned_out, 3)
            sp.dma_start(d.dn_conv_prompt[0, 0], nco[0:3]).then_inc(stored, 16)
            sp.dma_start(d.dn_conv_sample[0].rearrange("b j c -> (b j) c"), nco[3:27]).then_inc(stored, 16)
            sp.wait_ge(rotated, NT)
            flat = "b w h d -> b w (h d)"
            sp.dma_start(d.swa_k_prompt[0, 0].rearrange("w h d -> w (h d)"), qr[:, 3, 512:640]).then_inc(stored, 16)
            sp.dma_start(d.swa_v_prompt[0, 0].rearrange("w h d -> w (h d)"), ha[:, 3, 640:768]).then_inc(stored, 16)
            for b in range(NB):
                sp.dma_start(d.swa_k_sample[0].rearrange(flat)[b, P - NL:P], qr[NL * b:NL * b + NL, 4, 512:640]).then_inc(stored, 16)
                sp.dma_start(d.swa_v_sample[0].rearrange(flat)[b, P - NL:P], ha[NL * b:NL * b + NL, 4, 640:768]).then_inc(stored, 16)
            sp.wait_ge(cache_in, 32)
            sp.dma_start(d.swa_k_sample[0, :, 0:P - NL].rearrange("b w h d -> w b (h d)"), kc[NL:P]).then_inc(stored, 16)
            sp.dma_start(d.swa_v_sample[0, :, 0:P - NL].rearrange("b w h d -> w b (h d)"), vc[NL:P]).then_inc(stored, 16)
            sp.wait_ge(stored, 16 * (4 + 2 * NB + 2))

        @block.tensor
        def _(pe):
            for i, t in enumerate(turns):
                if i >= 4:
                    pe.wait_ge(turned_out, i - 3)
                o = bank(c, i % 4)
                if t[0] == "new":
                    for j in range(4):
                        ins = pe.transpose(o[0:27, P * j:P * j + P], newc[:, 4 * t[1] + j], ident)
                elif t[0] == "conv":
                    _, n, q = t
                    for j in range(4):
                        ins = pe.transpose(o[0:ROWS[n], P * j:P * j + P], sil[:, 4 * q + j, tile_cols(n)], ident)
                elif t[0] in "qk":
                    n, r = t[1], ROWS[t[1]]
                    pe.wait_ge(rotated, n + 1)
                    for j in range(4 if t[0] == "q" else 1):
                        c0 = P * j + (512 if t[0] == "k" else 0)
                        ins = pe.transpose(o[:, r * j:r * j + r], qr[0:r, n, c0:c0 + P], ident[0:r, 0:r])
                else:
                    pe.wait_ge(cache_in, 32)
                    for j in range(4):
                        ins = pe.transpose(o[:, P * j:P * j + P], kc[:, 4 * t[1] + j], ident)
                ins.then_inc(turned, 1)

            def scores(u):
                n, kv = units[u]
                if u >= 2:
                    pe.wait_ge(masked, u - 1)
                hp = slice(HD * kv, HD * kv + HD)
                for j in range(4):
                    lo = 0 if n else P
                    o = bank(c, 2 * (u % 2) + j // 2)[:, 256 * (j % 2) + lo:256 * (j % 2) + 256]
                    keys = qt[hp, 4, P * n - P + lo:P * n + P]
                    ins = pe.matmul(o, qt[hp, j, tile_cols(n)], keys, start=True, stop=True)
                ins.then_inc(scored, 1)

            def turn_probs(u):
                n, kv = units[u]
                pe.wait_ge(expd, u + 1)
                if u >= 1:
                    pe.wait_ge(pt_out, u)
                halves = (0, 1) if n else (1,)
                for h in halves:
                    for j in range(4):
                        ins = pe.transpose(bank(c, 4 + h)[:, P * j:P * j + P], sm[:, u % 2, j, P * h:P * h + P], ident)
                ins.then_inc(ptd, 1)

            def values(u):
                n, kv = units[u]
                halves = (0, 1) if n else (1,)
                pe.wait_ge(pt_out, u + 1)
                if u >= 2:
                    pe.wait_ge(av_out, u - 1)
                for j in range(4):
                    for h in halves:
                        v = ha[:, n - 1 + h, 640 + HD * kv:704 + HD * kv]
                        ins = pe.matmul(bank(c, 6 + u % 2)[:, HD * j:HD * j + HD], pt[:, 4 * h + j], v,
                                        start=(h == halves[0]), stop=(h == 1))
                ins.then_inc(av_done, 1)

            pe.wait_ge(turned_out, len(turns))
            scores(0)
            scores(1)
            for u in range(len(units)):
                turn_probs(u)
                if u + 2 < len(units):
                    scores(u + 2)
                values(u)

            nu = len(units)
            pe.wait_ge(masked, nu + 1)
            for kv in range(2):
                hp = slice(HD * kv, HD * kv + HD)
                o = bank(c, kv)
                for b in range(NB):
                    pe.matmul(o[:, 0:P], qm[hp, b], kct[hp, b], start=(b == 0), stop=(b == NB - 1))
                ins = pe.matmul(o[:, P:P + SAMP], qs[hp], qt[hp, 4, SEQ:TOK], start=True, stop=True)
                ins.then_inc(scored, 1)
            pe.wait_ge(pt_out, nu)
            pe.wait_ge(av_out, nu)
            for kv in range(2):
                pe.wait_ge(masked, nu + 2 + kv)
                pe.transpose(bank(c, 4 + kv)[:, 0:P], sm[:, kv, 0, 0:P], ident)
                pe.transpose(bank(c, 4 + kv)[0:SAMP, P:2 * P], sm[:, kv, 0, P:P + SAMP], ident).then_inc(ptd, 1)
            for kv in range(2):
                pe.wait_ge(pt_out, nu + 1 + kv)
                pk = pt[:, 2 * kv].rearrange("p (j q b l) -> p q b j l", q=2, b=NB, l=NL)
                pn = pt[0:SAMP, 2 * kv + 1].rearrange("p (j q t) -> p q j t", q=2, t=SAMP)
                for q in range(2):
                    o = bank(c, 6 + kv)[HD * q:HD * q + HD, 0:2 * SAMP].rearrange("p (j b l) -> p b j l", b=NB, l=NL)
                    pe.matmul(bank(c, 6 + kv)[HD * q:HD * q + HD, 0:2 * SAMP], ha[0:SAMP, 4, 640 + HD * kv:704 + HD * kv],
                              pn[:, q], start=True, stop=False)
                    for b in range(NB):
                        ins = pe.matmul(o[:, b], vc[:, b, HD * kv:HD * kv + HD], pk[:, q, b], start=False, stop=(b == NB - 1))
                ins.then_inc(av_done, 1)

        @block.scalar
        def _(act):
            for i, t in enumerate(turns):
                act.wait_ge(turned, i + 1)
                o = bank(c, i % 4)
                if t[0] == "new":
                    ins = act.copy(nco[:, 512 * t[1]:512 * t[1] + 512], o[0:27])
                elif t[0] == "conv":
                    r = ROWS[t[1]]
                    ins = act.copy(ct[0:r, t[1], 512 * t[2]:512 * t[2] + 512], o[0:r])
                elif t[0] == "q":
                    r = ROWS[t[1]]
                    ins = act.copy(qt[:, 0:4, tile_cols(t[1])], o[:, 0:4 * r].rearrange("p (j t) -> p j t", j=4))
                elif t[0] == "k":
                    ins = act.copy(qt[:, 4, tile_cols(t[1])], o[:, 0:ROWS[t[1]]])
                else:
                    ins = act.copy(kct[:, 4 * t[1]:4 * t[1] + 4], o.rearrange("p (b w) -> p b w", b=4))
                ins.then_inc(turned_out, 1)
            def exps(u):
                lo = 0 if units[u][0] else P
                act.wait_ge(masked, u + 1)
                act.activation(dsk[:, u % 4], dsk[:, u % 4], ACT.Exp)
                for j in range(4):
                    ins = act.activation(sm[:, u % 2, j, lo:], sm[:, u % 2, j, lo:], ACT.Exp, bias=nmx[:, u % 4, j:j + 1],
                                         accum_out=ssum[:, u % 4, j:j + 1])
                ins.then_inc(expd, 1)

            def keep_probs(u):
                act.wait_ge(ptd, u + 1)
                for h in ((0, 1) if units[u][0] else (1,)):
                    ins = act.copy(pt[:, 4 * h:4 * h + 4], bank(c, 4 + h).rearrange("p (j q) -> p j q", j=4))
                ins.then_inc(pt_out, 1)

            for u in range(len(units) + 1):
                if u < len(units):
                    exps(u)
                if u:
                    keep_probs(u - 1)
            nu = len(units)
            for kv in range(2):
                act.wait_ge(masked_s, kv + 1)
                act.activation(dsk[:, kv, 0:1], dsk[:, kv, 0:1], ACT.Exp)
                act.activation(sm[:, kv, 0, 0:P + SAMP], sm[:, kv, 0, 0:P + SAMP], ACT.Exp, bias=nmx[:, kv, 0:1],
                               accum_out=ssum[:, kv, 0:1]).then_inc(expd, 1)
            for kv in range(2):
                act.wait_ge(ptd, nu + 1 + kv)
                act.copy(pt[:, 2 * kv], bank(c, 4 + kv)[:, 0:P])
                act.copy(pt[0:SAMP, 2 * kv + 1], bank(c, 4 + kv)[0:SAMP, P:2 * P]).then_inc(pt_out, 1)
            for kv in range(2):
                act.wait_ge(av_done, nu + 1 + kv)
                act.copy(mixt[:, 2 * kv:2 * kv + 2, SEQ:TOK],
                         bank(c, 6 + kv)[:, 0:2 * SAMP].rearrange("p (j t) -> p j t", j=2)).then_inc(av_out, 1)
            act.wait_ge(av_out, nu + 2)

        @block.vector
        def _(v):
            step = c.dve_step.on(v)
            for n in range(NT):
                r = ROWS[n]
                h = ha[0:r, n, 0:640].rearrange("p (h s d) -> p s h d", s=2, d=32)
                cos = over(cst(c, K_COS + 32 * n, 32, r), 1, [r, 10, 32])
                sin = over(cst(c, K_SIN + 32 * n, 32, r), 1, [r, 10, 32])
                a, b_, e, f = (rt[0:r, i] for i in range(4))
                v.tensor_tensor(a, h[:, 0], cos, ALU.mult)
                v.tensor_tensor(b_, h[:, 1], sin, ALU.mult)
                v.tensor_tensor(e, h[:, 1], cos, ALU.mult)
                step(v.tensor_tensor(f, h[:, 0], sin, ALU.mult))
                q = qr[0:r, n, 0:512].rearrange("p (j g s d) -> p s g j d", g=2, s=2, d=32)
                k = qr[0:r, n, 512:640].rearrange("p (g s d) -> p s g d", s=2, d=32)
                for s, (x, y, op) in enumerate(((a, b_, ALU.subtract), (e, f, ALU.add))):
                    for g in range(2):
                        v.tensor_tensor(q[:, s, g], x[:, 4 * g:4 * g + 4], y[:, 4 * g:4 * g + 4], op)
                    ins = v.tensor_tensor(k[:, s], x[:, 8:10], y[:, 8:10], op)
                ins.then_inc(rotated, 1)
                v.wait_ge(rotated, n + 1)
            v.wait_ge(sink_in, 80)

            def mask(u):
                n, kv = units[u]
                lo = 0 if n else P
                v.wait_ge(scored, u + 1)
                if u >= 2:
                    v.wait_ge(ptd, u - 1)
                for i in range(2):
                    s = bank(c, 2 * (u % 2) + i).rearrange("p (j w) -> p j w", j=2)[:, :, lo:]
                    m = over(cst(c, K_SWA + lo, 2 * P - lo), 1, [P, 2, 2 * P - lo])
                    ins = v.scalar_tensor_tensor(sm[:, u % 2, 2 * i:2 * i + 2, lo:], s, HD ** -0.5, m, ALU.mult, ALU.add)
                step(ins)
                step(v.tensor_reduce(mx[:, u % 4], sm[:, u % 2, :, lo:], AX, ALU.max))
                sk = sink[:, 4 * kv:4 * kv + 4]
                step(v.tensor_tensor(mx[:, u % 4], mx[:, u % 4], sk, ALU.max))
                v.tensor_scalar(nmx[:, u % 4], mx[:, u % 4], -1.0, None, ALU.mult)
                v.tensor_tensor(dsk[:, u % 4], sk, mx[:, u % 4], ALU.subtract).then_inc(masked, 1)

            def divide(u):
                n, kv = units[u]
                v.wait_ge(expd, u + 1)
                step(v.tensor_tensor(den[:, u % 4], ssum[:, u % 4], dsk[:, u % 4], ALU.add))
                step(v.reciprocal(den[:, u % 4], den[:, u % 4]))
                v.wait_ge(av_done, u + 1)
                o = bank(c, 6 + u % 2)[:, 0:4 * HD].rearrange("p (j d) -> p j d", j=4)
                v.tensor_tensor(mix[:, n, 256 * kv:256 * kv + 256].rearrange("p (j d) -> p j d", j=4), o,
                                over(den[:, u % 4], 2, [P, 4, HD]), ALU.mult).then_inc(av_out, 1)

            nu = len(units)
            v.wait_ge(turned_out, len(turns))
            mask(0)
            mask(1)
            for u in range(nu):
                if u + 2 < nu:
                    mask(u + 2)
                divide(u)
            v.tensor_copy(qs.rearrange("p (j t) -> p j t", j=4), qt[:, 0:4, SEQ:TOK])
            v.tensor_tensor(qm[:].rearrange("p b (j t) -> p b j t", j=4), over(qt[:, 0:4, SEQ:TOK], 1, [P, NB, 4, SAMP]),
                            over(cst(c, K_BM, NB * SAMP).rearrange("p (b t) -> p b t", b=NB), 2, [P, NB, 4, SAMP]),
                            ALU.mult).then_inc(masked, 1)
            for kv in range(2):
                v.wait_ge(scored, nu + 1 + kv)
                v.wait_ge(ptd, nu)
                step(v.scalar_tensor_tensor(sm[:, kv, 0, 0:P + SAMP], bank(c, kv, P + SAMP), HD ** -0.5,
                                            cst(c, K_SMP, P + SAMP), ALU.mult, ALU.add))
                step(v.tensor_reduce(mx[:, kv, 0:1], sm[:, kv, 0, 0:P + SAMP], AX, ALU.max))
                step(v.tensor_tensor(mx[:, kv, 0:1], mx[:, kv, 0:1], sink_rows[:, kv:kv + 1], ALU.max))
                v.tensor_scalar(nmx[:, kv, 0:1], mx[:, kv, 0:1], -1.0, None, ALU.mult)
                v.tensor_tensor(dsk[:, kv, 0:1], sink_rows[:, kv:kv + 1], mx[:, kv, 0:1], ALU.subtract).then_inc(masked_s, 1)
            for kv in range(2):
                v.wait_ge(expd, nu + 1 + kv)
                step(v.tensor_tensor(den[:, kv, 0:1], ssum[:, kv, 0:1], dsk[:, kv, 0:1], ALU.add))
                step(v.reciprocal(den[:, kv, 0:1], den[:, kv, 0:1]))
                v.tensor_scalar(sm[:, kv, 0, 0:P + SAMP], sm[:, kv, 0, 0:P + SAMP], den[:, kv, 0:1], None,
                                ALU.mult).then_inc(masked, 1)


UW = 4 * 4 * P + 4 * SAMP
A_QT2 = A_HA
A_S = A_QT2 + 2 * 3 * 512
A_NG = A_S + 512
A_S0 = A_SIL
A_AM = A_S0 + NB * 512
A_VN = A_AM + 1024
A_GB = A_VN + 512
A_QE = A_GB + 512
assert A_QE + 512 <= A_CT
A_T = A_MIX + NT * D
A_TT, A_AT, A_M1, A_QET, A_QK = (A_T + UW * i for i in range(1, 6))
A_X1 = A_T + 6 * UW
A_WM = A_X1 + 1024
A_SM3 = A_WM + 2 * NB * SAMP
assert A_SM3 + 372 <= ARENA


def phase_delta(c):
    nc, d = c.nc, c.dram
    ct, mix, hd = words(c, A_CT, NT, CONV), words(c, A_MIX, NT, D), words(c, A_HD, NT, 520)
    qkt = words(c, A_QT2, 2, 3, 512)
    s_p, s_s = words(c, A_S, DNH, DK), words(c, A_S0, NB, DNH, DK)
    ng = words(c, A_NG, DK)
    am, vn, gb, qe = words(c, A_AM, 2, 512), words(c, A_VN, DNH, DK), words(c, A_GB, DNH, P), words(c, A_QE, 512)
    x1 = words(c, A_X1, 1024)
    wm = words(c, A_WM, 2, NB, SAMP)
    at = [A_SM3]

    def small(*shape):
        n = 1
        for s in shape:
            n *= s
        at[0] += n
        assert at[0] <= ARENA
        return words(c, at[0] - n, *shape)

    ss, beta, g, tz = small(NT, 8), small(NT, 4), small(NT, 4), small(NT, 4)
    gc, eg = small(NT, 8), small(NT, 8)
    egl, egs = small(4, 4), small(4, NB)
    alog, dtb, ms = small(4), small(4), small(NT, 4)

    def unit(base, n, rows=P):
        r = ROWS[n]
        return words(c, base + 512 * n, 4, r, rows=rows)

    def mask(k_prompt, k_sample, n):
        return cst(c, k_prompt, P) if n < 4 else cst(c, k_sample, SAMP, SAMP)

    ident = cst(c, K_ID, P)
    s = c.sem
    params_in, states_in = s("delta_params_in"), s("delta_states_in")
    z_done, small_act = s("delta_z_silu"), s("delta_small_by_act")
    squares, betas = s("delta_squares_summed"), s("delta_small_by_dve")
    spread, cums, gc_out, dd_set, exps, dd_exp = (s("delta_" + x) for x in ("decay_spread", "cumulated", "cumulated_out",
                                                                         "differences_set", "row_exps", "decay_exps"))
    prepared, turned3, turned3_act, turned3_dve, kk, at_set = (s("delta_" + x) for x in (
        "rows_prepared", "rows_turned", "turned_out_act", "turned_out_dve", "products", "a_set"))
    am_set, m1, m1_out, pp, t_new = (s("inverse_" + x) for x in ("a_masked", "m1", "m1_out", "products", "updated"))
    uw, u_out, w_out = s("delta_uw"), s("delta_u_out"), s("delta_w_out")
    ws, vnew, od, o_out, sd, s_new = (s("scan_" + x) for x in ("ws", "new_values", "outputs", "outputs_out", "state_delta",
                                                               "state_new"))
    wm_set, km_set = s("sample_w_masked"), s("sample_k_masked")
    root, sroot = s("delta_mean_squares"), s("delta_roots")
    s_zero = s("state_cleared")
    stored = s("delta_stored")
    beta_set, gain_set, units_set, bv_set, kg_set, sq_set = (s("delta_" + x) for x in (
        "beta_set", "gate_gains_set", "units_set", "beta_v_set", "decayed_k_set", "output_squares_set"))
    items = [(lev, n) for lev in range(LEVELS) for n in range(NT) if n < 4 or lev < 2]
    item_no = {x: i for i, x in enumerate(items)}

    def is_last(lev, n):
        return (lev + 1, n) not in item_no

    with nc.Block(no_gpsimd_drain=True) as block:
        @block.sync
        def _(sp):
            sp.dma_start(alog, d.dn_a_log[0].partition_broadcast(P)).then_inc(params_in, 16)
            sp.dma_start(dtb, d.dn_dt_bias[0].partition_broadcast(P)).then_inc(params_in, 16)
            sp.dma_start(ng, d.dn_norm_g[0].partition_broadcast(P)).then_inc(params_in, 16)
            sp.dma_start(s_s[:].rearrange("p b h v -> p (b h) v"), d.state_dn[0].rearrange("b h k v -> k (b h) v")).then_inc(states_in, 16)
            sp.wait_ge(s_new, 4)
            sp.dma_start(d.dn_state_prompt[0, 0].rearrange("h k v -> k h v"), s_p).then_inc(stored, 16)
            sp.wait_ge(s_new, 8)
            sp.dma_start(d.dn_state_sample[0].rearrange("b h k v -> k (b h) v"), s_s[:].rearrange("p b h v -> p (b h) v")).then_inc(stored, 16)
            sp.wait_ge(stored, 32)

        @block.tensor
        def _(pe):
            def cumulate(n):
                r = ROWS[n]
                ut, one = mask(K_UT, K_UTS, n), mask(K_ONE, K_ONES, n)
                pe.wait_ge(spread, n + 1)
                if n:
                    pe.wait_ge(gc_out, n)
                    pe.wait_ge(dd_set, n)
                pe.matmul(bank(c, 0, 4, r), ut, g[0:r, n], start=True, stop=True)
                pe.matmul(bank(c, 0, 8, r)[:, 4:8], one, g[0:r, n], start=True, stop=True)
                for h in range(DNH):
                    ins = pe.matmul(bank(c, 1)[:, r * h:r * h + r], gb[0:r, h], ut, start=True, stop=True)
                ins.then_inc(cums, 1)

            cumulate(0)
            for n in range(NT):
                r = ROWS[n]
                pe.wait_ge(prepared, n + 1)
                if n:
                    pe.wait_ge(turned3_act, n)
                    pe.wait_ge(turned3_dve, n)
                kb = x1[:, 0:512]
                for i, src in enumerate((ct[:, n, 0:512], ct[:, n, 512:1024], kb, qe)):
                    for h in range(DNH):
                        ins = pe.transpose(bank(c, 2 + i)[:, r * h:r * h + r], src[0:r, P * h:P * h + P], ident[0:r, 0:r])
                ins.then_inc(turned3, 1)
                if n + 1 < NT:
                    cumulate(n + 1)
                pe.wait_ge(turned3_act, n + 1)
                pe.wait_ge(turned3_dve, n + 1)
                if n:
                    pe.wait_ge(at_set, n)
                q3 = [qkt[:, n % 2, i, 0:4 * r].rearrange("p (h t) -> p h t", h=4) for i in range(3)]
                for h in range(DNH):
                    pe.matmul(bank(c, 6, 512, r)[:, r * h:r * h + r], q3[1][:, h], q3[2][:, h], start=True, stop=True)
                for h in range(DNH):
                    ins = pe.matmul(bank(c, 7, 512, r)[:, r * h:r * h + r], q3[1][:, h], q3[0][:, h], start=True, stop=True)
                ins.then_inc(kk, 1)

            def first(i):
                lev, n = items[i]
                r = ROWS[n]
                pe.wait_ge(am_set, i + 1)
                if lev:
                    pe.wait_ge(t_new, item_no[lev - 1, n] + 1)
                if i >= 2:
                    pe.wait_ge(m1_out, i - 1)
                a = am[0:r, i % 2, 0:4 * r].rearrange("p (h t) -> p h t", h=4)
                for h in range(DNH):
                    ins = pe.matmul(bank(c, i % 2, 512, r)[:, r * h:r * h + r], a[:, h], unit(A_T, n, r)[:, h], start=True, stop=True)
                ins.then_inc(m1, 1)

            def second(i):
                lev, n = items[i]
                r = ROWS[n]
                pe.wait_ge(m1_out, i + 1)
                if i >= 2:
                    pe.wait_ge(t_new, i - 1)
                tt, x = unit(A_TT, n, r), unit(A_M1, n, r)
                if not is_last(lev, n):
                    for h in range(DNH):
                        pe.matmul(bank(c, 2 + i % 2, 512, r)[:, r * h:r * h + r], tt[:, h], x[:, h], start=True, stop=True)
                for h in range(DNH):
                    ins = pe.matmul(bank(c, 4 + i % 2, 512, r)[:, r * h:r * h + r], x[:, h], tt[:, h], start=True, stop=True)
                ins.then_inc(pp, 1)

            pe.wait_ge(at_set, NT)
            pe.wait_ge(units_set, 1)
            for i in range(len(items) + 1):
                if i < len(items):
                    first(i)
                if i:
                    second(i - 1)

            pe.wait_ge(t_new, len(items))
            pe.wait_ge(bv_set, 1)
            pe.wait_ge(kg_set, NT)
            for n in range(NT):
                r = ROWS[n]
                if n >= 2:
                    pe.wait_ge(u_out, n - 1)
                    pe.wait_ge(w_out, n - 1)
                tt = unit(A_TT, n, r)
                for h in range(DNH):
                    pe.matmul(bank(c, n % 2, 512, r)[:, P * h:P * h + P], tt[:, h], ct[0:r, n, 1024 + P * h:1152 + P * h], start=True, stop=True)
                for h in range(DNH):
                    ins = pe.matmul(bank(c, 2 + n % 2)[:, r * h:r * h + r], ct[0:r, n, P * h:P * h + P], tt[:, h], start=True, stop=True)
                ins.then_inc(uw, 1)

            pe.wait_ge(u_out, NT)
            pe.wait_ge(w_out, NT)
            for n in range(4):
                if n:
                    pe.wait_ge(s_new, n)
                else:
                    pe.wait_ge(s_zero, 1)
                for h in range(DNH):
                    ins = pe.matmul(bank(c, 4)[:, P * h:P * h + P], unit(A_M1, n)[:, h], s_p[:, h], start=True, stop=True)
                ins.then_inc(ws, 1)
                pe.wait_ge(vnew, n + 1)
                for h in range(DNH):
                    ins = pe.matmul(bank(c, 5)[:, P * h:P * h + P], ct[:, n, 512 + P * h:640 + P * h], vn[:, h], start=True, stop=True)
                ins.then_inc(sd, 1)
                if n >= 2:
                    pe.wait_ge(o_out, n - 1)
                for h in range(DNH):
                    pe.matmul(bank(c, 6 + n % 2)[:, P * h:P * h + P], unit(A_QET, n)[:, h], s_p[:, h], start=True, stop=False)
                    ins = pe.matmul(bank(c, 6 + n % 2)[:, P * h:P * h + P], unit(A_QK, n)[:, h], vn[:, h], start=False, stop=True)
                ins.then_inc(od, 1)
            pe.wait_ge(states_in, 16)
            pe.wait_ge(o_out, 4)
            pe.wait_ge(s_new, 4)
            for h in range(DNH):
                pe.wait_ge(wm_set, h + 1)
                for b in range(NB):
                    ins = pe.matmul(bank(c, 4, 512, SAMP)[:, P * h:P * h + P], wm[:, 0, b], s_s[:, b, h], start=(b == 0), stop=(b == NB - 1))
                ins.then_inc(ws, 1)
                pe.wait_ge(vnew, 5 + h)
                for b in range(NB):
                    pe.matmul(bank(c, 6, 512, SAMP)[:, P * h:P * h + P], wm[:, 1, b], s_s[:, b, h], start=(b == 0), stop=False)
                pe.matmul(bank(c, 6, 512, SAMP)[:, P * h:P * h + P], unit(A_QK, 4, SAMP)[:, h], vn[0:SAMP, h], start=False, stop=True).then_inc(od, 1)
                pe.wait_ge(km_set, h + 1)
                km = x1[0:SAMP].rearrange("p (b k) -> p b k", b=NB)
                for b in range(NB):
                    ins = pe.matmul(bank(c, 2 + b // 4)[:, P * (b % 4):P * (b % 4) + P], km[:, b], vn[0:SAMP, h], start=True, stop=True)
                ins.then_inc(sd, 1)

        @block.scalar
        def _(act):
            step = c.act_step.on(act)
            for n in range(NT):
                ins = act.activation(hd[0:ROWS[n], n, 8:520], hd[0:ROWS[n], n, 8:520], ACT.Silu)
            ins.then_inc(z_done, 1)
            act.wait_ge(params_in, 48)
            act.activation(beta[:], hd[:, :, 0:4], ACT.Exp, scale=-1.0).then_inc(small_act, 1)
            act.activation(alog, alog, ACT.Exp).then_inc(small_act, 1)
            act.wait_ge(betas, 1)
            act.activation(g[:], g[:], ACT.Exp, scale=-1.0).then_inc(small_act, 1)
            act.wait_ge(betas, 2)
            act.activation(g[:], g[:], ACT.Ln).then_inc(small_act, 1)
            act.wait_ge(squares, 1)
            act.activation(ss[:], ss[:], ACT.Sqrt).then_inc(small_act, 1)
            for n in range(NT):
                r = ROWS[n]
                act.wait_ge(gc_out, n + 1)
                act.activation(eg[0:r, n], eg[0:r, n], ACT.Exp)
                total = egl[:, n] if n < 4 else egs[:]
                act.activation(total, total, ACT.Exp).then_inc(exps, 1)
                act.wait_ge(dd_set, n + 1)
                dd = x1[0:r, 512:512 + 4 * r]
                act.activation(dd, dd, ACT.Exp).then_inc(dd_exp, 1)
                act.wait_ge(turned3, n + 1)
                act.copy(qkt[:, n % 2, 1, 0:4 * r], bank(c, 3, 4 * r))
                act.copy(qkt[:, n % 2, 2, 0:4 * r], bank(c, 4, 4 * r)).then_inc(turned3_act, 1)
            for i, (lev, n) in enumerate(items):
                r = ROWS[n]
                act.wait_ge(m1, i + 1)
                act.copy(unit(A_M1, n, r), bank(c, i % 2, 4 * r, r).rearrange("p (h t) -> p h t", h=4)).then_inc(m1_out, 1)
            for n in range(NT):
                r = ROWS[n]
                act.wait_ge(uw, n + 1)
                act.copy(unit(A_M1, n), bank(c, 2 + n % 2, 4 * r).rearrange("p (h t) -> p h t", h=4)).then_inc(w_out, 1)
            for n in range(4):
                act.wait_ge(od, n + 1)
                act.copy(mix[:, n, 512:1024], bank(c, 6 + n % 2)).then_inc(o_out, 1)
            act.wait_ge(od, 8)
            act.copy(mix[0:SAMP, 4, 512:1024], bank(c, 6, 512, SAMP)).then_inc(o_out, 1)
            act.wait_ge(root, 1)
            act.activation(ms[:], ms[:], ACT.Sqrt).then_inc(sroot, 1)

        @block.vector
        def _(v):
            step = c.dve_step.on(v)
            step(v.memset(ss[:], 0.0))
            for n in range(NT):
                r = ROWS[n]
                step(v.tensor_tensor(x1[0:r], ct[0:r, n, 0:1024], ct[0:r, n, 0:1024], ALU.mult))
                step(v.tensor_reduce(ss[0:r, n], x1[0:r].rearrange("p (h k) -> p h k", h=8), AX, ALU.add))
            v.tensor_scalar(ss[:], ss[:], RMS_EPS, None, ALU.add).then_inc(squares, 1)
            v.wait_ge(params_in, 48)
            step(v.tensor_tensor(tz[:], hd[:, :, 4:8], over(dtb, 1, [P, NT, 4]), ALU.add))
            v.scalar_tensor_tensor(g[:], tz[:], -1.0, tz[:], ALU.mult, ALU.max).then_inc(betas, 1)
            v.wait_ge(small_act, 2)
            step(v.tensor_scalar(beta[:], beta[:], 1.0, None, ALU.add))
            v.reciprocal(beta[:], beta[:]).then_inc(beta_set, 1)
            v.wait_ge(beta_set, 1)
            v.wait_ge(small_act, 3)
            v.tensor_scalar(g[:], g[:], 1.0, None, ALU.add).then_inc(betas, 1)
            v.wait_ge(small_act, 4)
            step(v.scalar_tensor_tensor(g[:], tz[:], 0.0, g[:], ALU.max, ALU.add))
            step(v.scalar_tensor_tensor(g[:], g[:], -1.0, over(alog, 1, [P, NT, 4]), ALU.mult, ALU.mult))
            v.wait_ge(small_act, 5)
            step(v.reciprocal(ss[:], ss[:]))
            step(v.tensor_scalar(ss[:, :, 0:4], ss[:, :, 0:4], DK ** -0.5, None, ALU.mult))

            def rows(n, a, k, scale, out, heads=4):
                r = ROWS[n]
                src = ct[0:r, n, a:a + P * heads].rearrange("p (h k) -> p h k", h=heads)
                return v.tensor_tensor(out[0:r].rearrange("p (h k) -> p h k", h=heads), src, over(scale[0:r, n, k:k + heads], 2, [r, heads, P]), ALU.mult)

            def front(n):
                r = ROWS[n]
                v.tensor_copy(gb[0:r], over(g[0:r, n], 2, [r, 4, P])).then_inc(spread, 1)
                step(rows(n, 0, 0, ss, ct[:, n, 0:1024], 8))

            front(0)
            for n in range(NT):
                r = ROWS[n]
                v.wait_ge(cums, n + 1)
                v.tensor_copy(gc[0:r, n], bank(c, 0, 8, r))
                if n < 4:
                    ins = v.tensor_copy(egl[:, n], bank(c, 1).rearrange("p (h t) -> p h t", h=4)[:, :, P - 1])
                else:
                    ins = v.tensor_copy(egs[:], bank(c, 1, 4 * SAMP).rearrange("p (h b l) -> p h b l", h=4, l=NL)[:, :, :, NL - 1])
                step(ins)
                v.tensor_copy(eg[0:r, n, 0:4], gc[0:r, n, 0:4])
                v.tensor_tensor(eg[0:r, n, 4:8], gc[0:r, n, 4:8], gc[0:r, n, 0:4], ALU.subtract).then_inc(gc_out, 1)
                if n:
                    v.wait_ge(at_set, n)
                dd = x1[0:r, 512:512 + 4 * r].rearrange("p (h t) -> p h t", h=4)
                for h in range(DNH):
                    ins = v.tensor_scalar(dd[:, h], bank(c, 1, 4 * r, r)[:, r * h:r * h + r], gc[0:r, n, h:h + 1], 0.0, ALU.subtract, ALU.min)
                ins.then_inc(dd_set, 1)
                if n:
                    v.wait_ge(turned3, n)
                    v.wait_ge(kg_set, n)
                v.wait_ge(exps, n + 1)
                rows(n, 512, 0, beta, x1[:, 0:512])
                rows(n, 0, 0, eg, qe).then_inc(prepared, 1)
                if n + 1 < NT:
                    front(n + 1)
                v.wait_ge(dd_exp, n + 1)
                step(v.tensor_tensor(dd, dd, over(mask(K_UT, K_UTS, n), 1, [r, 4, r]), ALU.mult))
                v.wait_ge(turned3, n + 1)
                v.tensor_copy(qkt[:, n % 2, 0, 0:4 * r], bank(c, 2, 4 * r))
                v.tensor_copy(unit(A_QET, n), bank(c, 5, 4 * r).rearrange("p (h t) -> p h t", h=4)).then_inc(turned3_dve, 1)
                v.wait_ge(kk, n + 1)
                v.tensor_tensor(unit(A_AT, n, r), bank(c, 6, 4 * r, r).rearrange("p (h t) -> p h t", h=4), dd, ALU.mult)
                v.tensor_tensor(unit(A_QK, n, r), bank(c, 7, 4 * r, r).rearrange("p (h t) -> p h t", h=4), dd, ALU.mult).then_inc(at_set, 1)

            v.wait_ge(at_set, NT)

            def mask_a(i):
                lev, n = items[i]
                r = ROWS[n]
                if i >= 2:
                    v.wait_ge(m1, i - 1)
                v.tensor_tensor(am[0:r, i % 2, 0:4 * r].rearrange("p (h t) -> p h t", h=4), unit(A_AT, n, r),
                                over(cst(c, K_LEV + lev * P, r, r), 1, [r, 4, r]), ALU.mult).then_inc(am_set, 1)

            def update(i):
                lev, n = items[i]
                r = ROWS[n]
                v.wait_ge(pp, i + 1)
                for a, b_ in ((A_T, 2), (A_TT, 4))[is_last(lev, n):]:
                    ins = v.tensor_tensor(unit(a, n, r), unit(a, n, r), bank(c, b_ + i % 2, 4 * r, r).rearrange("p (h t) -> p h t", h=4), ALU.subtract)
                ins.then_inc(t_new, 1)

            mask_a(0)
            mask_a(1)
            for i in range(len(items)):
                if i + 2 < len(items):
                    mask_a(i + 2)
                update(i)
            v.memset(s_p[:], 0.0).then_inc(s_zero, 1)
            for n in range(NT):
                r = ROWS[n]
                v.wait_ge(uw, n + 1)
                v.tensor_copy(ct[0:r, n, 1024:1536], bank(c, n % 2, 512, r)).then_inc(u_out, 1)
            v.wait_ge(u_out, NT)
            for n in range(4):
                v.wait_ge(ws, n + 1)
                if n:
                    v.wait_ge(od, n)
                v.tensor_tensor(vn[:].rearrange("p h k -> p (h k)"), ct[:, n, 1024:1536], bank(c, 4), ALU.subtract).then_inc(vnew, 1)
                v.wait_ge(od, n + 1)
                v.wait_ge(exps, NT)
                for h in range(DNH):
                    ins = v.scalar_tensor_tensor(s_p[:, h], s_p[:, h], egl[:, n, h:h + 1], bank(c, 5)[:, P * h:P * h + P], ALU.mult, ALU.add)
                ins.then_inc(s_new, 1)
            v.wait_ge(states_in, 16)
            v.wait_ge(w_out, NT)
            v.wait_ge(kg_set, NT)
            bm = cst(c, K_BM, NB * SAMP).rearrange("p (b t) -> p b t", b=NB)
            for h in range(DNH):
                if h:
                    v.wait_ge(od, 4 + h)
                v.tensor_tensor(wm[:, 0], over(unit(A_M1, 4)[:, h], 1, [P, NB, SAMP]), bm, ALU.mult)
                v.tensor_tensor(wm[:, 1], over(unit(A_QET, 4)[:, h], 1, [P, NB, SAMP]), bm, ALU.mult).then_inc(wm_set, 1)
                if h:
                    v.wait_ge(sd, 4 + h)
                v.tensor_tensor(x1[0:SAMP].rearrange("p (b k) -> p b k", b=NB), over(ct[0:SAMP, 4, 512 + P * h:640 + P * h], 1, [SAMP, NB, DK]),
                                over(cst(c, K_BR, NB, SAMP), 2, [SAMP, NB, DK]), ALU.mult).then_inc(km_set, 1)
                v.wait_ge(ws, 5 + h)
                v.tensor_tensor(vn[0:SAMP, h], ct[0:SAMP, 4, 1024 + P * h:1152 + P * h], bank(c, 4, 512, SAMP)[:, P * h:P * h + P], ALU.subtract).then_inc(vnew, 1)
                v.wait_ge(od, 5 + h)
                step(v.tensor_tensor(s_s[:, :, h], s_s[:, :, h], over(egs[:, h], 2, [P, NB, DK]), ALU.mult))
                v.wait_ge(sd, 5 + h)
                for i in range(2):
                    ins = v.tensor_tensor(s_s[:, 4 * i:4 * i + 4, h], s_s[:, 4 * i:4 * i + 4, h], bank(c, 2 + i).rearrange("p (b k) -> p b k", b=4), ALU.add)
                ins.then_inc(s_new, 1)
            v.wait_ge(o_out, 5)
            step(v.memset(ms[:], 1.0))
            v.wait_ge(sd, 8)
            step(v.tensor_tensor(x1[0:SAMP, 0:512], mix[0:SAMP, 4, 512:1024], mix[0:SAMP, 4, 512:1024], ALU.mult))
            v.wait_ge(sq_set, 4)
            for n in range(NT):
                sq = unit(A_T, n) if n < 4 else x1[0:SAMP, 0:512].rearrange("p (h k) -> p h k", h=4)
                ins = v.tensor_reduce(ms[0:ROWS[n], n], sq, AX, ALU.add)
            step(ins)
            v.tensor_scalar(ms[:], ms[:], 1.0 / DK, RMS_EPS, ALU.mult, ALU.add).then_inc(root, 1)
            v.wait_ge(sroot, 1)
            step(v.reciprocal(ms[:], ms[:]))
            v.wait_ge(gain_set, 1)
            outs = [mix[0:ROWS[n], n, 512:1024].rearrange("p (h k) -> p h k", h=4) for n in range(NT)]
            for n, o in enumerate(outs):
                ins = v.tensor_tensor(o, o, over(ms[0:ROWS[n], n], 2, [ROWS[n], 4, P]), ALU.mult)
            step(ins)
            for n, o in enumerate(outs):
                ins = v.tensor_tensor(o, o, hd[0:ROWS[n], n, 8:520].rearrange("p (h k) -> p h k", h=4), ALU.mult)
            step(ins)

        @block.gpsimd
        def _(pool):
            for n in range(NT):
                r = ROWS[n]
                for a in (A_T, A_TT):
                    ins = pool.tensor_copy(unit(a, n, r), over(ident[0:r, 0:r], 1, [r, 4, r]))
            ins.then_inc(units_set, 1)
            pool.wait_ge(beta_set, 1)

            def rows(n, a, scale, k, src=None):
                r = ROWS[n]
                o = ct[0:r, n, a:a + 512].rearrange("p (h k) -> p h k", h=4)
                return pool.tensor_tensor(o, o if src is None else src, over(scale[0:r, n, k:k + 4], 2, [r, 4, P]), ALU.mult)

            for n in range(NT):
                pool.wait_ge(prepared, n + 1)
                pool.wait_ge(turned3, n + 1)
                rows(n, 0, eg, 0, x1[0:ROWS[n], 0:512].rearrange("p (h k) -> p h k", h=4))
                rows(n, 512, eg, 4).then_inc(kg_set, 1)
            for n in range(NT):
                ins = rows(n, 1024, beta, 0)
            ins.then_inc(bv_set, 1)
            pool.wait_ge(z_done, 1)
            pool.wait_ge(params_in, 48)
            for n in range(NT):
                r = ROWS[n]
                z = hd[0:r, n, 8:520].rearrange("p (h k) -> p h k", h=4)
                ins = pool.tensor_tensor(z, z, over(ng[0:r], 1, [r, 4, P]), ALU.mult)
            ins.then_inc(gain_set, 1)
            for n in range(4):
                pool.wait_ge(o_out, n + 1)
                o = mix[:, n, 512:1024].rearrange("p (h k) -> p h k", h=4)
                pool.tensor_tensor(unit(A_T, n), o, o, ALU.mult).then_inc(sq_set, 1)


class LayerNorm:
    def __init__(self, c, name, gain_bias, at):
        self.c, self.xa, self.gb = c, words(c, A_X, NT, D), gain_bias
        self.stats, self.mean_var = words(c, at, NT, 12), words(c, at + NT * 12, NT, 2)
        self.gb_in, self.var_set, self.std_set, self.normed = (c.sem(name + x) for x in ("_gain_in", "_var_set", "_std_set", "_tile_done"))

    SIZE = NT * 14

    def load(self, sp, g, b):
        sp.dma_start(self.gb[:, 0:D], g[0].partition_broadcast(P)).then_inc(self.gb_in, 16)
        sp.dma_start(self.gb[:, D:2 * D], b[0].partition_broadcast(P)).then_inc(self.gb_in, 16)

    def statistics(self, v, step, n):
        r = ROWS[n]
        st, mv = self.stats[0:r, n].rearrange("p (h s) -> p h s", h=2), self.mean_var[0:r, n]
        for h in range(2):
            ins = v.bn_stats(st[:, h], self.xa[0:r, n, 512 * h:512 * h + 512])
        step(ins)
        step(v.bn_aggr(mv, self.stats[0:r, n]))
        v.tensor_scalar(mv[:, 1:2], mv[:, 1:2], LN_EPS, None, ALU.add).then_inc(self.var_set, 1)

    def root(self, act, n):
        r = ROWS[n]
        act.wait_ge(self.var_set, n + 1)
        mv = self.mean_var[0:r, n]
        act.activation(mv[:, 1:2], mv[:, 1:2], ACT.Sqrt).then_inc(self.std_set, 1)

    def finish(self, v, step, n):
        r = ROWS[n]
        x, mv = self.xa[0:r, n], self.mean_var[0:r, n]
        v.wait_ge(self.std_set, n + 1)
        step(v.reciprocal(mv[:, 1:2], mv[:, 1:2]))
        step(v.tensor_scalar(x, x, mv[:, 0:1], mv[:, 1:2], ALU.subtract, ALU.mult))
        if n == 0:
            v.wait_ge(self.gb_in, 32)
        step(v.tensor_tensor(x, x, self.gb[0:r, 0:D], ALU.mult))
        v.tensor_tensor(x, x, self.gb[0:r, D:2 * D], ALU.add).then_inc(self.normed, 1)


def turn_x(pe, c, n, h, o):
    xa, ident, r = words(c, A_X, NT, D), cst(c, K_ID, P), ROWS[n]
    for j in range(4):
        k = 4 * h + j
        ins = pe.transpose(bank(c, o)[:, r * j:r * j + r], xa[0:r, n, P * k:P * k + P], ident[0:r, 0:r])
    return ins


def keep_turned_x(act, c, n, h, o):
    r = ROWS[n]
    return act.copy(words(c, A_XT, KD, TOK)[:, 4 * h:4 * h + 4, tile_cols(n)], bank(c, o, 4 * r).rearrange("p (k t) -> p k t", k=4))


L_G = A_FREE
R0 = L_G + 2 * D
R1, R2 = R0 + KD * D, R0 + 2 * KD * D
L_MEMT = R0 + 3 * KD * D
L_MEM = L_MEMT + KD * MEM
L_MKT = L_MEM + 2 * D
L_MV = L_MKT + KD * MEM
L_Q = L_MV + 2 * D
L_S = L_Q + KD * TOK
assert L_S + 1800 <= ARENA and R2 + KD * D > A_MIX


OUT_ORDER = [(0, 0), (1, 0), (0, 1), (1, 1)] + [(n, h) for n in range(2, NT) for h in range(2)]


def mix_plan():
    plan = [("mix", n, h, "act") for n in range(NT) for h in range(2) if n < 4 or h]
    plan += [("mem", m, h, "act") for m in range(2) for h in range(2)]
    plan += [("out", n, h, "dve") for n, h in OUT_ORDER]
    plan += [("mk", m, h, "act") for m in range(2) for h in range(2)]
    plan += [("mkt", m, h, "act") for m in range(2) for h in range(2)]
    plan += [("mv", m, h, "act") for m in range(2) for h in range(2)]
    return plan + [("x1", n, h, "act") for n in range(NT) for h in range(2)]


def emptied(plan, g, engine):
    return sum(1 for item in plan[:g + 1] if item[-1] == engine)


def phase_mix(c):
    nc, d = c.nc, c.dram
    xa, xt, mix = words(c, A_X, NT, D), words(c, A_XT, KD, TOK), words(c, A_MIX, NT, D)
    w_o, w_ck, w_cv = (words(c, a, KD, D) for a in (R0, R1, R2))
    memt, mem = words(c, L_MEMT, KD, MEM), words(c, L_MEM, 2, D)
    mkt, mv, mk = words(c, L_MKT, KD, MEM), words(c, L_MV, 2, D), words(c, L_Q, 2, D)
    ident = cst(c, K_ID, P)
    plan = mix_plan()
    last = {item[0]: g for g, item in enumerate(plan)}
    ln = LayerNorm(c, "ln1", words(c, L_G, 2 * D), L_S)
    wo_in = [c.sem(f"w_o_in{h}") for h in range(2)]
    mem_in, wck_in, wcv_in = (c.sem(x) for x in ("mem_in", "w_ck_in", "w_cv_in"))
    done, by_act, by_dve = c.sem("mix_group_done"), c.sem("mix_emptied_act"), c.sem("mix_emptied_dve")
    stored = c.sem("mem_kv_stored")
    c.wcq_in, c.wco_in = c.shared_sem("w_cq_in"), c.shared_sem("w_co_in")
    rows = "(k p) c -> p k c"

    with nc.Block(no_gpsimd_drain=True) as block:
        @block.sync
        def _(sp):
            sp.dma_start(mem, d.mem_prompt[0].rearrange("(m p) c -> p m c", p=P)).then_inc(mem_in, 16)
            for h in range(2):
                sp.dma_start(w_o[:, :, 512 * h:512 * h + 512], d.w_o[0].rearrange(rows, p=P)[:, :, 512 * h:512 * h + 512]).then_inc(wo_in[h], 16)
            ln.load(sp, d.ln1_g, d.ln1_b)
            sp.dma_start(w_ck, d.w_ck[0].rearrange(rows, p=P)).then_inc(wck_in, 16)
            sp.wait_ge(by_act, emptied(plan, last["mix"], "act"))
            sp.dma_start(w_cv, d.w_cv[0].rearrange(rows, p=P)).then_inc(wcv_in, 16)
            sp.wait_ge(done, last["mk"] + 1)
            sp.dma_start(w_ck, d.w_cq[0].rearrange(rows, p=P)).then_inc(c.wcq_in, 16)
            sp.wait_ge(by_act, emptied(plan, last["mk"], "act"))
            sp.dma_start(d.mem_k_prompt[0, 0].rearrange("(m p) h c -> p m (h c)", p=P), mk).then_inc(stored, 16)
            sp.wait_ge(by_act, emptied(plan, last["mv"], "act"))
            sp.dma_start(d.mem_v_prompt[0, 0].rearrange("(m p) h c -> p m (h c)", p=P), mv).then_inc(stored, 16)
            sp.dma_start(w_cv, d.w_co[0].rearrange(rows, p=P)).then_inc(c.wco_in, 16)
            sp.wait_ge(stored, 32)

        @block.tensor
        def _(pe):
            for g, (kind, n, h, _) in enumerate(plan):
                if g >= 8:
                    who = plan[g - 8][-1]
                    pe.wait_ge(by_act if who == "act" else by_dve, emptied(plan, g - 8, who))
                o = bank(c, g % 8)
                if kind == "mix":
                    r = ROWS[n]
                    for j in range(4):
                        k = 4 * h + j
                        ins = pe.transpose(o[:, r * j:r * j + r], mix[0:r, n, P * k:P * k + P], ident[0:r, 0:r])
                elif kind == "mem":
                    pe.wait_ge(mem_in, 16)
                    for j in range(4):
                        k = 4 * h + j
                        ins = pe.transpose(o[:, P * j:P * j + P], mem[:, n, P * k:P * k + P], ident)
                elif kind == "out":
                    if n == 0:
                        pe.wait_ge(wo_in[h], 16)
                        pe.wait_ge(by_act, emptied(plan, last["mix"], "act"))
                    for k in range(KD):
                        ins = pe.matmul(o[0:ROWS[n]], xt[:, k, tile_cols(n)], w_o[:, k, 512 * h:512 * h + 512], start=(k == 0), stop=(k == KD - 1))
                elif kind in ("mk", "mv"):
                    if (n, h) == (0, 0):
                        pe.wait_ge(wck_in if kind == "mk" else wcv_in, 16)
                        pe.wait_ge(by_act, emptied(plan, last["mem"], "act"))
                    w = w_ck if kind == "mk" else w_cv
                    for k in range(KD):
                        ins = pe.matmul(o, memt[:, k, P * n:P * n + P], w[:, k, 512 * h:512 * h + 512], start=(k == 0), stop=(k == KD - 1))
                elif kind == "mkt":
                    pe.wait_ge(by_act, emptied(plan, last["mk"], "act"))
                    for j in range(4):
                        k = 4 * h + j
                        ins = pe.transpose(o[:, P * j:P * j + P], mk[:, n, P * k:P * k + P], ident)
                else:
                    if h == 0:
                        pe.wait_ge(ln.normed, n + 1)
                    ins = turn_x(pe, c, n, h, g % 8)
                ins.then_inc(done, 1)

        @block.scalar
        def _(act):
            for g, (kind, n, h, who) in enumerate(plan):
                if who != "act":
                    if h:
                        ln.root(act, n)
                    continue
                act.wait_ge(done, g + 1)
                src = bank(c, g % 8)
                if kind == "mix":
                    r = ROWS[n]
                    cols = tile_cols(n)
                    ins = act.copy(xt[:, 4 * h:4 * h + 4, cols], src[:, 0:4 * r].rearrange("p (k t) -> p k t", k=4))
                elif kind in ("mem", "mkt"):
                    dst = memt if kind == "mem" else mkt
                    ins = act.copy(dst[:, 4 * h:4 * h + 4, P * n:P * n + P], src.rearrange("p (k t) -> p k t", k=4))
                elif kind in ("mk", "mv"):
                    ins = act.copy((mk if kind == "mk" else mv)[:, n, 512 * h:512 * h + 512], src)
                else:
                    ins = keep_turned_x(act, c, n, h, g % 8)
                ins.then_inc(by_act, 1)

        @block.vector
        def _(v):
            step = c.dve_step.on(v)
            for i, (n, h) in enumerate(OUT_ORDER):
                g, r = plan.index(("out", n, h, "dve")), ROWS[n]
                v.wait_ge(done, g + 1)
                x = xa[0:r, n, 512 * h:512 * h + 512]
                v.scalar_tensor_tensor(x, x, ALPHA, bank(c, g % 8, 512, r), ALU.mult, ALU.add).then_inc(by_dve, 1)
                if h:
                    v.wait_ge(by_dve, i + 1)
                    ln.statistics(v, step, n)
                    if n:
                        ln.finish(v, step, n - 1)
            ln.finish(v, step, NT - 1)


X_PT = R0
X_P = X_PT + XH * 2 * TOK
X_K, X_V = R1, R1 + 2 * 2 * D
X_KT = L_MEMT
X_QM = L_G
assert MEM * XH == D and X_P + 2 * D <= R1 and X_KT + 2 * KD * MEM <= L_MKT


def phase_cross(c):
    nc, d = c.nc, c.dram
    xa, xt, ot = words(c, A_X, NT, D), words(c, A_XT, KD, TOK), words(c, A_XT, KD, TOK)
    w_cq, w_co = words(c, R1, KD, D), words(c, R2, KD, D)
    mkt, mv, q = words(c, L_MKT, KD, MEM), words(c, L_MV, 2, D), words(c, L_Q, KD, TOK)
    pt, pr = words(c, X_PT, XH, 2, TOK), words(c, X_P, 2, XH, MEM)
    ks, kt = words(c, X_K, 2, 2 * D), words(c, X_KT, 2, KD * MEM)
    vs = [words(c, at, 2 * D) for at in (X_V, X_V + 2 * D, L_MKT, L_MV, X_K, X_K + 2 * D, X_V, X_V + 2 * D)]
    qm = words(c, X_QM, NB, KD, SAMP)
    pm, om = words(c, X_KT, NB, XH * 2, SAMP), words(c, X_KT + 2 * D, D, rows=SAMP)
    ident = cst(c, K_ID, P)
    mx, sums = words(c, L_S + LayerNorm.SIZE, NT, 4), words(c, L_S + LayerNorm.SIZE + 20, NT, 4)
    ln = LayerNorm(c, "ln2", words(c, L_G, 2 * D), L_S)
    scale = (D // XH) ** -0.5
    s = c.sem
    q_done, q_out, qm_set = s("cross_q_done"), s("cross_q_out"), s("cross_q_masked")
    scored, max_set, expd, prob_set, ptd, pt_out = (s("cross_" + x) for x in ("scored", "max_set", "exp_done", "probs_set",
                                                                             "probs_turned", "probs_turned_out"))
    av, av_out = s("cross_av_done"), s("cross_av_out")
    pm_set, om_set, om_turned = s("sample_probs_masked"), s("sample_av_rows_set"), s("sample_av_turned")
    k_in, v_in = [s(f"mem_k_in{i}") for i in range(2)], [s(f"mem_v_in{b}") for b in range(NB)]
    k_turned, k_out_act, k_out_dve, k_used, v_used = (s("mem_k_" + x) for x in ("turned", "out_act", "out_dve", "scored", "v_used"))
    od, resid, x2d, x2_out = s("cross_out_done"), s("cross_residual_set"), s("x2_turned"), s("x2_turned_out")

    with nc.Block(no_gpsimd_drain=True) as block:
        @block.sync
        def _(sp):
            def load_values(b):
                sp.dma_start(vs[b].rearrange("p (m c) -> p m c", m=2), d.cache_mem_v[0, b].rearrange("(m p) h c -> p m (h c)", p=P)).then_inc(v_in[b], 16)

            sp.wait_ge(q_done, 16)
            for b in range(NB):
                if b >= 2:
                    sp.wait_ge(k_used, b - 1)
                sp.dma_start(ks[:, b % 2].rearrange("p (m c) -> p m c", m=2), d.cache_mem_k[0, b].rearrange("(m p) h c -> p m (h c)", p=P)).then_inc(k_in[b % 2], 16)
                if b == 2:
                    sp.wait_ge(av, KD)
                if b < 4:
                    load_values(b)
            sp.wait_ge(k_used, NB)
            for b in range(4, 6):
                load_values(b)
            ln.load(sp, d.ln2_g, d.ln2_b)
            for b in range(6, NB):
                sp.wait_ge(v_used, b - 5)
                load_values(b)

        @block.tensor
        def _(pe):
            pe.wait_ge(c.wcq_in, 16)
            for g in range(16):
                ch, h = g // 2, g % 2
                if g >= 8:
                    pe.wait_ge(q_out, g - 7)
                for k in range(KD):
                    ins = pe.matmul(bank(c, g % 8, HALF), w_cq[:, k, P * ch:P * ch + P], xt[:, k, HALF * h:HALF * h + HALF], start=(k == 0), stop=(k == KD - 1))
                ins.then_inc(q_done, 1)
            pe.wait_ge(q_out, 16)

            def scores(n):
                if n >= 2:
                    pe.wait_ge(expd, n - 1)
                for h in range(XH):
                    for e in range(2):
                        ins = pe.matmul(bank(c, 2 * (n % 2) + h // 2)[:, MEM * (h % 2):MEM * (h % 2) + MEM], q[:, 2 * h + e, tile_cols(n)],
                                        mkt[:, 2 * h + e], start=(e == 0), stop=(e == 1))
                ins.then_inc(scored, 1)

            def turn_probs(n):
                r = ROWS[n]
                pe.wait_ge(prob_set, n + 1)
                if n:
                    pe.wait_ge(pt_out, n)
                for m in range(2):
                    for h in range(XH):
                        ins = pe.transpose(bank(c, 4 + m)[:, r * h:r * h + r], pr[0:r, n % 2, h, P * m:P * m + P], ident[0:r, 0:r])
                ins.then_inc(ptd, 1)

            for n in range(5):
                if n < 4:
                    scores(n)
                if n:
                    turn_probs(n - 1)
            pe.wait_ge(pt_out, 4)
            for g in range(KD):
                if g >= 2:
                    pe.wait_ge(av_out, g - 1)
                for m in range(2):
                    ins = pe.matmul(bank(c, 6 + g % 2), mv[:, m, P * g:P * g + P], pt[:, g // 2, m, 0:SEQ], start=(m == 0), stop=(m == 1))
                ins.then_inc(av, 1)
            pe.wait_ge(expd, 4)
            pe.wait_ge(av_out, KD)
            pe.wait_ge(qm_set, 1)
            for b in range(NB):
                pe.wait_ge(k_in[b % 2], 16 * (b // 2 + 1))
                if b:
                    pe.wait_ge(k_out_act, b)
                    pe.wait_ge(k_out_dve, b)
                for m in range(2):
                    for ch in range(KD):
                        ins = pe.transpose(bank(c, 2 * m + ch // 4)[:, P * (ch % 4):P * (ch % 4) + P], ks[:, b % 2, D * m + P * ch:D * m + P * ch + P], ident)
                ins.then_inc(k_turned, 1)
                pe.wait_ge(k_out_act, b + 1)
                pe.wait_ge(k_out_dve, b + 1)
                for h in range(XH):
                    for e in range(2):
                        ch = 2 * h + e
                        ins = pe.matmul(bank(c, 6 + h // 2, 512, SAMP)[:, MEM * (h % 2):MEM * (h % 2) + MEM], qm[:, b, ch], kt[:, b % 2, MEM * ch:MEM * ch + MEM],
                                        start=(b == 0 and e == 0 and h % 2 == 0), stop=(b == NB - 1 and e == 1), skip_group_check=True)
                ins.then_inc(k_used, 1)
            turn_probs(4)
            pe.wait_ge(pt_out, 5)
            pe.wait_ge(pm_set, 1)
            for b in range(NB):
                pe.wait_ge(v_in[b], 16)
                for h in range(XH):
                    for m in range(2):
                        ins = pe.matmul(bank(c, h // 2, 512, SAMP)[:, MEM * (h % 2):MEM * (h % 2) + MEM], pm[:, b, 2 * h + m],
                                        vs[b][:, D * m + MEM * h:D * m + MEM * h + MEM],
                                        start=(b == 0 and h % 2 == 0 and m == 0), stop=(b == NB - 1 and m == 1), skip_group_check=True)
                ins.then_inc(v_used, 1)
            pe.wait_ge(om_set, 1)
            for ch in range(KD):
                ins = pe.transpose(bank(c, 2)[:, SAMP * ch:SAMP * ch + SAMP], om[:, P * ch:P * ch + P], ident[0:SAMP, 0:SAMP])
            ins.then_inc(om_turned, 1)
            pe.wait_ge(av_out, KD + 1)
            pe.wait_ge(c.wco_in, 16)

            def project(n):
                if n >= 2:
                    pe.wait_ge(resid, 2 * (n - 1))
                for h in range(2):
                    for k in range(KD):
                        ins = pe.matmul(bank(c, 4 + 2 * (n % 2) + h, 512, ROWS[n]), ot[:, k, tile_cols(n)], w_co[:, k, 512 * h:512 * h + 512], start=(k == 0), stop=(k == KD - 1))
                    ins.then_inc(od, 1)

            def turn(n):
                pe.wait_ge(ln.normed, n + 1)
                for h in range(2):
                    if n >= 2:
                        pe.wait_ge(x2_out, 2 * n + h - 3)
                    turn_x(pe, c, n, h, (2 * n + h) % 4).then_inc(x2d, 1)

            for n in range(NT):
                project(n)
            for n in range(NT):
                turn(n)

        @block.scalar
        def _(act):
            for g in range(16):
                act.wait_ge(q_done, g + 1)
                act.copy(q[:, g // 2, HALF * (g % 2):HALF * (g % 2) + HALF], bank(c, g % 8, HALF)).then_inc(q_out, 1)

            def exps(n, b0):
                r = ROWS[n]
                act.wait_ge(max_set, n + 1)
                if n >= 2:
                    act.wait_ge(ptd, n - 1)
                for h in range(XH):
                    ins = act.activation(pr[0:r, n % 2, h], bank(c, b0 + h // 2, 512, r)[:, MEM * (h % 2):MEM * (h % 2) + MEM], ACT.Exp,
                                         bias=mx[0:r, n, h:h + 1], scale=scale, accum_out=sums[0:r, n, h:h + 1])
                ins.then_inc(expd, 1)

            def keep_probs(n):
                r = ROWS[n]
                act.wait_ge(ptd, n + 1)
                for m in range(2):
                    ins = act.copy(pt[:, :, m, tile_cols(n)], bank(c, 4 + m, 4 * r).rearrange("p (h t) -> p h t", h=XH))
                ins.then_inc(pt_out, 1)

            for n in range(5):
                if n < 4:
                    exps(n, 2 * (n % 2))
                if n:
                    keep_probs(n - 1)
            for g in range(KD):
                act.wait_ge(av, g + 1)
                act.copy(ot[:, g, 0:SEQ], bank(c, 6 + g % 2)).then_inc(av_out, 1)
            for b in range(NB):
                act.wait_ge(k_turned, b + 1)
                if b >= 2:
                    act.wait_ge(k_used, b - 1)
                dst = kt[:, b % 2].rearrange("p (c m t) -> p c m t", c=KD, m=2)
                for e in range(2):
                    ins = act.copy(dst[:, 4 * e:4 * e + 4, 0], bank(c, e).rearrange("p (c t) -> p c t", c=4))
                ins.then_inc(k_out_act, 1)
            exps(4, 6)
            keep_probs(4)
            act.wait_ge(v_used, NB)
            for i in range(2):
                ins = act.copy(om[:, 512 * i:512 * i + 512], bank(c, i, 512, SAMP))
            ins.then_inc(om_set, 1)
            act.wait_ge(om_turned, 1)
            act.copy(ot[:, :, SEQ:TOK], bank(c, 2, KD * SAMP).rearrange("p (c t) -> p c t", c=KD)).then_inc(av_out, 1)
            for n in range(NT):
                ln.root(act, n)
            for n in range(NT):
                for h in range(2):
                    act.wait_ge(x2d, 2 * n + h + 1)
                    keep_turned_x(act, c, n, h, (2 * n + h) % 4).then_inc(x2_out, 1)

        @block.vector
        def _(v):
            step = c.dve_step.on(v)

            def maxima(n, b0):
                r = ROWS[n]
                if n < 4:
                    v.wait_ge(scored, n + 1)
                for i in range(2):
                    ins = v.tensor_reduce(mx[0:r, n, 2 * i:2 * i + 2], bank(c, b0 + i, 512, r).rearrange("p (h m) -> p h m", h=2), AX, ALU.max)
                step(ins)
                v.tensor_scalar(mx[0:r, n], mx[0:r, n], -scale, None, ALU.mult).then_inc(max_set, 1)

            def divide(n):
                r = ROWS[n]
                v.wait_ge(expd, n + 1)
                step(v.reciprocal(sums[0:r, n], sums[0:r, n]))
                x = pr[0:r, n % 2]
                v.tensor_tensor(x, x, over(sums[0:r, n], 2, [r, XH, MEM]), ALU.mult).then_inc(prob_set, 1)

            v.wait_ge(q_out, 16)
            bm = cst(c, K_BM, NB * SAMP).rearrange("p (b t) -> p b t", b=NB)
            v.tensor_tensor(qm[:], over(q[:, :, SEQ:TOK], 1, [P, NB, KD, SAMP]), over(bm, 2, [P, NB, KD, SAMP]), ALU.mult).then_inc(qm_set, 1)
            for n in range(5):
                if n < 4:
                    maxima(n, 2 * (n % 2))
                if n:
                    divide(n - 1)
            for b in range(NB):
                v.wait_ge(k_turned, b + 1)
                if b >= 2:
                    v.wait_ge(k_used, b - 1)
                dst = kt[:, b % 2].rearrange("p (c m t) -> p c m t", c=KD, m=2)
                for e in range(2):
                    ins = v.tensor_copy(dst[:, 4 * e:4 * e + 4, 1], bank(c, 2 + e).rearrange("p (c t) -> p c t", c=4))
                ins.then_inc(k_out_dve, 1)
            v.wait_ge(k_used, NB)
            maxima(4, 6)
            divide(4)
            v.wait_ge(pt_out, NT)
            ps = pt[:, :, :, SEQ:TOK].rearrange("p h m t -> p (h m) t")
            v.tensor_tensor(pm[:], over(ps, 1, [P, NB, 2 * XH, SAMP]), over(bm, 2, [P, NB, 2 * XH, SAMP]), ALU.mult).then_inc(pm_set, 1)
            for n in range(NT + 1):
                if n < NT:
                    r = ROWS[n]
                    for h in range(2):
                        v.wait_ge(od, 2 * n + h + 1)
                        x = xa[0:r, n, 512 * h:512 * h + 512]
                        v.scalar_tensor_tensor(x, x, ALPHA, bank(c, 4 + 2 * (n % 2) + h, 512, r), ALU.mult, ALU.add).then_inc(resid, 1)
                    v.wait_ge(resid, 2 * n + 2)
                    ln.statistics(v, step, n)
                if n:
                    ln.finish(v, step, n - 1)


HI, LO = 0, 1


def plain(ap):
    return ap.bitcast(F32)


def passes3(pe, out, weights, moving, start=True, stop=True):
    last = len(weights) - 1
    for k, (w, m) in enumerate(zip(weights, moving)):
        pe.matmul(out, w[HI], m[HI], start=start and k == 0, stop=False)
        pe.matmul(out, w[HI], m[LO], start=False, stop=False)
        ins = pe.matmul(out, w[LO], m[HI], start=False, stop=stop and k == last)
    return ins


F_SC = A_FREE
F_SC_END = F_SC + NT * 16 * NK
F_W = F_SC_END
F_Q = F_W + 4 * KD * 2 * NK
F_KEY = F_Q + 2 * 2 * TOK
F_END = F_KEY + 4 * NK
LOWEST = -3e38


def phase_scores(c):
    nc, d = c.nc, c.dram
    xt, xr = words(c, A_XT, KD, TOK), shaped(c.xr[:, :], 2, KD, TOK)
    w, wr = words(c, F_W, 4, KD, 2 * NK), shaped(c.wr[:, :], 2, 2, KD, 2 * NK)
    q, key, keyt = words(c, F_Q, 2, 2, TOK), words(c, F_KEY, 2, NK), words(c, F_KEY + 2 * NK, 2, NK)
    sc = words(c, F_SC, NT, 16, NK)
    ident = cst(c, K_ID, P)
    s = c.sem
    w_in, key_in = [s(f"w_pq_in{h}") for h in range(4)], s("peer_keys_in")
    keys_turned, keys_out = s("keys_turned"), s("keys_turned_out")
    x_hi, x_lo, w_hi, w_lo = s("x2_high_set"), s("x2_low_set"), s("w_pq_high_set"), s("w_pq_low_set")
    q_done, q_out, scored, score_out = s("peer_q_done"), s("peer_q_out"), s("peer_scored"), s("peer_scores_out")
    PAIRS = 3

    with nc.Block(no_gpsimd_drain=True) as block:
        @block.sync
        def _(sp):
            for h in range(PH):
                if h >= 4:
                    sp.wait_ge(w_lo, h - 3)
                sp.dma_start(w[:, h % 4], d.w_pq[0, :, h].rearrange("(k p) c -> p k c", p=P)).then_inc(w_in[h % 4], 16)
                if h == 0:
                    sp.dma_start(key[:, 0], d.peer_keys1[0]).then_inc(key_in, 16)
                    sp.dma_start(key[:, 1], d.peer_keys2[0]).then_inc(key_in, 16)

        @block.tensor
        def _(pe):
            pe.wait_ge(key_in, 32)
            for i in range(2):
                ins = pe.transpose(bank(c, 7)[:, NK * i:NK * i + NK], key[:, i], ident)
            ins.then_inc(keys_turned, 1)
            pe.wait_ge(x_lo, KD)

            def queries(h):
                pe.wait_ge(w_lo, h + 1)
                for i in range(4):
                    g = 4 * h + i
                    ch, half = i // 2, i % 2
                    if g >= 4:
                        pe.wait_ge(q_out, g - 3)
                    cols = slice(HALF * half, HALF * half + HALF)
                    ins = passes3(pe, bank(c, i, HALF), [[wr[:, h % 2, x, k, NK * ch:NK * ch + NK] for x in (HI, LO)] for k in range(KD)],
                                  [[xr[:, x, k, cols] for x in (HI, LO)] for k in range(KD)])
                    ins.then_inc(q_done, 1)

            def scores(h):
                pe.wait_ge(q_out, 4 * h + 4)
                if h == 0:
                    pe.wait_ge(keys_out, 1)
                for i in range(PAIRS):
                    if h:
                        pe.wait_ge(score_out, PAIRS * h - PAIRS + i + 1)
                    for n in range(2 * i, min(2 * i + 2, NT)):
                        for j in range(2):
                            o = bank(c, 4 + i, 512, ROWS[n])[:, 256 * (n % 2) + NK * j:256 * (n % 2) + NK * j + NK]
                            ins = pe.matmul(o, q[:, h % 2, j, tile_cols(n)], keyt[:, j], start=True, stop=True)
                    ins.then_inc(scored, 1)

            for h in range(PH + 1):
                if h < PH:
                    queries(h)
                if h:
                    scores(h - 1)

        @block.scalar
        def _(act):
            for k in range(KD):
                act.copy(xr[:, HI, k], xt[:, k]).then_inc(x_hi, 1)
            act.wait_ge(keys_turned, 1)
            act.copy(keyt[:], bank(c, 7, 2 * NK).rearrange("p (i k) -> p i k", i=2)).then_inc(keys_out, 1)

            def split(h):
                act.wait_ge(w_in[h % 4], 16 * (h // 4 + 1))
                if h >= 2:
                    act.wait_ge(q_done, 4 * h - 4)
                act.copy(wr[:, h % 2, HI], w[:, h % 4]).then_inc(w_hi, 1)

            split(0)
            for h in range(PH):
                if h + 1 < PH:
                    split(h + 1)
                for i in range(4):
                    act.wait_ge(q_done, 4 * h + i + 1)
                    if h >= 2 and i == 0:
                        act.wait_ge(scored, PAIRS * (h - 1))
                    act.copy(q[:, h % 2, i // 2, HALF * (i % 2):HALF * (i % 2) + HALF], bank(c, i, HALF)).then_inc(q_out, 1)

        @block.vector
        def _(v):
            for k in range(KD):
                v.wait_ge(x_hi, k + 1)
                v.tensor_tensor(xr[:, LO, k], xt[:, k], plain(xr[:, HI, k]), ALU.subtract).then_inc(x_lo, 1)

            def split(h):
                v.wait_ge(w_hi, h + 1)
                v.tensor_tensor(wr[:, h % 2, LO], w[:, h % 4], plain(wr[:, h % 2, HI]), ALU.subtract).then_inc(w_lo, 1)

            split(0)
            split(1)
            for h in range(PH):
                if h + 2 < PH:
                    split(h + 2)
                for i in range(PAIRS):
                    v.wait_ge(scored, PAIRS * h + i + 1)
                    if i < 2:
                        ins = v.tensor_copy(sc[:, 2 * i:2 * i + 2, 2 * h:2 * h + 2], bank(c, 4 + i).rearrange("p (n j k) -> p n j k", n=2, j=2))
                    else:
                        ins = v.tensor_copy(sc[0:SAMP, 4, 2 * h:2 * h + 2], bank(c, 6, 256, SAMP).rearrange("p (j k) -> p j k", j=2))
                    ins.then_inc(score_out, 1)


TG = 32
NTG = TOK // TG
UG = 2
NQ = NK // UG
QG = TG // 4
BEFORE = NQ - 2 * NTG
H_U = F_SC_END
H_UT = H_U + 2 * UG * D
H_G = A_XT
H_C = H_G + 2 * UG * TOK
assert H_C + PH * 256 <= A_FREE
H_E = H_UT + 2 * D
H_V = H_E + PH * 256
H_B = H_V + 3 * 256
H_K = H_B + 6 * 128
H_T = H_K + NT * 3 * 128
H_END = H_T + 4 * TOK
F_GST = (F_SC, F_SC + NK * TG)
F_EXP = F_SC + 2 * NK * TG
assert F_EXP + 2 * TOK <= F_SC_END


def after(eng, sem, n):
    if not isinstance(n, int) or n > 0:
        eng.wait_ge(sem, n)


UNROLL = 2


def looped(eng, first, stop, last, body):
    assert (stop - first) % UNROLL == 0
    for i in range(first):
        body(i, i % 2)
    with eng.Fori(first, stop - UNROLL + 1, UNROLL) as i:
        body(i, first % 2)
        for more in range(1, UNROLL):
            body(i + more, (first + more) % 2)
    for i in range(stop, last):
        body(i, i % 2)


def loads(i, slot):
    return 16 * (i // 2 + 1) if isinstance(i, int) else (i - slot) * 8 + 16


def phase_hidden(c):
    nc, d = c.nc, c.dram
    xr = shaped(c.xr[:, :], 2, KD, TOK)
    sc = words(c, F_SC, NT, 16, NK)
    u, ut, hid = words(c, H_U, 2, UG, D), words(c, H_UT, 2, KD, P), words(c, H_G, 2, UG, TOK)
    utr = shaped(c.utr[:, :], 2, 2, KD, P)
    best, where, wheref = words(c, H_V, 16, 16), words(c, H_V + 256, 256).bitcast(U32), words(c, H_V + 512, 16, 16)
    where = where.rearrange("p (g k) -> p g k", g=16)
    cand, hot16 = words(c, H_C, PH, 256), words(c, H_E, PH, 256)
    row = [words(c, H_B + 128 * i, 128) for i in range(6)]
    top, pair, hi, lo, hif, lof = row[0], row[1].bitcast(U32), row[2].bitcast(U32), row[3].bitcast(U32), row[4], row[5]
    kept, kt = words(c, H_K, NT, 3, 128), words(c, H_T, 4, TOK)
    gate, inv = words(c, F_EXP, 2, TOK)[:, 0], words(c, F_EXP, 2, TOK)[:, 1]
    hot, gst = shaped(c.hot[:, :], 2, 3, 4 * P), [words(c, a, NK, TG) for a in F_GST]
    gate_hi = c.gate_hi[:, :]
    ident, iota, one_head = cst(c, K_ID, P), cst(c, K_IOTA, NK), cst(c, K_HEAD, P)
    s = c.sem
    u_in, hid_stored, gates_stored = ([s(f"{x}{i}") for i in range(2)] for x in ("expert_u_in", "hidden_stored", "gates_stored"))
    turned, ut_kept, ut_low, hid_done, gelu_done = (s("expert_" + x) for x in ("u_turned", "u_kept", "u_low_set", "hidden_done", "gelu_done"))
    picked, pairs_turned, pairs_out, exps, sums, gates_set = (s("peer_" + x) for x in (
        "tile_picked", "pairs_turned", "pairs_turned_out", "gate_exps", "gate_sums", "gates_set"))
    hot_set, made, gkept = s("one_hots_set"), s("gates_made"), s("gates_kept")
    u_rows = d.peer_u[0].rearrange("(b a) d -> a b d", a=P)

    def engine_program(eng, group, between, tokens):
        looped(eng, 2, BEFORE, BEFORE, lambda q, slot: [group(q, slot, b) for b in range(UG)])
        between()

        def body(tg, slot):
            for j in range(2 * UG):
                group(BEFORE + tg * 2 + j // UG, j // UG, j % UG)
                tokens(tg, slot, j)
        looped(eng, 3, NTG - 2, NTG, body)

    with nc.Block(no_gpsimd_drain=True) as block:
        @block.sync
        def _(sp):
            def load(q, slot):
                after(sp, turned, q * (2 * UG) - 2 * UG)
                sp.dma_start(u[:, slot], u_rows[:, bass.ds(q * UG, UG)]).then_inc(u_in[slot], 16)

            def group(q, slot, b):
                if b == 0:
                    if not isinstance(q, int) or q + 1 < NQ:
                        load(q + 1, 1 - slot)
                else:
                    if not isinstance(q, int) or q > 0:
                        store(q - 1, 1 - slot)

            def store(q, slot):
                sp.wait_ge(gelu_done, q * (2 * UG) + 2 * UG)
                sp.dma_start(c.hidden_dram[:, bass.ds(q * UG, UG)], hid[:, slot]).then_inc(hid_stored[slot], 16)

            def store_gates(tg, slot):
                sp.wait_ge(gkept, tg * QG + QG)
                sp.dma_start(c.gates_dram[:, bass.ds(tg, 1)].rearrange("p g k t -> p (g k) t"), gst[slot]).then_inc(gates_stored[slot], 16)

            def tokens(tg, slot, j):
                if j == 1 and (not isinstance(tg, int) or tg > 0):
                    store_gates(tg - 1, 1 - slot)

            load(0, 0)
            engine_program(sp, group, lambda: None, tokens)
            store(NQ - 1, (NQ - 1) % 2)
            store_gates(NTG - 1, (NTG - 1) % 2)
            for i in range(2):
                sp.wait_ge(hid_stored[i], 16 * (NQ // 2))
                sp.wait_ge(gates_stored[i], 16 * ((NTG + 1 - i) // 2))

        @block.tensor
        def _(pe):
            def turn(n, slot, b):
                for h in range(2):
                    after(pe, ut_kept, 2 * n - 1 + h)
                    for j in range(4):
                        k = 4 * h + j
                        ins = pe.transpose(bank(c, h)[:, P * j:P * j + P], u[:, slot, b, P * k:P * k + P], ident)
                    ins.then_inc(turned, 1)

            def hidden(n, b):
                pe.wait_ge(ut_kept, 2 * n + 2)
                for h in range(2):
                    cols = slice(HALF * h, HALF * h + HALF)
                    after(pe, gelu_done, 2 * n - 1 + h)
                    for k in range(KD):
                        pe.matmul(bank(c, 2 + h, HALF), utr[:, b, HI, k], xr[:, HI, k, cols], start=(k == 0), stop=False)
                        pe.matmul(bank(c, 2 + h, HALF), utr[:, b, HI, k], xr[:, LO, k, cols], start=False, stop=False)
                pe.wait_ge(ut_low, 2 * n + 2)
                for h in range(2):
                    for k in range(KD):
                        ins = pe.matmul(bank(c, 2 + h, HALF), utr[:, b, LO, k], xr[:, HI, k, HALF * h:HALF * h + HALF], start=False, stop=(k == KD - 1))
                    ins.then_inc(hid_done, 1)

            def group(q, slot, b):
                n = q * UG + b
                if b == 0:
                    turn(n + 1, slot, 1)
                elif not isinstance(q, int) or q + 1 < NQ:
                    pe.wait_ge(u_in[1 - slot], loads(q + 1, 1 - slot))
                    turn(n + 1, 1 - slot, 0)
                hidden(n, b)

            def between():
                for n in range(NT):
                    r = ROWS[n]
                    pe.wait_ge(picked, n + 1)
                    if n >= 2:
                        pe.wait_ge(pairs_out, n - 1)
                    for i in range(3):
                        ins = pe.transpose(bank(c, 4 + n % 2)[:, r * i:r * i + r], kept[0:r, n, i], ident[0:r, 0:r])
                    ins.then_inc(pairs_turned, 1)
                pe.wait_ge(exps, 1)
                for h in range(2):
                    ins = pe.matmul(bank(c, 6 + h, HALF), one_head, gate[:, HALF * h:HALF * h + HALF], start=True, stop=True)
                ins.then_inc(sums, 1)

            def tokens(tg, slot, j):
                if isinstance(tg, int) and tg == 0 and j == 0:
                    pe.wait_ge(gates_set, 1)
                for i in range(2 * j, 2 * j + 2):
                    g = tg * QG + i
                    pe.wait_ge(hot_set, g + 1)
                    after(pe, gkept, g - 3)
                    for t in range(4):
                        k2, hi_gates, lo_gates = (hot[:, i % 2, x, P * t:P * t + P] for x in range(3))
                        pe.matmul(bank(c, 4 + i % 4)[:, P * t:P * t + P], k2, hi_gates, start=True, stop=False)
                        ins = pe.matmul(bank(c, 4 + i % 4)[:, P * t:P * t + P], k2, lo_gates, start=False, stop=True)
                    ins.then_inc(made, 1)

            pe.wait_ge(u_in[0], 16)
            turn(0, 0, 0)
            engine_program(pe, group, between, tokens)

        @block.scalar
        def _(act):
            def keep(n, b):
                after(act, ut_low, 2 * n - 2)
                after(act, hid_done, 2 * n - 2)
                for h in range(2):
                    act.wait_ge(turned, 2 * n + 1 + h)
                    src = bank(c, h).rearrange("p (k a) -> p k a", k=4)
                    act.copy(utr[:, b, HI, 4 * h:4 * h + 4], src)
                    act.copy(ut[:, b, 4 * h:4 * h + 4], src).then_inc(ut_kept, 1)

            def group(q, slot, b):
                n = q * UG + b
                if b == 0 or not isinstance(q, int) or q + 1 < NQ:
                    keep(n + 1, 1 - b)
                if b == 0:
                    after(act, hid_stored[slot], loads(q, slot) - 16)
                for h in range(2):
                    act.wait_ge(hid_done, 2 * n + 1 + h)
                    act.activation(hid[:, slot, b, HALF * h:HALF * h + HALF], bank(c, 2 + h, HALF), ACT.Gelu_apprx_tanh).then_inc(gelu_done, 1)

            def between():
                for n in range(NT):
                    r = ROWS[n]
                    act.wait_ge(pairs_turned, n + 1)
                    act.copy(kt[:, 0:3, tile_cols(n)], bank(c, 4 + n % 2, 3 * r).rearrange("p (i t) -> p i t", i=3)).then_inc(pairs_out, 1)
                act.wait_ge(pairs_out, NT)
                act.activation(gate, kt[:, 2], ACT.Exp).then_inc(exps, 1)

            def tokens(tg, slot, j):
                if j == 0:
                    after(act, gates_stored[slot], loads(tg, slot) - 16)
                for i in range(2 * j, 2 * j + 2):
                    act.wait_ge(made, tg * QG + (i + 1))
                    act.copy(gst[slot][:, :, 4 * i:4 * i + 4].rearrange("p k t -> p t k"), bank(c, 4 + i % 4).rearrange("p (t k) -> p t k", t=4)).then_inc(gkept, 1)

            keep(0, 0)
            engine_program(act, group, between, tokens)

        @block.gpsimd
        def _(pool):
            def split(n, b):
                for h in range(2):
                    k = slice(4 * h, 4 * h + 4)
                    pool.wait_ge(ut_kept, 2 * n + 1 + h)
                    pool.tensor_tensor(utr[:, b, LO, k], ut[:, b, k], plain(utr[:, b, HI, k]), ALU.subtract).then_inc(ut_low, 1)

            def group(q, slot, b):
                if b == 0 or not isinstance(q, int) or q + 1 < NQ:
                    split(q * UG + (b + 1), 1 - b)

            split(0, 0)
            engine_program(pool, group, lambda: None, lambda tg, slot, j: None)

        @block.vector
        def _(v):
            step = c.dve_step.on(v)

            def best16(values, vals, idx, groups):
                for half in range(2):
                    k = slice(8 * half, 8 * half + 8)
                    for g in range(groups):
                        ins = v.max(vals(g)[:, k], values(g))
                    step(ins)
                    for g in range(groups):
                        ins = v.max_index(idx(g)[:, k], vals(g)[:, k], values(g))
                    step(ins)
                    if half == 0:
                        for g in range(groups):
                            ins = v.match_replace(values(g), vals(g)[:, k], values(g), LOWEST)
                        step(ins)

            for n in range(NT):
                r = ROWS[n]
                best16(lambda g: sc[0:r, n, g], lambda g: best[0:r, g], lambda g: where[0:r, g], 16)
                v.tensor_copy(wheref[0:r], where[0:r])
                b2 = best[0:r].rearrange("p (h s) k -> p s h k", s=2)
                c3 = cand[0:r].rearrange("p h (i j) -> p h i j", i=16)
                step(v.tensor_tensor(c3, over(b2[:, 0], 3, [r, PH, 16, 16]), over(b2[:, 1], 2, [r, PH, 16, 16]), ALU.add))
                t3, p3 = (x[0:r].rearrange("p (h k) -> p h k", h=PH) for x in (top, pair))
                best16(lambda g: cand[0:r, g], lambda g: t3[:, g], lambda g: p3[:, g], PH)
                v.tensor_scalar(hi[0:r], pair[0:r], 4, None, ALU.logical_shift_right)
                step(v.tensor_scalar(lo[0:r], pair[0:r], 15, None, ALU.bitwise_and))
                v.tensor_tensor(kept[0:r, n, 2].rearrange("p (h k) -> p h k", h=PH), t3, over(t3[:, :, 0], 2, [r, PH, 16]), ALU.subtract)
                v.tensor_copy(hif[0:r], hi[0:r])
                step(v.tensor_copy(lof[0:r], lo[0:r]))
                for i, x in enumerate((hif, lof)):
                    h3 = hot16[0:r].rearrange("p h (k j) -> p (h k) j", j=16)
                    h4 = hot16[0:r].rearrange("p h (k j) -> p h k j", j=16)
                    keys = wheref[0:r].rearrange("p (h s) k -> p s h k", s=2)[:, i]
                    step(v.tensor_tensor(h3, over(x[0:r], 2, [r, 128, 16]), over(iota[0:r, 0:16], 1, [r, 128, 16]), ALU.is_equal))
                    step(v.tensor_tensor(h4, h4, over(keys, 2, [r, PH, 16, 16]), ALU.mult))
                    ins = v.tensor_reduce(kept[0:r, n, i], h3, AX, ALU.add)
                    if i == 0:
                        step(ins)
                ins.then_inc(picked, 1)
                v.wait_ge(picked, n + 1)
            v.wait_ge(sums, 1)
            for h in range(2):
                ins = v.reciprocal(inv[:, HALF * h:HALF * h + HALF], bank(c, 6 + h, HALF))
            step(ins)
            step(v.tensor_tensor(gate, gate, inv, ALU.mult))
            step(v.tensor_copy(gate_hi, gate))
            v.tensor_copy(kt[:, 2], plain(gate_hi))
            v.tensor_tensor(kt[:, 3], gate, plain(gate_hi), ALU.subtract).then_inc(gates_set, 1)
            v.wait_ge(gates_set, 1)

            def body(tg, slot):
                for j in range(QG):
                    after(v, made, tg * QG + (j - 1))
                    for t in range(4):
                        col = bass.ds(tg * TG + (4 * j + t), 1)
                        k2, hi_gates, lo_gates = (hot[:, j % 2, x, P * t:P * t + P] for x in range(3))
                        v.tensor_scalar(k2, iota, kt[:, 1, col], None, ALU.is_equal)
                        v.tensor_scalar(hi_gates, iota, kt[:, 0, col], kt[:, 2, col], ALU.is_equal, ALU.mult)
                        ins = v.tensor_scalar(lo_gates, iota, kt[:, 0, col], kt[:, 3, col], ALU.is_equal, ALU.mult)
                    ins.then_inc(hot_set, 1)
            looped(v, 3, NTG - 2, NTG, body)


GB = 4
NG = NK // GB
O_V = A_FREE
O_G = O_V + 2 * 2 * D
O_H = O_G + 2 * GB * TOK
O_GH = O_H + 2 * GB * TOK
O_END = O_GH + 2 * TOK
E_ACC = A_XT


def phase_combine(c):
    nc, d = c.nc, c.dram
    acc = words(c, E_ACC, KD, TOK)
    vv, gt, ht, gated = words(c, O_V, 2, 2, D), words(c, O_G, 2, NTG, GB, TG), words(c, O_H, 2, GB, TOK), words(c, O_GH, 2, TOK)
    vr, gr = shaped(c.vr[:, :], 2, 2, GB * D), shaped(c.gr[:, :], 2, 2, GB * TOK)
    s = c.sem
    v_in, g_in, h_in = ([s(f"{x}_in{i}") for i in range(2)] for x in ("expert_v", "gates", "hidden"))
    v_hi, v_lo, gated_set, g_hi, g_lo, out_done, added, cleared = (s("expert_" + x) for x in (
        "v_high_set", "v_low_set", "gated", "gated_high_set", "gated_low_set", "out_done", "added", "cleared"))
    v_rows = d.peer_v[0].rearrange("(b a) d -> a b d", a=P)
    OPS = 2 * KD
    PER = OPS // GB

    with nc.Block(no_gpsimd_drain=True) as block:
        @block.sync
        def _(sp):
            def body(g, slot):
                for e in range(2):
                    after(sp, v_lo, (g - 1) * GB + (2 * e + 2))
                    sp.dma_start(vv[:, e], v_rows[:, bass.ds(g * GB + 2 * e, 2)]).then_inc(v_in[e], 16)
                    if e == 0:
                        after(sp, gated_set, (g - 1) * GB)
                        sp.dma_start(gt[:, slot].rearrange("p g b t -> p g (b t)"),
                                     c.gates_dram[:, :, bass.ds(g * GB, GB)].rearrange("p g b t -> p g (b t)")).then_inc(g_in[slot], 16)
                        sp.dma_start(ht[:, slot], c.hidden_dram[:, bass.ds(g * GB, GB)]).then_inc(h_in[slot], 16)
            looped(sp, 4, NG, NG, body)

        @block.tensor
        def _(pe):
            def body(g, slot):
                pe.wait_ge(v_lo, g * GB + GB)
                pe.wait_ge(g_lo, g * GB + GB)
                for i in range(OPS):
                    ch, h = i // 2, i % 2
                    after(pe, added, g * OPS + (i - 7))
                    passes3(pe, bank(c, i % 8, HALF), [[vr[:, slot, x, D * b + P * ch:D * b + P * ch + P] for x in (HI, LO)] for b in range(GB)],
                            [[gr[:, slot, x, TOK * b + HALF * h:TOK * b + HALF * h + HALF] for x in (HI, LO)] for b in range(GB)]).then_inc(out_done, 1)
            looped(pe, 4, NG, NG, body)

        @block.scalar
        def _(act):
            def body(g, slot):
                after(act, out_done, (g - 1) * OPS)
                for b in range(GB):
                    n = g * GB + b
                    if b % 2 == 0:
                        act.wait_ge(v_in[b // 2], g * 16 + 16)
                    act.copy(vr[:, slot, HI, D * b:D * b + D], vv[:, b // 2, b % 2]).then_inc(v_hi, 1)
                    act.wait_ge(gated_set, n + 1)
                    act.copy(gr[:, slot, HI, TOK * b:TOK * b + TOK], gated[:, b % 2]).then_inc(g_hi, 1)
            looped(act, 4, NG, NG, body)

        @block.gpsimd
        def _(pool):
            def body(g, slot):
                for b in range(GB):
                    pool.wait_ge(v_hi, g * GB + (b + 1))
                    pool.tensor_tensor(vr[:, slot, LO, D * b:D * b + D], vv[:, b // 2, b % 2], plain(vr[:, slot, HI, D * b:D * b + D]),
                                       ALU.subtract).then_inc(v_lo, 1)
            looped(pool, 4, NG, NG, body)

        @block.vector
        def _(v):
            def add(g, part):
                for i in range(PER * part, PER * part + PER):
                    ch, h = i // 2, i % 2
                    v.wait_ge(out_done, g * OPS + (i + 1))
                    after(v, added, g * OPS + (i - 15))
                    a = acc[:, ch, HALF * h:HALF * h + HALF]
                    v.tensor_tensor(a, a, bank(c, i % 8, HALF), ALU.add).then_inc(added, 1)

            def gate(g, slot, b):
                n = g * GB + b
                after(v, g_lo, n - 1)
                v.tensor_tensor(gated[:, b % 2].rearrange("p (g t) -> p g t", t=TG), ht[:, slot, b].rearrange("p (g t) -> p g t", t=TG),
                                gt[:, slot, :, b], ALU.mult).then_inc(gated_set, 1)

            def body(g, slot):
                v.wait_ge(g_in[slot], loads(g, slot))
                v.wait_ge(h_in[slot], loads(g, slot))
                for b in range(GB):
                    n = g * GB + b
                    gate(g, slot, b)
                    if b == 0:
                        after(v, out_done, (g - 1) * OPS)
                    v.wait_ge(g_hi, n + 1)
                    v.tensor_tensor(gr[:, slot, LO, TOK * b:TOK * b + TOK], gated[:, b % 2], plain(gr[:, slot, HI, TOK * b:TOK * b + TOK]),
                                    ALU.subtract).then_inc(g_lo, 1)
                    if not isinstance(g, int) or g > 0:
                        add(g - 1, b)
            v.memset(acc[:], 0.0).then_inc(cleared, 1)
            v.wait_ge(cleared, 1)
            looped(v, 4, NG, NG, body)
            for part in range(GB):
                add(NG - 1, part)


def phase_finish(c):
    nc, d = c.nc, c.dram
    xa, acc, ident = words(c, A_X, NT, D), words(c, E_ACC, KD, TOK), cst(c, K_ID, P)
    ln = LayerNorm(c, "ln3", words(c, A_FREE, 2 * D), A_FREE + 2 * D)
    turned, resid, stored = c.sem("ffn_turned"), c.sem("ffn_residual_set"), c.sem("y_stored")

    with nc.Block(no_gpsimd_drain=True) as block:
        @block.sync
        def _(sp):
            ln.load(sp, d.ln3_g, d.ln3_b)
            for n in range(NT):
                sp.wait_ge(ln.normed, n + 1)
                dst = d.y_prompt[0, P * n:P * n + P] if n < 4 else d.y_sample.rearrange("b l d -> (b l) d")
                sp.dma_start(dst, xa[0:ROWS[n], n]).then_inc(stored, 16)
            sp.wait_ge(stored, 16 * NT)

        @block.tensor
        def _(pe):
            for n in range(NT):
                r = ROWS[n]
                for h in range(2):
                    g = 2 * n + h
                    if g >= 8:
                        pe.wait_ge(resid, g - 7)
                    for j in range(4):
                        ins = pe.transpose(bank(c, g % 8, 512, r)[:, P * j:P * j + P], acc[:, 4 * h + j, tile_cols(n)], ident)
                    ins.then_inc(turned, 1)

        @block.scalar
        def _(act):
            for n in range(NT):
                ln.root(act, n)

        @block.vector
        def _(v):
            step = c.dve_step.on(v)
            for n in range(NT + 1):
                if n < NT:
                    r = ROWS[n]
                    for h in range(2):
                        g = 2 * n + h
                        v.wait_ge(turned, g + 1)
                        x = xa[0:r, n, 512 * h:512 * h + 512]
                        v.scalar_tensor_tensor(x, x, ALPHA, bank(c, g % 8, 512, r), ALU.mult, ALU.add).then_inc(resid, 1)
                    v.wait_ge(resid, 2 * n + 2)
                    ln.statistics(v, step, n)
                if n:
                    ln.finish(v, step, n - 1)



_INS = ["x_prompt", "x_sample", "cache_swa_k", "cache_swa_v", "state_dn", "state_dn_conv", "cache_mem_k", "cache_mem_v",
        "mem_prompt", "w_in", "w_conv", "dn_a_log", "dn_dt_bias", "dn_norm_g", "attn_sinks", "w_o", "ln1_g", "ln1_b",
        "w_cq", "w_ck", "w_cv", "w_co", "ln2_g", "ln2_b", "w_pq", "peer_keys1", "peer_keys2", "peer_u", "peer_v",
        "ln3_g", "ln3_b"]
_OUTS = [("y_prompt", (1, SEQ, D)), ("y_sample", (NB, NL, D)), ("swa_k_prompt", (1, 1, P, 2, HD)),
         ("swa_v_prompt", (1, 1, P, 2, HD)), ("dn_state_prompt", (1, 1, DNH, DK, DK)), ("dn_conv_prompt", (1, 1, 3, CONV)),
         ("mem_k_prompt", (1, 1, MEM, XH, D // XH)), ("mem_v_prompt", (1, 1, MEM, XH, D // XH)),
         ("swa_k_sample", (1, NB, P, 2, HD)), ("swa_v_sample", (1, NB, P, 2, HD)),
         ("dn_state_sample", (1, NB, DNH, DK, DK)), ("dn_conv_sample", (1, NB, 3, CONV))]


def run_phases(c, phases):
    nc = c.nc
    for phase in phases:
        own = []
        c.sem = lambda name: own.append(nc.alloc_semaphore(name)) or own[-1]
        phase(c)
        nc.clear_and_free_semaphores(own)
        nc.all_engine_barrier()


def hymba_step(nc, dram):
    with ExitStack() as ctx:
        c = Program(nc, dram)
        c.shared_sem = lambda name: ctx.enter_context(nc.semaphore(name))
        c.ps = ctx.enter_context(nc.psum_tensor("ps", [P, 8 * 512], F32))
        c.dve_step = Steps(c.shared_sem("dve_step"))
        c.act_step = Steps(c.shared_sem("act_step"))
        c.gates_dram = nc.dram_tensor("gates", (P, NTG, NK, TG), F32)[:, :, :, :]
        c.hidden_dram = nc.dram_tensor("hidden", (P, NK, TOK), F32)[:, :, :]
        c.tensors = {0: ctx.enter_context(nc.sbuf_tensor("kept", [P, A_FREE], F32))}

        def memory(scope, name, start, end):
            c.tensors[start] = scope.enter_context(nc.sbuf_tensor(name, [P, end - start], F32))
            scope.callback(c.tensors.pop, start)

        def high_low(scope, name, n):
            return scope.enter_context(nc.sbuf_tensor(name, [P, n], F32R))

        with ExitStack() as layer:
            memory(layer, "layer", A_FREE, ARENA)
            run_phases(c, (phase_project, phase_window, phase_delta, phase_mix, phase_cross))
        with ExitStack() as search:
            c.xr = high_low(search, "x2_high_low", 2 * KD * TOK)
            memory(search, "scores", F_SC, F_SC_END)
            with ExitStack() as queries:
                c.wr = high_low(queries, "w_pq_high_low", 4 * KD * 2 * NK)
                memory(queries, "queries", F_SC_END, F_END)
                run_phases(c, (phase_scores,))
            with ExitStack() as experts:
                c.utr = high_low(experts, "u_high_low", 4 * D)
                c.hot = high_low(experts, "one_hots", 2 * 3 * 4 * P)
                c.gate_hi = high_low(experts, "gates_high", TOK)
                memory(experts, "experts", F_SC_END, H_END)
                run_phases(c, (phase_hidden,))
        with ExitStack() as outputs:
            c.vr = high_low(outputs, "v_high_low", 4 * GB * D)
            c.gr = high_low(outputs, "gated_high_low", 4 * GB * TOK)
            memory(outputs, "outputs", A_FREE, O_END)
            run_phases(c, (phase_combine,))
        with ExitStack() as finish:
            memory(finish, "last_norm", A_FREE, A_FREE + 3 * D)
            run_phases(c, (phase_finish,))


def kernel(**inputs):
    from collections import namedtuple
    import numpy as np
    import concourse.bacc as bacc
    from concourse.bass_utils import run_bass_kernel_spmd

    nc = bacc.Bacc("TRN2", target_bir_lowering=False, num_devices=1)
    arrays = {"consts": constants()}
    for name in _INS:
        arrays[name] = np.ascontiguousarray(inputs[name])
    aps = {}
    for name, a in arrays.items():
        aps[name] = nc.dram_tensor(name, a.shape, mybir.dt.from_np(a.dtype), kind="ExternalInput").ap()
    for name, shape in _OUTS:
        aps[name] = nc.dram_tensor(name, shape, F32, kind="ExternalOutput").ap()
    hymba_step(nc, namedtuple("Dram", aps)(*aps.values()))
    r = run_bass_kernel_spmd(nc, [arrays], core_ids=[0])
    return tuple(r.results[0][name] for name, _ in _OUTS)
```
